# Optimizing a Trainium2 kernel written in Bass

```python
import math
import jax, jax.numpy as jnp
from jax import lax
import numpy as np

D_MODEL = 1024
BATCH = 1
SEQ = 256
DEPTH = 2

N_A_LAYERS = DEPTH // 2
N_B_LAYERS = DEPTH - N_A_LAYERS
LRU_WIDTH = 1280
LRU_BLOCK = 256
LRU_HEADS = LRU_WIDTH // LRU_BLOCK
CONV_WIDTH = 4
LRU_C = 8.0
N_HEADS = 8
N_KV_HEADS = 4
HEAD_DIM = 128
KV_GROUP = N_HEADS // N_KV_HEADS
MOBA_BLOCK = 256
MOBA_TOPK = 3
Q_CHUNK = 16
REL_BUCKETS = 32
REL_MAX_DIST = 128
D_FF = -(-8 * D_MODEL // (3 * 256)) * 256
RMS_EPS = 1e-6
NEG_INF = -1e30


def rmsnorm(x, g):
    xf = x.astype(jnp.float32)
    y = xf * lax.rsqrt(jnp.mean(xf * xf, axis=-1, keepdims=True) + RMS_EPS)
    return (y * g.astype(jnp.float32)).astype(x.dtype)

def modulate(h, shift, scale):
    return h * (1 + scale[:, None, :]) + shift[:, None, :]

def swiglu(h, w_gate, w_up, w_down):
    return (jax.nn.silu(h @ w_gate) * (h @ w_up)) @ w_down

def _lru_combine(left, right):
    a_l, b_l = left
    a_r, b_r = right
    return a_l * a_r, a_r * b_l + b_r

def rglru_mixer(h, w_in, conv_w, conv_b, w_gates, b_gates, lru_lambda, w_out):
    B, S, _ = h.shape
    u = h @ w_in
    y_br = jax.nn.gelu(u[..., :LRU_WIDTH])
    x_br = u[..., LRU_WIDTH:]
    xp = jnp.pad(x_br, ((0, 0), (CONV_WIDTH - 1, 0), (0, 0)))
    xc = sum(xp[:, k:k + S, :] * conv_w[k] for k in range(CONV_WIDTH)) + conv_b
    xb = xc.reshape(B, S, LRU_HEADS, LRU_BLOCK)
    g = jnp.einsum('bshi,hio->bsho', xb, w_gates)
    gr = g[..., :LRU_BLOCK].reshape(B, S, LRU_WIDTH) + b_gates[0]
    gi = g[..., LRU_BLOCK:].reshape(B, S, LRU_WIDTH) + b_gates[1]
    r = jax.nn.sigmoid(gr.astype(jnp.float32))
    i = jax.nn.sigmoid(gi.astype(jnp.float32))
    log_a = -LRU_C * r * jax.nn.softplus(-lru_lambda.astype(jnp.float32))
    a = jnp.exp(log_a)
    mult = jnp.sqrt(-jnp.expm1(2.0 * log_a))
    b = mult * (i * xc.astype(jnp.float32))
    _, hs = lax.associative_scan(_lru_combine, (a, b), axis=1)
    return (hs.astype(h.dtype) * y_br) @ w_out

def shared_kv(x, shift, scale, g, w_kv):
    B, S, _ = x.shape
    h = modulate(rmsnorm(x, g), shift, scale)
    kv = h @ w_kv
    nb = -(-S // MOBA_BLOCK)
    pad = nb * MOBA_BLOCK - S
    def blk(t):
        t = t.reshape(B, S, N_KV_HEADS, HEAD_DIM).transpose(0, 2, 1, 3)
        t = jnp.pad(t, ((0, 0), (0, 0), (0, pad), (0, 0)))
        return t.reshape(B, N_KV_HEADS, nb, MOBA_BLOCK, HEAD_DIM)
    k_blocks = blk(kv[..., :N_KV_HEADS * HEAD_DIM])
    v_blocks = blk(kv[..., N_KV_HEADS * HEAD_DIM:])
    k_mean = jnp.mean(k_blocks.astype(jnp.float32), axis=3)
    return k_blocks, v_blocks, k_mean

def t5_bucket(dist):
    dist = jnp.maximum(dist, 0)
    max_exact = REL_BUCKETS // 2
    d = jnp.maximum(dist, 1).astype(jnp.float32)
    large = max_exact + (jnp.log(d / max_exact) / math.log(REL_MAX_DIST / max_exact)
                         * (REL_BUCKETS - max_exact)).astype(jnp.int32)
    large = jnp.minimum(large, REL_BUCKETS - 1)
    return jnp.where(dist < max_exact, dist, large)

def moba_mixer(h, w_q, w_o, k_blocks, v_blocks, k_mean, rel_bias):
    B, S, _ = h.shape
    nb = k_blocks.shape[2]
    s_pad = nb * MOBA_BLOCK
    n_sel = min(MOBA_TOPK, nb)
    scale = HEAD_DIM ** -0.5
    q = (h @ w_q).reshape(B, S, N_HEADS, HEAD_DIM).transpose(0, 2, 1, 3)
    q = jnp.pad(q, ((0, 0), (0, 0), (0, s_pad - S), (0, 0)))
    kv_head = jnp.arange(N_HEADS) // KV_GROUP
    km = k_mean[:, kv_head]
    bi = jnp.arange(B)[:, None, None, None]
    kvh = kv_head[None, :, None, None]
    hi5 = jnp.arange(N_HEADS)[None, :, None, None, None]
    bias_tab = rel_bias.astype(jnp.float32)
    blk_pos = jnp.arange(MOBA_BLOCK)

    def chunk(ci):
        t0 = ci * Q_CHUNK
        qf = lax.dynamic_slice_in_dim(q, t0, Q_CHUNK, axis=2).astype(jnp.float32)
        pos = t0 + jnp.arange(Q_CHUNK)
        own = t0 // MOBA_BLOCK
        gate = jnp.einsum('bhcd,bhnd->bhcn', qf, km)
        gate = jnp.where(jnp.arange(nb) < own, gate, NEG_INF)
        _, idx = lax.top_k(gate, n_sel)
        sel_valid = jnp.arange(n_sel) < own
        ksel = k_blocks[bi, kvh, idx].astype(jnp.float32)
        vsel = v_blocks[bi, kvh, idx].astype(jnp.float32)
        s_sel = jnp.einsum('bhcd,bhcnkd->bhcnk', qf, ksel) * scale
        kpos_sel = idx[..., None] * MOBA_BLOCK + blk_pos
        dist_sel = pos[None, None, :, None, None] - kpos_sel
        s_sel = jnp.where(sel_valid[:, None], s_sel + bias_tab[hi5, t5_bucket(dist_sel)], NEG_INF)
        k_own = lax.dynamic_index_in_dim(k_blocks, own, axis=2, keepdims=False)[:, kv_head].astype(jnp.float32)
        v_own = lax.dynamic_index_in_dim(v_blocks, own, axis=2, keepdims=False)[:, kv_head].astype(jnp.float32)
        s_own = jnp.einsum('bhcd,bhkd->bhck', qf, k_own) * scale
        dist_own = pos[:, None] - (own * MOBA_BLOCK + blk_pos)[None, :]
        s_own = jnp.where(dist_own >= 0, s_own + bias_tab[:, t5_bucket(dist_own)], NEG_INF)
        logits = jnp.concatenate([s_sel.reshape(B, N_HEADS, Q_CHUNK, n_sel * MOBA_BLOCK), s_own], axis=-1)
        p = jax.nn.softmax(logits, axis=-1)
        p_sel = p[..., :n_sel * MOBA_BLOCK].reshape(B, N_HEADS, Q_CHUNK, n_sel, MOBA_BLOCK)
        p_own = p[..., n_sel * MOBA_BLOCK:]
        o = jnp.einsum('bhcnk,bhcnkd->bhcd', p_sel, vsel) + jnp.einsum('bhck,bhkd->bhcd', p_own, v_own)
        return o.astype(h.dtype)

    o = lax.map(chunk, jnp.arange(s_pad // Q_CHUNK))
    o = o.transpose(1, 0, 3, 2, 4).reshape(B, s_pad, N_HEADS * HEAD_DIM)[:, :S]
    return o @ w_o

def first_inputs(seed: int = 0) -> dict:
    key = jax.random.key(seed)
    ks = jax.random.split(key, 32)
    nrm = lambda k, shape, s: jax.random.normal(k, shape, jnp.float32) * s
    D = D_MODEL
    u = jax.random.uniform(ks[10], (N_A_LAYERS, LRU_WIDTH), jnp.float32, 0.9, 0.999)
    a_base = u ** (1.0 / LRU_C)
    lru_lambda = jnp.log(a_base) - jnp.log1p(-a_base)
    return {
        "x": nrm(ks[0], (BATCH, SEQ, D), 1.0),
        "c": nrm(ks[1], (BATCH, D), 1.0),
        "mod_w": nrm(ks[2], (DEPTH, D, 6 * D), 0.5 * D ** -0.5),
        "mod_b": nrm(ks[3], (DEPTH, 6 * D), 0.02),
        "norm_mix": 1.0 + nrm(ks[4], (DEPTH, D), 0.02),
        "norm_ffn": 1.0 + nrm(ks[5], (DEPTH, D), 0.02),
        "lru_w_in": nrm(ks[6], (N_A_LAYERS, D, 2 * LRU_WIDTH), D ** -0.5),
        "lru_conv_w": nrm(ks[7], (N_A_LAYERS, CONV_WIDTH, LRU_WIDTH), CONV_WIDTH ** -0.5),
        "lru_conv_b": nrm(ks[8], (N_A_LAYERS, LRU_WIDTH), 0.02),
        "lru_w_gates": nrm(ks[9], (N_A_LAYERS, LRU_HEADS, LRU_BLOCK, 2 * LRU_BLOCK), LRU_BLOCK ** -0.5),
        "lru_b_gates": nrm(ks[11], (N_A_LAYERS, 2, LRU_WIDTH), 0.02),
        "lru_lambda": lru_lambda,
        "lru_w_out": nrm(ks[12], (N_A_LAYERS, LRU_WIDTH, D), LRU_WIDTH ** -0.5),
        "kv_mod_w": nrm(ks[13], (D, 2 * D), 0.5 * D ** -0.5),
        "kv_mod_b": nrm(ks[14], (2 * D,), 0.02),
        "kv_norm": 1.0 + nrm(ks[15], (D,), 0.02),
        "w_kv": nrm(ks[16], (D, 2 * N_KV_HEADS * HEAD_DIM), D ** -0.5),
        "attn_w_q": nrm(ks[17], (N_B_LAYERS, D, N_HEADS * HEAD_DIM), D ** -0.5),
        "attn_w_o": nrm(ks[18], (N_B_LAYERS, N_HEADS * HEAD_DIM, D), (N_HEADS * HEAD_DIM) ** -0.5),
        "rel_bias": nrm(ks[19], (N_HEADS, REL_BUCKETS), 0.2),
        "ffn_w_gate": nrm(ks[20], (DEPTH, D, D_FF), D ** -0.5),
        "ffn_w_up": nrm(ks[21], (DEPTH, D, D_FF), D ** -0.5),
        "ffn_w_down": nrm(ks[22], (DEPTH, D_FF, D), D_FF ** -0.5),
        "final_norm": 1.0 + nrm(ks[23], (D,), 0.02),
    }

def first_block(x, c, mod_w, mod_b, norm_mix, norm_ffn, lru_w_in, lru_conv_w, lru_conv_b,
              lru_w_gates, lru_b_gates, lru_lambda, lru_w_out, kv_mod_w, kv_mod_b, kv_norm,
              w_kv, attn_w_q, attn_w_o, rel_bias, ffn_w_gate, ffn_w_up, ffn_w_down, final_norm):
    D = D_MODEL
    cs = jax.nn.silu(c)
    kv = None
    for l in range(DEPTH):
        if l == N_A_LAYERS:
            kv_mod = cs @ kv_mod_w + kv_mod_b
            kv = shared_kv(x, kv_mod[:, :D], kv_mod[:, D:], kv_norm, w_kv)
        mod = cs @ mod_w[l] + mod_b[l]
        sh_m, sc_m, g_m = mod[:, :D], mod[:, D:2 * D], mod[:, 2 * D:3 * D]
        sh_f, sc_f, g_f = mod[:, 3 * D:4 * D], mod[:, 4 * D:5 * D], mod[:, 5 * D:]
        h = modulate(rmsnorm(x, norm_mix[l]), sh_m, sc_m)
        if l < N_A_LAYERS:
            mix = rglru_mixer(h, lru_w_in[l], lru_conv_w[l], lru_conv_b[l], lru_w_gates[l],
                              lru_b_gates[l], lru_lambda[l], lru_w_out[l])
        else:
            j = l - N_A_LAYERS
            mix = moba_mixer(h, attn_w_q[j], attn_w_o[j], kv[0], kv[1], kv[2], rel_bias)
        x = x + g_m[:, None, :] * mix
        h = modulate(rmsnorm(x, norm_ffn[l]), sh_f, sc_f)
        x = x + g_f[:, None, :] * swiglu(h, ffn_w_gate[l], ffn_w_up[l], ffn_w_down[l])
    return rmsnorm(x, final_norm)


PLE_DIM = 256
D_MIX = D_MODEL
MLA_HEADS = 8
MLA_NOPE = 64
MLA_ROPE = 32
MLA_V = 64
Q_LORA = 256
KV_LORA = 128
DIL_HEADS = 8
DIL_HEAD_DIM = 64
DIL_CONFIGS = ((128, 1), (512, 4), (2048, 16))
D_FF_2 = 2816
MACARON = 0.5
ROPE_THETA = 10000.0
EPS = 1e-6
Q_BLOCK = 128
NEG = -1e30
N_NORMS = 8

MLA_WIDTH = MLA_HEADS * MLA_V
DIL_WIDTH = DIL_HEADS * DIL_HEAD_DIM
N_IN = Q_LORA + KV_LORA + MLA_ROPE + 3 * DIL_WIDTH


def rmsnorm_2(x, g):
    xf = x.astype(jnp.float32)
    y = xf * lax.rsqrt(jnp.mean(xf * xf, axis=-1, keepdims=True) + EPS)
    return (y * g.astype(jnp.float32)).astype(x.dtype)

def rope_tables(positions, dim, dtype):
    inv = ROPE_THETA ** (-jnp.arange(0, dim, 2, dtype=jnp.float32) / dim)
    ang = positions.astype(jnp.float32)[..., None] * inv
    return jnp.cos(ang)[:, :, None, :].astype(dtype), jnp.sin(ang)[:, :, None, :].astype(dtype)

def apply_rope(x, cos, sin):
    x1, x2 = jnp.split(x, 2, axis=-1)
    return jnp.concatenate([x1 * cos - x2 * sin, x2 * cos + x1 * sin], axis=-1)

def swiglu_2(x, w_gate, w_up, w_down):
    return (jax.nn.silu(x @ w_gate) * (x @ w_up)) @ w_down

def mla_attention(q_nope, q_rope, k_nope, k_rope, v):
    B, S, H, _ = q_nope.shape
    nb = S // Q_BLOCK
    scale = (MLA_NOPE + MLA_ROPE) ** -0.5
    key_pos = jnp.arange(S)

    def block(n):
        start = n * Q_BLOCK
        qn = lax.dynamic_slice_in_dim(q_nope, start, Q_BLOCK, axis=1)
        qr = lax.dynamic_slice_in_dim(q_rope, start, Q_BLOCK, axis=1)
        s = (jnp.einsum('bqhd,bkhd->bhqk', qn, k_nope)
             + jnp.einsum('bqhd,bkd->bhqk', qr, k_rope)).astype(jnp.float32) * scale
        q_pos = start + jnp.arange(Q_BLOCK)
        causal = key_pos[None, :] <= q_pos[:, None]
        s = jnp.where(causal[None, None], s, NEG)
        w = jax.nn.softmax(s, axis=-1).astype(v.dtype)
        return jnp.einsum('bhqk,bkhd->bqhd', w, v)

    out = lax.map(block, jnp.arange(nb))
    return out.transpose(1, 0, 2, 3, 4).reshape(B, S, H * v.shape[-1])

def dilated_branch(q, k, v, window, dilation):
    B, S, H, dh = q.shape
    L = S // dilation
    w_sub = window // dilation
    nb = -(-L // Q_BLOCK)
    Lp = nb * Q_BLOCK

    def to_sub(t):
        t = t.reshape(B, L, dilation, H, dh).transpose(0, 2, 1, 3, 4).reshape(B * dilation, L, H, dh)
        t = jnp.pad(t, ((0, 0), (0, Lp - L), (0, 0), (0, 0)))
        return t.reshape(B * dilation, nb, Q_BLOCK, H, dh)

    def with_prev(t):
        prev = jnp.pad(t, ((0, 0), (1, 0), (0, 0), (0, 0), (0, 0)))[:, :-1]
        return jnp.concatenate([prev, t], axis=2)

    qs, ks, vs = to_sub(q), to_sub(k), to_sub(v)
    kk, vv = with_prev(ks), with_prev(vs)
    s = jnp.einsum('gnqhd,gnkhd->gnhqk', qs, kk).astype(jnp.float32) * (dh ** -0.5)
    qi = jnp.arange(Q_BLOCK)[:, None]
    ki = jnp.arange(2 * Q_BLOCK)[None, :]
    dist = qi + Q_BLOCK - ki
    key_sub = jnp.arange(nb)[:, None, None] * Q_BLOCK + ki[None] - Q_BLOCK
    valid = (dist >= 0)[None] & (dist <= w_sub)[None] & (key_sub >= 0)
    s = jnp.where(valid[None, :, None], s, NEG)
    m = jnp.max(s, axis=-1, keepdims=True)
    e = jnp.exp(s - m)
    den = jnp.sum(e, axis=-1, keepdims=True)
    lse = (m + jnp.log(den))[..., 0]
    o = jnp.einsum('gnhqk,gnkhd->gnqhd', (e / den).astype(v.dtype), vv)
    o = (o.reshape(B * dilation, Lp, H, dh)[:, :L]
         .reshape(B, dilation, L, H, dh).transpose(0, 2, 1, 3, 4).reshape(B, S, H, dh))
    lse = (lse.transpose(0, 1, 3, 2).reshape(B * dilation, Lp, H)[:, :L]
           .reshape(B, dilation, L, H).transpose(0, 2, 1, 3).reshape(B, S, H))
    return o, lse

def dilated_attention(q, k, v):
    outs, lses = [], []
    for window, dilation in DIL_CONFIGS:
        o, l = dilated_branch(q, k, v, window, dilation)
        outs.append(o)
        lses.append(l)
    wts = jax.nn.softmax(jnp.stack(lses, axis=0), axis=0).astype(q.dtype)
    return jnp.einsum('kbsh,kbshd->bshd', wts, jnp.stack(outs, axis=0))

def hybrid_mixer(h, cos_m, sin_m, cos_d, sin_d, w_in, q_norm, w_q_up, kv_norm, w_kv_up, grp_gain, w_out):
    B, S, _ = h.shape
    z = h @ w_in
    c0 = Q_LORA
    c1 = c0 + KV_LORA
    c2 = c1 + MLA_ROPE
    q_lat, kv_lat, k_rope, qkv_d = jnp.split(z, [c0, c1, c2], axis=-1)
    q = (rmsnorm_2(q_lat, q_norm) @ w_q_up).reshape(B, S, MLA_HEADS, MLA_NOPE + MLA_ROPE)
    q_nope = q[..., :MLA_NOPE]
    q_rope = apply_rope(q[..., MLA_NOPE:], cos_m, sin_m)
    kv = (rmsnorm_2(kv_lat, kv_norm) @ w_kv_up).reshape(B, S, MLA_HEADS, MLA_NOPE + MLA_V)
    k_nope, v_mla = kv[..., :MLA_NOPE], kv[..., MLA_NOPE:]
    k_rope = apply_rope(k_rope[:, :, None, :], cos_m, sin_m)[:, :, 0]
    o_mla = mla_attention(q_nope, q_rope, k_nope, k_rope, v_mla)
    qd, kd, vd = [t.reshape(B, S, DIL_HEADS, DIL_HEAD_DIM) for t in jnp.split(qkv_d, 3, axis=-1)]
    qd = apply_rope(qd, cos_d, sin_d)
    kd = apply_rope(kd, cos_d, sin_d)
    o_dil = dilated_attention(qd, kd, vd).reshape(B, S, DIL_WIDTH)
    merged = jnp.concatenate([rmsnorm_2(o_mla, grp_gain[:MLA_WIDTH]),
                              rmsnorm_2(o_dil, grp_gain[MLA_WIDTH:])], axis=-1)
    return merged @ w_out

def second_inputs(seed: int = 0) -> dict:
    key = jax.random.key(seed)
    ks = jax.random.split(key, 16)
    f32 = jnp.float32

    def w(k, shape, fan_in):
        return jax.random.normal(k, shape, f32) * (fan_in ** -0.5)

    def gain(k, shape):
        return 1.0 + 0.02 * jax.random.normal(k, shape, f32)

    return {
        "x": jax.random.normal(ks[0], (BATCH, SEQ, D_MODEL), f32),
        "p": jax.random.normal(ks[1], (DEPTH, BATCH, SEQ, PLE_DIM), f32),
        "positions": jnp.broadcast_to(jnp.arange(SEQ, dtype=jnp.int32), (BATCH, SEQ)),
        "norm_gains": gain(ks[2], (DEPTH, N_NORMS, D_MODEL)),
        "w_in": w(ks[3], (DEPTH, D_MODEL, N_IN), D_MODEL),
        "q_norm": gain(ks[4], (DEPTH, Q_LORA)),
        "w_q_up": w(ks[5], (DEPTH, Q_LORA, MLA_HEADS * (MLA_NOPE + MLA_ROPE)), Q_LORA),
        "kv_norm": gain(ks[6], (DEPTH, KV_LORA)),
        "w_kv_up": w(ks[7], (DEPTH, KV_LORA, MLA_HEADS * (MLA_NOPE + MLA_V)), KV_LORA),
        "group_out_norm": gain(ks[8], (DEPTH, D_MIX)),
        "w_out": w(ks[9], (DEPTH, D_MIX, D_MODEL), D_MIX),
        "ffn_gate": w(ks[10], (DEPTH, 2, D_MODEL, D_FF_2), D_MODEL),
        "ffn_up": w(ks[11], (DEPTH, 2, D_MODEL, D_FF_2), D_MODEL),
        "ffn_down": w(ks[12], (DEPTH, 2, D_FF_2, D_MODEL), D_FF_2),
        "w_ple": w(ks[13], (DEPTH, PLE_DIM, D_MODEL), PLE_DIM),
        "w_ple_gate": w(ks[14], (DEPTH, D_MODEL, D_MODEL), D_MODEL),
    }

def second_block(x, p, positions, norm_gains, w_in, q_norm, w_q_up, kv_norm, w_kv_up,
              group_out_norm, w_out, ffn_gate, ffn_up, ffn_down, w_ple, w_ple_gate):
    cos_m, sin_m = rope_tables(positions, MLA_ROPE, x.dtype)
    cos_d, sin_d = rope_tables(positions, DIL_HEAD_DIM, x.dtype)
    h = x
    for i in range(DEPTH):
        g = norm_gains[i]
        f = swiglu_2(rmsnorm_2(h, g[0]), ffn_gate[i, 0], ffn_up[i, 0], ffn_down[i, 0])
        h = h + MACARON * rmsnorm_2(f, g[1])
        mix = hybrid_mixer(rmsnorm_2(h, g[2]), cos_m, sin_m, cos_d, sin_d, w_in[i], q_norm[i],
                           w_q_up[i], kv_norm[i], w_kv_up[i], group_out_norm[i], w_out[i])
        h = h + rmsnorm_2(mix, g[3])
        f = swiglu_2(rmsnorm_2(h, g[4]), ffn_gate[i, 1], ffn_up[i, 1], ffn_down[i, 1])
        h = h + MACARON * rmsnorm_2(f, g[5])
        gate = jax.nn.sigmoid(rmsnorm_2(h, g[6]) @ w_ple_gate[i])
        h = h + rmsnorm_2((p[i].astype(h.dtype) @ w_ple[i]) * gate, g[7])
    return h


def setup_inputs(seed=0):
    out = dict(first_inputs(seed))
    for name, value in second_inputs(seed + 1).items():
        if name != "x":
            out[name + "_2"] = value
    return out


def reference(
    x, c, mod_w, mod_b, norm_mix, norm_ffn, lru_w_in, lru_conv_w, lru_conv_b, lru_w_gates,
    lru_b_gates, lru_lambda, lru_w_out, kv_mod_w, kv_mod_b, kv_norm, w_kv, attn_w_q, attn_w_o,
    rel_bias, ffn_w_gate, ffn_w_up, ffn_w_down, final_norm, p_2, positions_2, norm_gains_2,
    w_in_2, q_norm_2, w_q_up_2, kv_norm_2, w_kv_up_2, group_out_norm_2, w_out_2, ffn_gate_2,
    ffn_up_2, ffn_down_2, w_ple_2, w_ple_gate_2,
):
    x = first_block(
        x, c, mod_w, mod_b, norm_mix, norm_ffn, lru_w_in, lru_conv_w, lru_conv_b, lru_w_gates,
        lru_b_gates, lru_lambda, lru_w_out, kv_mod_w, kv_mod_b, kv_norm, w_kv, attn_w_q,
        attn_w_o, rel_bias, ffn_w_gate, ffn_w_up, ffn_w_down, final_norm,
    )
    return second_block(
        x, p_2, positions_2, norm_gains_2, w_in_2, q_norm_2, w_q_up_2, kv_norm_2, w_kv_up_2,
        group_out_norm_2, w_out_2, ffn_gate_2, ffn_up_2, ffn_down_2, w_ple_2, w_ple_gate_2,
    )


_drawn_inputs = setup_inputs


def setup_inputs(seed=0):
    import zlib

    import numpy as np

    out = dict(_drawn_inputs(seed))
    spreads = {}
    factors = {'norm_mix': 8.0,
     'norm_ffn': 6.23,
     'lru_b_gates': 8.0,
     'kv_mod_b': 3.214,
     'kv_norm': 8.0,
     'rel_bias': 3.537,
     'q_norm_2': 8.0,
     'kv_norm_2': 4.403,
     'group_out_norm_2': 3.312}
    for name, (base, spread) in spreads.items():
        noise = np.random.default_rng([zlib.crc32(name.encode()), seed]).standard_normal(out[name].shape)
        drawn = base * np.exp(spread * noise) if base else spread * noise
        out[name] = __import__('jax').numpy.asarray(drawn.astype(out[name].dtype))
    for name, factor in factors.items():
        out[name] = (out[name] * factor).astype(out[name].dtype)
    return out
```

```python
import math
from contextlib import ExitStack

import numpy as np

import concourse.bass as bass
from concourse import mybir

F32 = mybir.dt.float32
F32R = mybir.dt.float32r
I32 = mybir.dt.int32
ALU = mybir.AluOpType
ACT = mybir.ActivationFunctionType

P = 128
S = 256
D = 1024
CH = D // P
DFF = 2816
FJ = DFF // 256
LRU = 1280
LCH = LRU // P
LHEADS = 5
HEADS = 8
KVH = 4
LAYERS2 = 2
DINNER = 2048
EPS = 1e-6
NEG = -1e30
MAGIC = 12582912.0
TWO_PI = 2.0 * math.pi
C1 = 6.28125
C2 = float(np.float32(np.round((TWO_PI - C1) * 2**21) / 2**21))
C3 = TWO_PI - C1 - C2
PI_SAFE = 3.1415925

B_WIN = 0
B_GATE = B_WIN + 10
B_LOUT = B_GATE + 3
B_FFN0 = B_LOUT + 5
B_KV = B_FFN0 + 3 * FJ
B_Q = B_KV + 4
B_O = B_Q + 4
B_FFN1 = B_O + 4
B_L2 = B_FFN1 + 3 * FJ
M_MIX = 3 * FJ
M_OUT = M_MIX + 10
M_FFN = M_OUT + 4
M_PLE = M_FFN + 3 * FJ
M_PGATE = M_PLE + 1
PER_L2 = M_PGATE + 4
SLABS = B_L2 + LAYERS2 * PER_L2
RING = 3

MOD_GROUPS = 7
MOD_RING = 2
G_MIX0, G_A0, G_B0, G_KV, G_MIX1, G_A1, G_B1 = range(MOD_GROUPS)

N_MIX0, N_FFN0, N_KV, N_FFN1, N_FIN = range(5)
L_PRE1, L_POST1, L_PREMIX, L_QLAT, L_KVLAT, L_GMLA, L_GDIL, L_POSTMIX, L_PRE2, L_POST2, L_PREPLE, L_POSTPLE = range(12)
NORM_CHUNKS = [CH] * 5 + [8, 8, 8, 2, 1, 4, 4, 8, 8, 8, 8, 8] * LAYERS2
A_MIX0, A_FFN0, A_KV, A_MIX1, A_FFN1 = range(5)
LA_PRE1, LA_PREMIX, LA_QLAT, LA_KVLAT, LA_GMLA, LA_GDIL, LA_PRE2, LA_PREPLE = range(8)
APPLY_CHUNKS = [CH] * 5 + [8, 8, 2, 1, 4, 4, 8, 8] * LAYERS2


def before(counts, n):
    return sum(counts[:n])


def norm2(l, k):
    return 5 + 12 * l + k


def apply2(l, k):
    return 5 + 8 * l + k


def norm_at(n):
    return {L_KVLAT: 2, L_GDIL: 4}.get((n - 5) % 12, 0) if n >= 5 else 0


def base2(l, k=0):
    return B_L2 + l * PER_L2 + k


COLS = [("c", CH), ("norm_mix", 2 * CH), ("norm_ffn", 2 * CH), ("kv_norm", CH), ("final_norm", CH),
        ("gains2", LAYERS2 * 8 * CH), ("q_norm2", LAYERS2 * 2), ("kv_norm2", LAYERS2), ("group2", LAYERS2 * CH),
        ("conv_w", 4 * LCH), ("conv_b", LCH), ("b_gates", 2 * LCH), ("lambda", LCH), ("mod_b", MOD_GROUPS * 16),
        ("inv_mla", 1), ("inv_dil", 1), ("sign_mla", 1)]
COL_AT = {}
_n = 0
for _name, _k in COLS:
    COL_AT[_name] = _n
    _n += _k
NCOLS = _n


def build(nc, stream, mods, x_t, cols_d, onehot, rb_t, masks, pos, p_t, out_t):
    scratch = nc.dram_tensor("bias_rows", (HEADS, P, 512), F32, kind="Internal").ap()
    with ExitStack() as ctx:
        def sb(name, shape, dt=F32):
            return ctx.enter_context(nc.sbuf_tensor(name, shape, dt))

        def sem(name):
            return ctx.enter_context(nc.semaphore(name))

        bank = [ctx.enter_context(nc.psum_tensor(f"bank{i}", [P, 512], F32)) for i in range(8)]

        raw = sb("raw", [P, RING, DINNER])
        w_hi = sb("w_hi", [P, RING, DINNER], F32R)
        w_lo = sb("w_lo", [P, RING, DINNER], F32R)
        x = sb("x", [P, CH, S])
        a_hi = sb("a_hi", [P, LCH, S], F32R)
        a_lo = sb("a_lo", [P, LCH, S], F32R)
        hid_hi = sb("hid_hi", [P, 2, 2, S], F32R)
        hid_lo = sb("hid_lo", [P, 2, 2, S], F32R)
        sq = sb("sq", [P, CH, S])
        var = sb("var", [P, S])
        rs0 = sb("rs0", [P, S])
        nwt = sb("nwt", [P, S])
        rstd = sb("rstd", [P, 2, S])
        ones = sb("ones", [P, P])
        ident = sb("ident", [P, P])
        cols = sb("cols", [P, NCOLS])
        modc = sb("modc", [P, MOD_GROUPS * 16])
        cs = sb("cs", [P, CH])
        scale1 = sb("scale1", [P, 5 * CH])
        half_g = sb("half_g", [P, LAYERS2 * 2 * CH])
        lam = sb("lam", [P, 8, LCH])
        shared = sb("shared", [P, 4 * 2048])
        mod_raw = shared[:, 0:4096].rearrange("p (r n) -> p r n", r=2)
        mod_acc = shared[:, 4096:8192].rearrange("p (r n) -> p r n", r=2)
        f = shared[:, 0:2048].rearrange("p (c s) -> p c s", c=CH)
        rope = shared[:, 2048:3072].rearrange("p (k s) -> p k s", k=4)
        mask = shared[:, 3072:3840].rearrange("p (k s) -> p k s", k=2)
        ptok = shared[:, 3840:4864].rearrange("p (l c s) -> p l c s", l=2, c=2)
        pos_i = shared[:, 4864:5120].bitcast(I32)
        pos_f = shared[:, 5120:5376]
        ang = shared[:, 5376:5632]
        turn = shared[:, 5632:6144].rearrange("p (k s) -> p k s", k=2)
        red = shared[:, 6144:6656].rearrange("p (k s) -> p k s", k=2)
        work = sb("work", [P, 10752])

        def area(at, *shape):
            n = int(np.prod(shape))
            v = work[:, at:at + n]
            if len(shape) == 2:
                v = v.rearrange("p (a b) -> p a b", a=shape[0])
            elif len(shape) == 3:
                v = v.rearrange("p (a b c) -> p a b c", a=shape[0], b=shape[1])
            return v

        y_br = area(0, LCH, S)
        xc = area(2560, LCH, S)
        r_g = area(5120, LCH, S)
        i_g = area(7680, LCH, S)
        rbb = area(5120, HEADS, P)
        bias_rows = area(6144, HEADS, 512)
        onehot_sb = area(10240, 512)
        gate_s = area(0, 2, 512)
        hid = area(1024, 2, 512)
        q_a = area(0, CH, S)
        k_a = area(2048, KVH, S)
        v_a = area(3072, 2, 512)
        bias = area(7168, HEADS, 384)
        q_dil = area(0, 4, S)
        k_dil = area(1024, 4, S)
        v_dil = area(2048, 2, 512)
        q_nope = area(3072, 4, S)
        q_rope = area(4096, 2, S)
        k_nope = area(4608, 4, S)
        v_mla = area(5632, 2, 512)
        q_lat = area(8960, 2, S)
        kv_lat = area(9472, 1, S)
        kr = area(9728, S)
        sc = area(4096, 2, 384)
        prob = area(4864, 2, 384)
        prob_t = area(5632, 2, 384)
        sc2 = area(6656, 2, 384)
        prob2 = area(7424, 2, 384)
        prob_t2 = area(8192, 2, 384)
        rt = area(6656, 4, S)
        nmax = sb("nmax", [P, 2, 2])
        ssum = sb("ssum", [P, 2, 2])
        rsum = sb("rsum", [P, 2, 2])
        xp = sb("xp", [P, 2, 2, S + 3])
        rb_sb = sb("rb_sb", [32, HEADS])

        def col(name, k):
            return cols[:, COL_AT[name] + k:COL_AT[name] + k + 1]

        def modcol(g, k):
            return modc[:, 16 * g + k:16 * g + k + 1]

        s_cols, s_x, s_rb, s_oh = sem("cols_landed"), sem("x_landed"), sem("rb_landed"), sem("onehot_landed")
        landed = [sem(f"slab_landed{r}") for r in range(RING)]
        mod_landed = [sem(f"mod_landed{r}") for r in range(MOD_RING)]
        s_late = sem("late_landed")
        s_rows = sem("bias_rows_stored")
        s_bias = sem("bias_landed")
        s_out = sem("out_stored")
        hi_ready, lo_ready, slab_done = sem("hi_ready"), sem("lo_ready"), sem("slab_done")
        bank_done = sem("bank_done")
        sq_ready, stat_ready, var_ready, rs0_ready = sem("sq_ready"), sem("stat_ready"), sem("var_ready"), sem("rs0_ready")
        newton, rstd_ready = sem("newton"), sem("rstd_ready")
        nt_ready, nh_ready, nl_ready = sem("normed_ready"), sem("normed_hi_ready"), sem("normed_lo_ready")
        x_ready, f_ready, f_scaled = sem("x_ready"), sem("f_ready"), sem("f_scaled")
        silu_done, hid_done, hh_ready, hl_ready = sem("silu_done"), sem("hid_done"), sem("hid_hi_ready"), sem("hid_lo_ready")
        const_ready = sem("const_ready")
        ident0 = sem("ident_zeroed")
        rbb_ready = sem("rbb_ready")
        row_mm, row_ev = sem("bias_row_made"), sem("bias_row_copied")
        cs_ready = sem("cs_ready")
        mod_step, mod_red, modc_ready = sem("mod_step"), sem("mod_reduced"), sem("modc_ready")
        acc_zero = sem("acc_zero")
        scale_ready = sem("scale_ready")
        half_ready = sem("half_ready")
        lam_act, lam_dve = sem("lambda_act"), sem("lambda_dve")
        pad_zero = sem("pad_zero")
        xbr_ready, conv_step, conv_done, y_ready = sem("xbr_copied"), sem("conv_step"), sem("conv_done"), sem("gelu_ready")
        xch_ready, xcl_ready = sem("conv_hi_ready"), sem("conv_lo_ready")
        gate_done, gates_ready = sem("gates_made"), sem("gates_ready")
        bi_ready, decay_ready = sem("gated_input_ready"), sem("decay_ready")
        mult2_step, mult2_ready, mult_ready = sem("mult2_step"), sem("mult2_ready"), sem("mult_ready")
        scan_step, z_ready, zh_ready, zl_ready = sem("scan_step"), sem("z_ready"), sem("z_hi_ready"), sem("z_lo_ready")
        qkv_act, qkv_dve, rope_step = sem("qkv_copied_act"), sem("qkv_copied_dve"), sem("rope_step")
        qk_done, sc_done, exp_done, rs_done, pn_done = sem("qk_done"), sem("scores_done"), sem("exp_done"), sem("rsum_done"), sem("probs_done")
        tr_done, pt_done, pv_done, o_done, oh_done = sem("probs_turned"), sem("probs_t_done"), sem("pv_done"), sem("o_done"), sem("o_hi_done")
        up_done = sem("latent_up_done")
        trig_step, trig_act, rope_ready = sem("trig_step"), sem("trig_act"), sem("rope_ready")
        ph_ready, pl_ready = sem("p_hi_ready"), sem("p_lo_ready")
        pg_ready = sem("ple_gate_ready")

        block = ctx.enter_context(nc.Block())

        U_LRU, U_FFN0, U_MOBA, U_FFN1, U_FIN = range(5)

        def u2(l, k):
            return 5 + 4 * l + k

        U_LAST = u2(LAYERS2 - 1, 3)

        @block.sync
        def _(sp):
            sp.dma_start(cols[:, :], cols_d).then_inc(s_cols, 16)
            sp.dma_start(x[:, :, :], x_t.rearrange("(c p) s -> p c s", p=P)).then_inc(s_x, 16)
            for s in range(RING):
                sp.dma_start(raw[:, s, :], stream[s]).then_inc(landed[s], 16)
            with sp.Fori(1, SLABS // RING) as i:
                for r in range(RING):
                    src = stream[bass.ds(i * RING + r, 1)].rearrange("a p n -> p (a n)")
                    split = sp.snap(i * RING + (r - RING + 1))
                    sp.wait_ge(lo_ready, split)
                    sp.dma_start(raw[:, r, :], src).then_inc(landed[r], 16)
            for s in range(SLABS // RING * RING, SLABS):
                sp.wait_ge(lo_ready, s - RING + 1)
                sp.dma_start(raw[:, s % RING, :], stream[s]).then_inc(landed[s % RING], 16)
            for c in range(CH):
                sp.wait_ge(x_ready, CH * U_LAST + c + 1)
                sp.dma_start(out_t[c * P:(c + 1) * P, :], x[:, c, :]).then_inc(s_out, 16)
            sp.wait_ge(s_out, 16 * CH)

        @block.gpsimd
        def _(pool):
            for s in range(MOD_RING):
                pool.dma_start(mod_raw[:, s, :], mods[s]).then_inc(mod_landed[s], 16)
            pool.dma_start(rb_sb[:, :], rb_t).then_inc(s_rb, 16)
            pool.dma_start(onehot_sb[0:33, :], onehot).then_inc(s_oh, 16)
            nc.gpsimd.memset(ident[:, :], 0.0).then_inc(ident0, 1)
            pool.wait_ge(ident0, 1)
            nc.gpsimd.affine_select(out=ident[:, :], in_=ident[:, :], compare_op=ALU.not_equal, fill=1.0, base=0,
                                    pattern=[[-1, P]], channel_multiplier=1)
            nc.gpsimd.memset(ones[:, :], 1.0).then_inc(const_ready, 1)
            with pool.Fori(1, 8 * MOD_GROUPS // MOD_RING) as i:
                for r in range(MOD_RING):
                    src = mods[bass.ds(i * MOD_RING + r, 1)].rearrange("a p n -> p (a n)")
                    used = pool.snap(i * MOD_RING + (r - MOD_RING + 1))
                    pool.wait_ge(mod_step, used)
                    pool.dma_start(mod_raw[:, r, :], src).then_inc(mod_landed[r], 16)
            pool.wait_ge(mod_red, MOD_GROUPS)
            pool.dma_start(mask, masks.rearrange("k p s -> p k s")).then_inc(s_late, 16)
            pool.dma_start(pos_i, pos).then_inc(s_late, 16)
            pool.dma_start(ptok, p_t.rearrange("l (c p) s -> p l c s", p=P)).then_inc(s_late, 16)

        @block.tensor
        def _(pe):
            def product(out, w_h, w_l, v_h, v_l, start, stop):
                pe.matmul(out, w_h, v_h, start=start, stop=False, skip_group_check=True)
                pe.matmul(out, w_h, v_l, start=False, stop=False, skip_group_check=True)
                return pe.matmul(out, w_l, v_h, start=False, stop=stop, skip_group_check=True)

            def weights(s, lo, n):
                return w_hi[:, s % RING, lo:lo + n], w_lo[:, s % RING, lo:lo + n]

            def need_slab(s):
                pe.wait_ge(lo_ready, s + 1)

            def feature_slab(slot, out, chunk_ready=None, m_chunks=2, width=256):
                for c in range(CH):
                    if chunk_ready is not None:
                        pe.wait_ge(nl_ready, chunk_ready + c + 1)
                    for m in range(m_chunks):
                        mm = product(out[:, m * S:(m + 1) * S], *weights(slot, c * width + m * P, P), a_hi[:, c, :], a_lo[:, c, :],
                                     start=(c == 0 and m == 0), stop=(c == CH - 1))
                return mm

            def token_slab(slot, out, chunks=CH):
                for c in range(chunks):
                    for t in range(2):
                        wh, wl = weights(slot, c * 256, 256)
                        o = out[:, t * 256:(t + 1) * 256]
                        lh, ll = a_hi[:, c, t * P:(t + 1) * P], a_lo[:, c, t * P:(t + 1) * P]
                        pe.matmul(o, lh, wh, start=(c == 0 and t == 0), stop=False, skip_group_check=True)
                        pe.matmul(o, ll, wh, start=False, stop=False, skip_group_check=True)
                        mm = pe.matmul(o, lh, wl, start=False, stop=(c == chunks - 1), skip_group_check=True)
                return mm

            def sums_slab(slot, v_h, v_l, first, last):
                def one(k, m):
                    return product(bank[4 + m // 2][:, (m % 2) * S:(m % 2 + 1) * S], *weights(slot, k * D + m * P, P),
                                   v_h[:, k, :], v_l[:, k, :], start=(first and k == 0 and m % 2 == 0), stop=(last and k == 1))
                if not last:
                    for k in range(2):
                        for m in range(CH):
                            mm = one(k, m)
                    return mm
                for m in range(CH):
                    for k in range(2):
                        mm = one(k, m)
                    if m in (1, 3, 5):
                        mm.then_inc(bank_done, 1)
                return mm

            def norm_stat(n, b):
                chunks = NORM_CHUNKS[n]
                for c in range(chunks):
                    pe.wait_ge(sq_ready, before(NORM_CHUNKS, n) + c + 1)
                    mm = pe.matmul(bank[b][:, 0:S], ones[:, :], sq[:, norm_at(n) + c, :], start=(c == 0), stop=(c == chunks - 1))
                mm.then_inc(stat_ready, 1)

            def mod_reduce(g, b, steps):
                pe.wait_ge(mod_step, steps)
                for m in range(16):
                    mm = pe.matmul(bank[b][:, m:m + 1], mod_acc[:, g % 2, m * P:(m + 1) * P], ones[:, 0:1],
                                   start=True, stop=True)
                mm.then_inc(mod_red, 1)

            def ffn(i, b, ap):
                f0 = FJ * i

                def group(j, ready, slot, chunk_ready=None, j_par=None):
                    par = j_par
                    for k, out in enumerate((bank[par], bank[2 + par])):
                        pe.wait_ge(lo_ready, ready + k)
                        if j is not None:
                            pe.wait_ge(hid_done, j + (f0 - 1))
                        feature_slab(slot + k, out, chunk_ready if k == 0 else None).then_inc(slab_done, 1)

                def down(j, ready, slot, par, first=False, last=False):
                    pe.wait_ge(lo_ready, ready)
                    pe.wait_ge(hl_ready, j + (f0 + 1))
                    sums_slab(slot, hid_hi[:, par], hid_lo[:, par], first, last).then_inc(slab_done, 1)

                group(None, b + 1, b, before(APPLY_CHUNKS, ap), 0)
                group(None, b + 3, b + 2, None, 1)
                down(0, b + 5, b + 4, 0, first=True)
                with pe.Fori(0, (FJ - 3) // 2) as k:
                    for h in range(2):
                        group(2 * k + (2 + h), 6 * k + (b + 6 + 3 * h), b + 5 + 3 * h, None, h)
                        down(2 * k + (1 + h), 6 * k + (b + 8 + 3 * h), b + 7 + 3 * h, (1 + h) % 2)
                j = FJ - 1
                group(j, b + 3 * j, b + 3 * j - 1, None, j % 2)
                down(j - 1, b + 3 * j + 2, b + 3 * j + 1, (j - 1) % 2)
                down(j, b + 3 * j + 3, b + 3 * j + 2, j % 2, last=True)

            def attention(heads, qk, pv, o0):
                n = len(heads)

                def score(k):
                    if k >= 2:
                        pe.wait_ge(sc_done, heads[k] - 1)
                    for t in range(2):
                        out = bank[k % 2][:, 0:P] if t == 0 else bank[k % 2][:, P:384]
                        parts = qk(k, t)
                        for i, (lhs, rhs) in enumerate(parts):
                            mm = pe.matmul(out, lhs, rhs, start=(t == 0 and i == 0), stop=(i == len(parts) - 1), skip_group_check=True)
                    mm.then_inc(qk_done, 1)

                def turn(k):
                    pe.wait_ge(pn_done, heads[k] + 1)
                    if k >= 2:
                        pe.wait_ge(pt_done, heads[k] - 1)
                    pr = (prob if heads[k] < HEADS else prob2)[:, heads[k] % 2]
                    for t in range(3):
                        mm = pe.transpose(bank[2 + k % 2][:, t * P:(t + 1) * P], pr[:, t * P:(t + 1) * P], ident[:, :])
                    mm.then_inc(tr_done, 1)

                def weigh(k):
                    pe.wait_ge(pt_done, heads[k] + 1)
                    lhs, out, gate = pv(k)
                    if gate is not None:
                        pe.wait_ge(o_done, gate)
                    pt = (prob_t if heads[k] < HEADS else prob_t2)[:, heads[k] % 2]
                    pe.matmul(out[:, 0:256], lhs(0), pt[:, 0:256], start=True, stop=False, skip_group_check=True)
                    pe.matmul(out[:, 128:256], lhs(1), pt[:, 256:384], start=False, stop=True, skip_group_check=True).then_inc(pv_done, 1)

                score(0)
                score(1)
                for k in range(n):
                    turn(k)
                    if k + 2 < n:
                        score(k + 2)
                    weigh(k)

            pe.wait_ge(const_ready, 1)
            pe.wait_ge(rbb_ready, 2)
            pe.wait_ge(s_oh, 16)
            for h in range(HEADS):
                if h >= 2:
                    pe.wait_ge(row_ev, h - 1)
                pe.matmul(bank[h % 2][:, :], rbb[0:33, h, :], onehot_sb[0:33, :], start=True, stop=True).then_inc(row_mm, 1)
            norm_stat(N_MIX0, 6)
            mod_reduce(G_MIX0, 7, 8)

            for i in range(10):
                s = B_WIN + i
                need_slab(s)
                if i in (0, 1):
                    pe.wait_ge(row_ev, HEADS)
                if 4 <= i < 9:
                    pe.wait_ge(xbr_ready, i - 3)
                if i == 9:
                    pe.wait_ge(y_ready, 1)
                feature_slab(s, bank[i % 4], before(APPLY_CHUNKS, A_MIX0) if i == 0 else None).then_inc(slab_done, 1)
            for hd in range(LHEADS):
                s = B_GATE + hd // 2
                if hd % 2 == 0:
                    need_slab(s)
                pe.wait_ge(xcl_ready, hd + 1)
                for k in range(2):
                    b = (2 * hd + k) % 4
                    if hd >= 2:
                        pe.wait_ge(gates_ready, 2 * (hd - 2) + k + 1)
                    for c in range(2):
                        for m in range(2):
                            mm = product(bank[b][:, m * S:(m + 1) * S], *weights(s, (hd % 2) * 1024 + c * 512 + k * 256 + m * P, P),
                                         a_hi[:, 2 * hd + c, :], a_lo[:, 2 * hd + c, :], start=(c == 0 and m == 0), stop=(c == 1))
                    mm.then_inc(slab_done if k == 1 and hd in GATE_ENDS else gate_done, 1)
            pe.wait_ge(gates_ready, 2 * LHEADS)
            mod_reduce(G_A0, 2, 16)
            mod_reduce(G_B0, 3, 24)
            for i in range(LHEADS):
                need_slab(B_LOUT + i)
                pe.wait_ge(zl_ready, i + 1)
                sums_slab(B_LOUT + i, a_hi[:, 2 * i:2 * i + 2], a_lo[:, 2 * i:2 * i + 2], i == 0, i == LHEADS - 1).then_inc(slab_done, 1)
            norm_stat(N_FFN0, 0)
            ffn(0, B_FFN0, A_FFN0)

            mod_reduce(G_KV, 2, 40)
            mod_reduce(G_MIX1, 3, 40)
            norm_stat(N_KV, 0)
            for i in range(4):
                need_slab(B_KV + i)
                if i >= 2:
                    pe.wait_ge(modc_ready, i + 2)
                if i < 2:
                    mm = feature_slab(B_KV + i, bank[i], before(APPLY_CHUNKS, A_KV) if i == 0 else None)
                else:
                    mm = token_slab(B_KV + i, bank[i])
                mm.then_inc(slab_done, 1)
            for i in range(4):
                need_slab(B_Q + i)
                pe.wait_ge(qkv_act, i + 1)
                feature_slab(B_Q + i, bank[i], before(APPLY_CHUNKS, A_MIX1) if i == 0 else None).then_inc(slab_done, 1)
            pe.wait_ge(qkv_act, 8)
            attention(list(range(HEADS)),
                      lambda k, t: [(q_a[:, k, t * P:(t + 1) * P], k_a[:, k // 2, 0:P * (t + 1)])],
                      lambda k: (lambda kt: v_a[:, kt, (k // 2) * P:(k // 2 + 1) * P], bank[4 + k % 2][:, 0:256], k - 1 if k >= 2 else None), 0)
            mod_reduce(G_A1, 0, 56)
            mod_reduce(G_B1, 1, 56)
            for i in range(4):
                need_slab(B_O + i)
                pe.wait_ge(o_done, 2 * i + 2 if i else HEADS)
                sums_slab(B_O + i, a_hi[:, 2 * i:2 * i + 2], a_lo[:, 2 * i:2 * i + 2], i == 0, i == 3).then_inc(slab_done, 1)
            norm_stat(N_FFN1, 2)
            ffn(1, B_FFN1, A_FFN1)
            norm_stat(N_FIN, 0)

            for l in range(LAYERS2):
                norm_stat(norm2(l, L_PRE1), 1)
                ffn(2 + 2 * l, base2(l), apply2(l, LA_PRE1))
                norm_stat(norm2(l, L_POST1), 0)
                norm_stat(norm2(l, L_PREMIX), 1)
                b = base2(l, M_MIX)
                d0, c0 = 8 * l, 8 + 8 * l
                for i in range(8):
                    need_slab(b + i)
                    if i in (4, 5, 6, 7):
                        pe.wait_ge(qkv_dve, d0 + i - 3)
                    if i < 6:
                        mm = feature_slab(b + i, bank[i % 4], before(APPLY_CHUNKS, apply2(l, LA_PREMIX)) if i == 0 else None)
                    else:
                        mm = token_slab(b + i, bank[i % 4])
                    mm.then_inc(slab_done, 1)
                    if i == 5:
                        norm_stat(norm2(l, L_QLAT), 6)
                    if i == 6:
                        norm_stat(norm2(l, L_KVLAT), 7)
                sC, sQ = b + 8, b + 9
                need_slab(sC)
                pe.wait_ge(qkv_dve, d0 + 5)
                feature_slab(sC, bank[0], None, 1, P).then_inc(up_done, 1)
                at = before(APPLY_CHUNKS, apply2(l, LA_KVLAT))
                pe.wait_ge(nl_ready, at + 1)
                pe.wait_ge(qkv_dve, d0 + 6)
                lat_h, lat_l = hid_hi[:, 0, 0, :], hid_lo[:, 0, 0, :]
                for k in range(2):
                    if k == 1:
                        pe.wait_ge(qkv_act, c0 + 1)
                    for m in range(2):
                        mm = product(bank[1 + k][:, m * S:(m + 1) * S], *weights(sC, 1024 + (2 * k + m) * P, P), lat_h, lat_l,
                                     start=(m == 0), stop=True)
                    mm.then_inc(up_done, 1)
                for t in range(2):
                    wh, wl = weights(sC, 1024 + 512, 512)
                    tk = slice(t * P, (t + 1) * P)
                    mm = product(bank[4 + t][:, :], lat_h[:, tk], lat_l[:, tk], wh, wl, start=True, stop=True)
                    if t == 0:
                        mm.then_inc(up_done, 1)
                mm.then_inc(slab_done, 1)
                need_slab(sQ)
                at = before(APPLY_CHUNKS, apply2(l, LA_QLAT))
                pe.wait_ge(nl_ready, at + 2)
                pe.wait_ge(qkv_act, c0 + 2)
                for k, out in enumerate((bank[3], bank[6], bank[7], bank[0])):
                    if k == 3:
                        pe.wait_ge(qkv_dve, d0 + 7)
                    for c in range(2):
                        for m in range(2):
                            mm = product(out[:, m * S:(m + 1) * S], *weights(sQ, c * 1024 + (2 * k + m) * P, P),
                                         a_hi[:, 8 + c, :], a_lo[:, 8 + c, :], start=(c == 0 and m == 0), stop=(c == 1))
                    if k < 2:
                        mm.then_inc(up_done, 1)
                mm.then_inc(slab_done, 1)
                pe.wait_ge(qkv_act, c0 + 8)
                pe.wait_ge(qkv_dve, d0 + 8)

                def qk(k, t):
                    tk, keys = slice(t * P, (t + 1) * P), slice(0, P * (t + 1))
                    h = k % HEADS
                    if k < HEADS:
                        r, g = slice(32 * (h % 4), 32 * (h % 4) + 32), 2 * (h // 4)
                        return [(q_dil[r, g + i, tk], k_dil[r, g + i, keys]) for i in range(2)]
                    r = slice(64 * (h % 2), 64 * (h % 2) + 64)
                    at = 32 * rope_slot(h)
                    return [(q_nope[r, h // 2, tk], k_nope[r, h // 2, keys]), (q_rope[at:at + 32, h // 4, tk], kr[at:at + 32, keys])]

                def pv(k):
                    h = k % HEADS
                    v = v_dil if k < HEADS else v_mla
                    r = slice(64 * (h % 2), 64 * (h % 2) + 64)
                    gate = 8 + 8 * l + k // 2 - 1 if k >= 4 and k % 2 == 0 else None
                    return lambda kt: v[:, kt, h * 64:(h + 1) * 64], bank[4 + (k // 2) % 2][r, 0:256], gate

                attention([HEADS + 16 * l + k for k in range(16)], qk, pv, 0)
                norm_stat(norm2(l, L_GMLA), 0)
                norm_stat(norm2(l, L_GDIL), 1)
                for i in range(4):
                    need_slab(base2(l, M_OUT) + i)
                    pe.wait_ge(nl_ready, before(APPLY_CHUNKS, apply2(l, LA_GMLA)) + 2 * i + 2)
                    sums_slab(base2(l, M_OUT) + i, a_hi[:, 2 * i:2 * i + 2], a_lo[:, 2 * i:2 * i + 2], i == 0, i == 3).then_inc(slab_done, 1)
                norm_stat(norm2(l, L_POSTMIX), 0)
                norm_stat(norm2(l, L_PRE2), 1)
                ffn(3 + 2 * l, base2(l, M_FFN), apply2(l, LA_PRE2))
                norm_stat(norm2(l, L_POST2), 0)
                need_slab(base2(l, M_PLE))
                pe.wait_ge(pl_ready, l + 1)
                pe.wait_ge(f_ready, 4 * (4 * l + 2) + 4)
                for m in range(CH):
                    for k in range(2):
                        mm = product(bank[4 + m // 2][:, (m % 2) * S:(m % 2 + 1) * S], *weights(base2(l, M_PLE), k * D + m * P, P),
                                     hid_hi[:, 1, k, :], hid_lo[:, 1, k, :], start=(k == 0 and m % 2 == 0), stop=(k == 1))
                mm.then_inc(slab_done, 1)
                norm_stat(norm2(l, L_PREPLE), 1)
                for i in range(4):
                    need_slab(base2(l, M_PGATE) + i)
                    if i == 1:
                        pe.wait_ge(var_ready, norm2(l, L_PREPLE) + 1)
                    feature_slab(base2(l, M_PGATE) + i, bank[i], before(APPLY_CHUNKS, apply2(l, LA_PREPLE)) if i == 0 else None).then_inc(slab_done, 1)
                norm_stat(norm2(l, L_POSTPLE), 0)

        @block.scalar
        def _(act):
            made = [0]

            def split_to(n):
                for s in range(made[0], min(n, SLABS)):
                    act.wait_ge(landed[s % RING], 16 * (s // RING + 1))
                    if s >= RING:
                        act.wait_ge(slab_done, s - RING + 1)
                    act.copy(w_hi[:, s % RING, :], raw[:, s % RING, :]).then_inc(hi_ready, 1)
                made[0] = max(made[0], min(n, SLABS))

            def squares(n, src, ready):
                for c in range(NORM_CHUNKS[n]):
                    ready(c)
                    act.activation(sq[:, norm_at(n) + c, :], src(c), ACT.Square).then_inc(sq_ready, 1)

            def rsqrt(n):
                act.wait_ge(var_ready, n + 1)
                act.activation(rs0[:, :], var[:, :], ACT.Abs_reciprocal_sqrt).then_inc(rs0_ready, 1)

            def normed_hi(ap, out, shift=None, free=None, at=0):
                if free is not None:
                    act.wait_ge(slab_done, free)
                for c in range(APPLY_CHUNKS[ap]):
                    act.wait_ge(nt_ready, before(APPLY_CHUNKS, ap) + c + 1)
                    if shift is None:
                        ins = act.copy(out(c), sq[:, at + c, :])
                    else:
                        ins = act.activation(out(c), sq[:, c, :], ACT.Identity, bias=shift(c))
                    ins.then_inc(nh_ready, 1)

            def residual(u):
                return lambda c: act.wait_ge(x_ready, CH * u + c + 1)

            def x_norm(n, u):
                squares(n, lambda c: x[:, c, :], residual(u))
                rsqrt(n)

            def a_out(c):
                return a_hi[:, c, :]

            def ffn(i, b):
                f0 = FJ * i

                def silu(j, par, done):
                    act.wait_ge(slab_done, done)
                    if j is not None:
                        act.wait_ge(hid_done, j + (f0 - 1))
                    act.activation(gate_s[:, par, :], bank[par][:, :], ACT.Silu).then_inc(silu_done, 1)

                def hidden_hi(j, par, done):
                    act.wait_ge(hid_done, j + (f0 + 1))
                    if done is not None:
                        act.wait_ge(slab_done, done)
                    act.copy(hid_hi[:, par].rearrange("p c s -> p (c s)"), hid[:, par, :]).then_inc(hh_ready, 1)

                def high(count, land, slot):
                    act.wait_ge(landed[slot], land)
                    act.wait_ge(slab_done, count)
                    act.copy(w_hi[:, slot, :], raw[:, slot, :]).then_inc(hi_ready, 1)

                silu(None, 0, b + 1)
                split_to(b + 5)
                hidden_hi(0, 0, None)
                silu(None, 1, b + 3)
                split_to(b + 7)
                hidden_hi(1, 1, None)
                split_to(b + 8)
                with act.Fori(0, (FJ - 3) // 2) as k:
                    for h in range(2):
                        g = b + 5 + 3 * h
                        silu(2 * k + (2 + h), h, 6 * k + (g + 1))
                        for d in (0, 1):
                            high(6 * k + (g + d + 1), 32 * k + 16 * ((g + d + 3) // RING + 1), (g + d) % RING)
                        hidden_hi(2 * k + (2 + h), h, 6 * k + (b + 5 + 3 * h))
                        high(6 * k + (g + 3), 32 * k + 16 * ((g + 5) // RING + 1), (g + 2) % RING)
                made[0] = b + 3 * (FJ - 2) + 5
                j = FJ - 1
                silu(j, j % 2, b + 3 * j)
                split_to(b + 3 * j + 4)
                hidden_hi(j, j % 2, b + 3 * j - 1)
                split_to(b + 3 * j + 5)

            act.wait_ge(s_cols, 16)
            act.activation(cs[:, :], cols[:, COL_AT["c"]:COL_AT["c"] + CH], ACT.Silu).then_inc(cs_ready, 1)
            lam_c = cols[:, COL_AT["lambda"]:COL_AT["lambda"] + LCH]
            act.activation(lam[:, 0, :], lam_c, ACT.Abs).then_inc(lam_act, 1)
            act.wait_ge(lam_act, 1)
            act.activation(lam[:, 1, :], lam[:, 0, :], ACT.Exp, scale=-1.0).then_inc(lam_act, 1)
            act.wait_ge(s_x, 16)
            squares(N_MIX0, lambda c: x[:, c, :], lambda c: None)
            for h in range(HEADS):
                act.wait_ge(row_mm, h + 1)
                act.copy(bias_rows[:, h, :], bank[h % 2][:, :]).then_inc(row_ev, 1)
            act.wait_ge(row_ev, HEADS)
            act.dma_start(scratch.rearrange("h p s -> p h s"), bias_rows).then_inc(s_rows, 16)
            split_to(RING)
            rsqrt(N_MIX0)
            normed_hi(A_MIX0, a_out, lambda c: modcol(G_MIX0, c))

            for i in range(5):
                s = B_WIN + i
                act.wait_ge(slab_done, s + 1)
                if i == 0:
                    act.wait_ge(pad_zero, 1)
                if i >= 2:
                    act.wait_ge(conv_done, i - 1)
                sums = bank[i % 4]
                act.copy(xp[:, i % 2, :, 3:S + 3], sums[:, :].rearrange("p (c s) -> p c s", c=2))
                for m in range(2):
                    c = 2 * i + m
                    ins = act.activation(xc[:, c, :], sums[:, m * S:(m + 1) * S], ACT.Identity,
                                         scale=col("conv_w", 3 * LCH + c), bias=col("conv_b", c))
                ins.then_inc(xbr_ready, 1)
                split_to(s + 4)
            for i in range(5):
                s = B_WIN + 5 + i
                act.wait_ge(slab_done, s + 1)
                act.activation(y_br[:, 2 * i:2 * i + 2, :].rearrange("p c s -> p (c s)"), bank[(5 + i) % 4][:, :],
                               ACT.Gelu_apprx_tanh).then_inc(y_ready, 1)
                split_to(s + 4)
            act.wait_ge(slab_done, B_GATE)
            for hd in range(LHEADS):
                act.wait_ge(conv_done, hd + 1)
                act.copy(a_hi[:, 2 * hd:2 * hd + 2, :], xc[:, 2 * hd:2 * hd + 2, :]).then_inc(xch_ready, 1)
            act.wait_ge(s_rows, 16)
            for hd in range(LHEADS):
                for k, dst in enumerate((r_g, i_g)):
                    if k == 1 and hd in GATE_ENDS:
                        act.wait_ge(slab_done, B_GATE + hd // 2 + 1)
                    else:
                        act.wait_ge(gate_done, 2 * hd + k + 1 - sum(h < hd for h in GATE_ENDS))
                    for m in range(2):
                        c = 2 * hd + m
                        ins = act.activation(dst[:, c, :], bank[(2 * hd + k) % 4][:, m * S:(m + 1) * S], ACT.Sigmoid,
                                             bias=col("b_gates", k * LCH + c))
                    ins.then_inc(gates_ready, 1)
            act.wait_ge(lam_dve, LAM_STEPS)
            for hd in range(LHEADS):
                act.wait_ge(bi_ready, hd + 1)
                for c in (2 * hd, 2 * hd + 1):
                    act.activation(xc[:, c, :], r_g[:, c, :], ACT.Exp, scale=lam[:, 6, c:c + 1])
                    ins = act.activation(r_g[:, c, :], r_g[:, c, :], ACT.Tanh, scale=lam[:, 7, c:c + 1])
                ins.then_inc(decay_ready, 1)
            for hd in range(LHEADS):
                act.wait_ge(mult2_ready, hd + 1)
                v = r_g[:, 2 * hd:2 * hd + 2, :]
                act.activation(v, v, ACT.Sqrt).then_inc(mult_ready, 1)
            for hd in range(LHEADS):
                act.wait_ge(z_ready, hd + 1)
                act.copy(a_hi[:, 2 * hd:2 * hd + 2, :], i_g[:, 2 * hd:2 * hd + 2, :]).then_inc(zh_ready, 1)
            split_to(B_FFN0 + 2)
            x_norm(N_FFN0, U_LRU)
            normed_hi(A_FFN0, a_out, lambda c: modcol(G_A0, CH + c))
            act.wait_ge(zl_ready, LHEADS)
            for t, n in ((0, P), (1, 256)):
                skew = bass.AP(tensor=scratch.tensor, offset=255 - P * t, ap=[[511, P], [512 * P, HEADS], [1, n]])
                act.dma_start(bias[:, :, P * t:P * t + n], skew).then_inc(s_bias, 16)
            split_to(B_FFN0 + 3)
            ffn(0, B_FFN0)

            split_to(B_KV + 2)
            x_norm(N_KV, U_FFN0)
            normed_hi(A_KV, a_out, lambda c: modcol(G_KV, c))
            split_to(B_KV + 3)
            for i in range(4):
                act.wait_ge(slab_done, B_KV + i + 1)
                dst = k_a[:, 2 * i:2 * i + 2, :] if i < 2 else v_a[:, :, 256 * (i - 2):256 * (i - 1)]
                act.copy(dst, bank[i][:, :].rearrange("p (c s) -> p c s", c=2)).then_inc(qkv_act, 1)
                if i == 3:
                    normed_hi(A_MIX1, a_out, lambda c: modcol(G_MIX1, c), B_Q)
                split_to(B_KV + i + 4)
            for i in range(4):
                act.wait_ge(slab_done, B_Q + i + 1)
                act.activation(q_a[:, 2 * i:2 * i + 2, :], bank[i][:, :].rearrange("p (c s) -> p c s", c=2), ACT.Copy,
                               scale=P ** -0.5).then_inc(qkv_act, 1)
                split_to(B_Q + i + 4)

            def attention(heads, copy_out=None):
                n = len(heads)

                def exps(k):
                    h = heads[k]
                    act.wait_ge(sc_done, h + 1)
                    if k >= 2:
                        act.wait_ge(tr_done, h - 1)
                    src, dst = (sc, prob) if h < HEADS else (sc2, prob2)
                    for t, (lo, hi) in enumerate(((0, P), (P, 384))):
                        ins = act.activation(dst[:, h % 2, lo:hi], src[:, h % 2, lo:hi], ACT.Exp, scale=-1.0,
                                             bias=nmax[:, h % 2, t:t + 1], accum_out=ssum[:, h % 2, t:t + 1])
                    ins.then_inc(exp_done, 1)

                def turned(k):
                    h = heads[k]
                    act.wait_ge(tr_done, h + 1)
                    if k >= 2:
                        act.wait_ge(pv_done, h - 1)
                    act.copy((prob_t if h < HEADS else prob_t2)[:, h % 2, :], bank[2 + k % 2][:, 0:384]).then_inc(pt_done, 1)

                exps(0)
                for k in range(n):
                    if k + 1 < n:
                        exps(k + 1)
                    turned(k)
                    if copy_out is not None and k >= 1:
                        copy_out(k - 1)
                if copy_out is not None:
                    copy_out(n - 1)

            def moba_out(h):
                act.wait_ge(pv_done, h + 1)
                act.copy(a_hi[:, h, :], bank[4 + h % 2][:, 0:256]).then_inc(oh_done, 1)

            attention(list(range(HEADS)), moba_out)
            split_to(B_FFN1 + 2)
            x_norm(N_FFN1, U_MOBA)
            normed_hi(A_FFN1, a_out, lambda c: modcol(G_A1, CH + c))
            split_to(B_FFN1 + 3)
            ffn(1, B_FFN1)
            split_to(B_L2 + 2)
            x_norm(N_FIN, U_FFN1)

            def post(l, k, n):
                for c in range(CH):
                    act.wait_ge(f_ready, 4 * (4 * l + k) + c // 2 + 1)
                    act.activation(sq[:, c, :], f[:, c, :], ACT.Square).then_inc(sq_ready, 1)
                rsqrt(n)

            for l in range(LAYERS2):
                x_norm(norm2(l, L_PRE1), U_FIN if l == 0 else u2(l - 1, 3))
                normed_hi(apply2(l, LA_PRE1), a_out)
                split_to(base2(l) + 3)
                if l == 0:
                    for k in range(4):
                        act.wait_ge(trig_step, TRIG_AT[k])
                        act.activation(rope[:, k, :], red[:, k % 2, :], ACT.Sin).then_inc(trig_act, 1)
                ffn(2 + 2 * l, base2(l))
                b = base2(l, M_MIX)
                split_to(b + 2)
                post(l, 0, norm2(l, L_POST1))
                x_norm(norm2(l, L_PREMIX), u2(l, 0))
                normed_hi(apply2(l, LA_PREMIX), a_out)
                split_to(b + 3)
                c0, d0 = 8 + 8 * l, 8 * l
                split_to(b + 4)
                squares(norm2(l, L_QLAT), lambda c: q_lat[:, c, :], lambda c: act.wait_ge(qkv_dve, d0 + 1))
                split_to(b + 5)
                split_to(b + 9)
                rsqrt(norm2(l, L_QLAT))
                normed_hi(apply2(l, LA_QLAT), lambda c: a_hi[:, 8 + c, :])
                squares(norm2(l, L_KVLAT), lambda c: kv_lat[:, c, :], lambda c: act.wait_ge(qkv_dve, d0 + 2))
                act.wait_ge(slab_done, b + 7)
                act.copy(v_dil[:, :, 0:256], bank[2][:, :].rearrange("p (c s) -> p c s", c=2)).then_inc(qkv_act, 1)
                split_to(b + 10)
                rsqrt(norm2(l, L_KVLAT))
                normed_hi(apply2(l, LA_KVLAT), lambda c: hid_hi[:, 0, 0, :], at=2)
                act.wait_ge(slab_done, b + 8)
                act.copy(v_dil[:, :, 256:512], bank[3][:, :].rearrange("p (c s) -> p c s", c=2)).then_inc(qkv_act, 1)
                split_to(b + 11)
                for k in range(2):
                    act.wait_ge(up_done, UP2 * l + 2 + k)
                    act.copy(k_nope[:, 2 * k:2 * k + 2, :], bank[1 + k][:, :].rearrange("p (c s) -> p c s", c=2)).then_inc(qkv_act, 1)
                act.wait_ge(up_done, UP2 * l + 4)
                act.copy(v_mla[:, 0, :], bank[4][:, :]).then_inc(qkv_act, 1)
                act.wait_ge(slab_done, b + 9)
                act.copy(v_mla[:, 1, :], bank[5][:, :]).then_inc(qkv_act, 1)
                split_to(b + 12)
                for k, src in enumerate((bank[3], bank[6])):
                    act.wait_ge(up_done, UP2 * l + 5 + k)
                    act.activation(q_nope[:, 2 * k:2 * k + 2, :], src[:, :].rearrange("p (c s) -> p c s", c=2), ACT.Copy,
                                   scale=96 ** -0.5).then_inc(qkv_act, 1)
                act.wait_ge(slab_done, b + 10)
                split_to(b + 13)
                attention([HEADS + 16 * l + k for k in range(16)])
                o0 = 8 + 8 * l
                squares(norm2(l, L_GMLA), lambda c: f[:, c, :], lambda c: act.wait_ge(o_done, o0 + 8))
                squares(norm2(l, L_GDIL), lambda c: f[:, 4 + c, :], lambda c: None)
                rsqrt(norm2(l, L_GMLA))
                rsqrt(norm2(l, L_GDIL))
                normed_hi(apply2(l, LA_GMLA), a_out, None, b + 10)
                normed_hi(apply2(l, LA_GDIL), lambda c: a_hi[:, 4 + c, :], at=4)
                bf = base2(l, M_FFN)
                split_to(bf + 2)
                post(l, 1, norm2(l, L_POSTMIX))
                x_norm(norm2(l, L_PRE2), u2(l, 1))
                normed_hi(apply2(l, LA_PRE2), a_out)
                split_to(bf + 3)
                ffn(3 + 2 * l, bf)
                act.wait_ge(slab_done, bf + 3 * FJ)
                act.copy(hid_hi[:, 1], ptok[:, l]).then_inc(ph_ready, 1)
                split_to(bf + 3 * FJ + 3)
                post(l, 2, norm2(l, L_POST2))
                x_norm(norm2(l, L_PREPLE), u2(l, 2))
                normed_hi(apply2(l, LA_PREPLE), a_out)
                split_to(bf + 3 * FJ + 4)
                for i in range(4):
                    act.wait_ge(slab_done, base2(l, M_PGATE) + i + 1)
                    if i >= 2:
                        act.wait_ge(f_ready, 4 * (4 * l + 3) + i - 1)
                    act.activation(gate_s[:, i % 2, :], bank[i][:, :], ACT.Sigmoid).then_inc(pg_ready, 1)
                    split_to(base2(l, M_PGATE) + i + 4)
                post(l, 3, norm2(l, L_POSTPLE))

        @block.vector
        def _(dve):
            made = [0]
            steps = [0]
            trig = [0]

            def split_to(n):
                for s in range(made[0], min(n, SLABS)):
                    dve.wait_ge(hi_ready, s + 1)
                    dve.tensor_tensor(w_lo[:, s % RING, :], raw[:, s % RING, :], w_hi[:, s % RING, :].bitcast(F32),
                                      ALU.subtract).then_inc(lo_ready, 1)
                made[0] = max(made[0], min(n, SLABS))

            def mod(g, kc):
                s = steps[0]
                dve.wait_ge(mod_landed[s % MOD_RING], 16 * (s // MOD_RING + 1))
                acc = mod_acc[:, g % 2, :]
                if kc == 0:
                    if g >= 2:
                        dve.wait_ge(mod_red, g - 1)
                    ins = dve.tensor_scalar(acc, mod_raw[:, s % MOD_RING, :], cs[:, 0:1], None, ALU.mult)
                else:
                    dve.wait_ge(mod_step, s)
                    ins = dve.scalar_tensor_tensor(out=acc, in0=mod_raw[:, s % MOD_RING, :], scalar=cs[:, kc:kc + 1], in1=acc,
                                                   op0=ALU.mult, op1=ALU.add)
                ins.then_inc(mod_step, 1)
                steps[0] += 1

            def mod_columns(g, b):
                dve.wait_ge(mod_red, g + 1)
                at = COL_AT["mod_b"] + 16 * g
                dve.tensor_tensor(modc[:, 16 * g:16 * g + 16], bank[b][:, 0:16], cols[:, at:at + 16], ALU.add).then_inc(modc_ready, 1)

            def scale_of(k, g, at, gain):
                dve.wait_ge(modc_ready, g + 1)
                dve.scalar_tensor_tensor(out=scale1[:, CH * k:CH * k + CH], in0=modc[:, 16 * g + at:16 * g + at + CH], scalar=1.0,
                                         in1=cols[:, gain:gain + CH], op0=ALU.add, op1=ALU.mult).then_inc(scale_ready, 1)

            def root(n, b, features):
                dve.wait_ge(stat_ready, n + 1)
                dve.tensor_scalar(var[:, :], bank[b][:, 0:S], 1.0 / features, EPS, ALU.mult, ALU.add).then_inc(var_ready, 1)
                dve.wait_ge(rs0_ready, n + 1)
                dve.scalar_tensor_tensor(out=nwt[:, :], in0=rs0[:, :], scalar=-0.5, in1=rs0[:, :], op0=ALU.mult, op1=ALU.mult).then_inc(newton, 1)
                dve.wait_ge(newton, 2 * n + 1)
                dve.tensor_tensor(nwt[:, :], nwt[:, :], var[:, :], ALU.mult).then_inc(newton, 1)
                dve.wait_ge(newton, 2 * n + 2)
                dve.scalar_tensor_tensor(out=rstd[:, n % 2, :], in0=nwt[:, :], scalar=1.5, in1=rs0[:, :], op0=ALU.add, op1=ALU.mult).then_inc(rstd_ready, 1)
                dve.wait_ge(rstd_ready, n + 1)

            def normed(ap, n, src, gain, hi, lo, shift=None, at=0):
                a0, m = before(APPLY_CHUNKS, ap), APPLY_CHUNKS[ap]

                def low(c):
                    dve.wait_ge(nh_ready, a0 + c + 1)
                    if shift is None:
                        ins = dve.tensor_tensor(lo(c), sq[:, at + c, :], hi(c).bitcast(F32), ALU.subtract)
                    else:
                        ins = dve.scalar_tensor_tensor(out=lo(c), in0=sq[:, at + c, :], scalar=shift(c), in1=hi(c).bitcast(F32),
                                                       op0=ALU.add, op1=ALU.subtract)
                    ins.then_inc(nl_ready, 1)

                for c in range(m):
                    dve.scalar_tensor_tensor(out=sq[:, at + c, :], in0=src(c), scalar=gain(c), in1=rstd[:, n % 2, :],
                                             op0=ALU.mult, op1=ALU.mult).then_inc(nt_ready, 1)
                    if c >= 1:
                        low(c - 1)
                low(m - 1)

            def x_src(c):
                return x[:, c, :]

            def a_h(c):
                return a_hi[:, c, :]

            def a_l(c):
                return a_lo[:, c, :]

            def bank_sums(phase, b4, slab):
                if b4 < 3:
                    dve.wait_ge(bank_done, 3 * phase + b4 + 1)
                else:
                    dve.wait_ge(slab_done, slab + 1)

            def add_gated(phase, slab, gate):
                for c in range(CH):
                    if c % 2 == 0:
                        bank_sums(phase, c // 2, slab)
                    dve.scalar_tensor_tensor(out=x[:, c, :], in0=bank[4 + c // 2][:, (c % 2) * S:(c % 2 + 1) * S], scalar=gate(c),
                                             in1=x[:, c, :], op0=ALU.mult, op1=ALU.add).then_inc(x_ready, 1)

            def ffn(i, b, mods_in_loop=False):
                f0 = FJ * i

                def hidden(j, par, up):
                    dve.wait_ge(silu_done, j + (f0 + 1))
                    dve.wait_ge(slab_done, up)
                    dve.tensor_tensor(hid[:, par, :], bank[2 + par][:, :], gate_s[:, par, :], ALU.mult).then_inc(hid_done, 1)

                def hidden_lo(j, par):
                    dve.wait_ge(hh_ready, j + (f0 + 1))
                    dve.tensor_tensor(hid_lo[:, par].rearrange("p c s -> p (c s)"), hid[:, par, :],
                                      hid_hi[:, par].rearrange("p c s -> p (c s)").bitcast(F32), ALU.subtract).then_inc(hl_ready, 1)

                def low(count, slot):
                    dve.wait_ge(hi_ready, count)
                    dve.tensor_tensor(w_lo[:, slot, :], raw[:, slot, :], w_hi[:, slot, :].bitcast(F32), ALU.subtract).then_inc(lo_ready, 1)

                split_to(b + 4)
                hidden(0, 0, b + 2)
                split_to(b + 5)
                hidden_lo(0, 0)
                split_to(b + 6)
                hidden(1, 1, b + 4)
                split_to(b + 7)
                hidden_lo(1, 1)
                split_to(b + 8)
                if mods_in_loop:
                    for g in (G_KV, G_MIX1):
                        dve.wait_ge(mod_red, g - 1)
                        dve.memset(mod_acc[:, g % 2, :], 0.0).then_inc(acc_zero, 1)
                    dve.wait_ge(acc_zero, 2)
                s0 = steps[0]
                with dve.Fori(0, (FJ - 3) // 2) as k:
                    for h in range(2):
                        g = b + 5 + 3 * h
                        low(6 * k + (g + 4), g % RING)
                        hidden(2 * k + (2 + h), h, 6 * k + (g + 2))
                        low(6 * k + (g + 5), (g + 1) % RING)
                        hidden_lo(2 * k + (2 + h), h)
                        low(6 * k + (g + 6), (g + 2) % RING)
                        if mods_in_loop:
                            for m, gr in enumerate((G_KV, G_MIX1)):
                                e = 2 * h + m
                                dve.wait_ge(mod_landed[(s0 + e) % MOD_RING], 32 * k + 16 * ((s0 + e) // MOD_RING + 1))
                                dve.wait_ge(mod_step, 4 * k + (s0 + e - 1))
                                acc = mod_acc[:, gr % 2, :]
                                dve.scalar_tensor_tensor(out=acc, in0=mod_raw[:, (s0 + e) % MOD_RING, :], scalar=cs[:, bass.ds(2 * k + h, 1)],
                                                         in1=acc, op0=ALU.mult, op1=ALU.add).then_inc(mod_step, 1)
                if mods_in_loop:
                    steps[0] += 16
                made[0] = b + 3 * (FJ - 2) + 5
                j = FJ - 1
                split_to(b + 3 * j + 3)
                hidden(j, j % 2, b + 3 * j + 1)
                split_to(b + 3 * j + 4)
                hidden_lo(j, j % 2)
                split_to(b + 3 * j + 5)

            dve.wait_ge(s_rb, 16)
            dve.tensor_copy(rbb[0:32, :, :], rb_sb[:, :].unsqueeze(2).to_broadcast([32, HEADS, P])).then_inc(rbb_ready, 1)
            dve.memset(rbb[32:33, :, :], 1.0).then_inc(rbb_ready, 1)
            dve.memset(xp[:, :, :, 0:3], 0.0).then_inc(pad_zero, 1)
            dve.wait_ge(cs_ready, 1)
            for kc in range(8):
                mod(G_MIX0, kc)
            dve.wait_ge(lam_act, 2)
            lam_n = [0]

            def lam_link(ins):
                lam_n[0] += 1
                ins.then_inc(lam_dve, 1)
                dve.wait_ge(lam_dve, lam_n[0])

            u, s1, s2, v = lam[:, 1, :], lam[:, 2, :], lam[:, 3, :], lam[:, 4, :]
            lam_link(dve.tensor_scalar(v, u, 2.0, None, ALU.add))
            lam_link(dve.reciprocal(s2, v))
            lam_link(dve.tensor_tensor(s1, u, s2, ALU.mult))
            lam_link(dve.tensor_tensor(s2, s1, s1, ALU.mult))
            lam_link(dve.tensor_scalar(v, s2, 1.0 / ATANH_LAST, None, ALU.mult))
            for d in range(ATANH_LAST - 2, 1, -2):
                lam_link(dve.scalar_tensor_tensor(out=v, in0=v, scalar=1.0 / d, in1=s2, op0=ALU.add, op1=ALU.mult))
            lam_link(dve.scalar_tensor_tensor(out=v, in0=v, scalar=1.0, in1=s1, op0=ALU.add, op1=ALU.mult))
            at = COL_AT["lambda"]
            lam_link(dve.tensor_scalar(lam[:, 5, :], cols[:, at:at + LCH], -1.0, 0.0, ALU.mult, ALU.max))
            lam_link(dve.scalar_tensor_tensor(out=v, in0=v, scalar=2.0, in1=lam[:, 5, :], op0=ALU.mult, op1=ALU.add))
            lam_link(dve.tensor_scalar(lam[:, 6, :], v, -8.0, None, ALU.mult))
            lam_link(dve.tensor_scalar(lam[:, 7, :], v, 8.0, None, ALU.mult))
            assert lam_n[0] == LAM_STEPS
            for l in range(LAYERS2):
                for k in range(2):
                    at = COL_AT["gains2"] + 64 * l + CH * (1 + 4 * k)
                    dve.tensor_scalar(half_g[:, 16 * l + CH * k:16 * l + CH * k + CH], cols[:, at:at + CH], 0.5, None, ALU.mult).then_inc(half_ready, 1)
            mod_columns(G_MIX0, 7)
            scale_of(0, G_MIX0, CH, COL_AT["norm_mix"])
            split_to(RING)
            root(N_MIX0, 6, D)
            dve.wait_ge(scale_ready, 1)
            normed(A_MIX0, N_MIX0, x_src, lambda c: scale1[:, c:c + 1], a_h, a_l, lambda c: modcol(G_MIX0, c))

            for i in range(5):
                s = B_WIN + i
                dve.wait_ge(xbr_ready, i + 1)
                for k in range(3):
                    for m in range(2):
                        c = 2 * i + m
                        if k:
                            dve.wait_ge(conv_step, conv_count(i, k - 1, m))
                        ins = dve.scalar_tensor_tensor(out=xc[:, c, :], in0=xp[:, i % 2, m, k:k + S], scalar=col("conv_w", k * LCH + c),
                                                       in1=xc[:, c, :], op0=ALU.mult, op1=ALU.add)
                        ins.then_inc(conv_done if (k, m) == (2, 1) else conv_step, 1)
                split_to(s + 4)
                mod(G_A0, i)
            for i in range(5):
                s = B_WIN + 5 + i
                split_to(s + 4)
                mod(*((G_A0, 5 + i) if i < 3 else (G_B0, i - 3)))
            for hd in range(LHEADS):
                dve.wait_ge(xch_ready, hd + 1)
                dve.tensor_tensor(a_lo[:, 2 * hd:2 * hd + 2, :], xc[:, 2 * hd:2 * hd + 2, :], a_hi[:, 2 * hd:2 * hd + 2, :].bitcast(F32),
                                  ALU.subtract).then_inc(xcl_ready, 1)
            for hd in range(LHEADS):
                h2 = slice(2 * hd, 2 * hd + 2)
                dve.wait_ge(gates_ready, 2 * hd + 2)
                dve.tensor_tensor(i_g[:, h2, :], i_g[:, h2, :], xc[:, h2, :], ALU.mult).then_inc(bi_ready, 1)
                mod(G_B0, 2 + hd)
            mod(G_B0, 7)
            mod_columns(G_A0, 2)
            mod_columns(G_B0, 3)
            scale_of(1, G_B0, 0, COL_AT["norm_ffn"])
            for hd in range(LHEADS):
                h2, tmp = slice(2 * hd, 2 * hd + 2), sq[:, 2 * (hd % 4):2 * (hd % 4) + 2, :]
                dve.wait_ge(decay_ready, hd + 1)
                dve.tensor_tensor(tmp, xc[:, h2, :], xc[:, h2, :], ALU.mult).then_inc(mult2_step, 1)
                dve.wait_ge(mult2_step, hd + 1)
                dve.scalar_tensor_tensor(out=r_g[:, h2, :], in0=tmp, scalar=1.0, in1=r_g[:, h2, :], op0=ALU.add, op1=ALU.mult).then_inc(mult2_ready, 1)

            def z_low(hd):
                h2 = slice(2 * hd, 2 * hd + 2)
                dve.wait_ge(zh_ready, hd + 1)
                dve.tensor_tensor(a_lo[:, h2, :], i_g[:, h2, :], a_hi[:, h2, :].bitcast(F32), ALU.subtract).then_inc(zl_ready, 1)

            for hd in range(LHEADS):
                h2 = slice(2 * hd, 2 * hd + 2)
                dve.wait_ge(mult_ready, hd + 1)
                dve.tensor_tensor(i_g[:, h2, :], i_g[:, h2, :], r_g[:, h2, :], ALU.mult).then_inc(scan_step, 1)
                dve.wait_ge(scan_step, 2 * hd + 1)
                for c in (2 * hd, 2 * hd + 1):
                    ins = dve.tensor_tensor_scan(r_g[:, c, :], xc[:, c, :], i_g[:, c, :], 0.0, ALU.mult, ALU.add)
                ins.then_inc(scan_step, 1)
                dve.wait_ge(scan_step, 2 * hd + 2)
                dve.tensor_tensor(i_g[:, h2, :], r_g[:, h2, :], y_br[:, h2, :], ALU.mult).then_inc(z_ready, 1)
                if hd:
                    z_low(hd - 1)
            z_low(LHEADS - 1)
            split_to(B_FFN0 + 2)
            add_gated(0, B_LOUT + 4, lambda c: modcol(G_A0, c))
            root(N_FFN0, 0, D)
            dve.wait_ge(scale_ready, 2)
            normed(A_FFN0, N_FFN0, x_src, lambda c: scale1[:, CH + c:CH + c + 1], a_h, a_l, lambda c: modcol(G_A0, CH + c))
            split_to(B_FFN0 + 3)
            ffn(0, B_FFN0, True)

            mod_columns(G_KV, 2)
            mod_columns(G_MIX1, 3)
            scale_of(2, G_KV, CH, COL_AT["kv_norm"])
            scale_of(3, G_MIX1, CH, COL_AT["norm_mix"] + CH)
            split_to(B_KV + 2)
            add_gated(1, B_FFN0 + 3 * FJ - 1, lambda c: modcol(G_B0, CH + c))
            root(N_KV, 0, D)
            dve.wait_ge(scale_ready, 4)
            normed(A_KV, N_KV, x_src, lambda c: scale1[:, 2 * CH + c:2 * CH + c + 1], a_h, a_l, lambda c: modcol(G_KV, c))
            split_to(B_KV + 3)
            for i in range(3):
                split_to(B_KV + i + 4)
                mod(G_A1, i)
            normed(A_MIX1, N_KV, x_src, lambda c: scale1[:, 3 * CH + c:3 * CH + c + 1], a_h, a_l, lambda c: modcol(G_MIX1, c))
            split_to(B_KV + 7)
            for i in range(4):
                split_to(B_Q + i + 4)
                mod(G_A1, 3 + i)

            def attention(heads, add, copy_out):
                n = len(heads)

                def scores(k):
                    h = heads[k]
                    dve.wait_ge(qk_done, h + 1)
                    if k >= 2:
                        dve.wait_ge(exp_done, h - 1)
                    dst = sc if h < HEADS else sc2
                    for t, (lo, hi) in enumerate(((0, P), (P, 384))):
                        ins = dve.tensor_tensor_reduce(dst[:, h % 2, lo:hi], bank[k % 2][:, lo:hi], add(k)[:, lo:hi], -1.0, 3.0e38,
                                                       ALU.add, ALU.min, nmax[:, h % 2, t:t + 1])
                    ins.then_inc(sc_done, 1)

                def normalise(k):
                    h = heads[k]
                    pr = prob if h < HEADS else prob2
                    dve.wait_ge(exp_done, h + 1)
                    dve.reciprocal(rsum[:, h % 2, :], ssum[:, h % 2, :]).then_inc(rs_done, 1)
                    dve.wait_ge(rs_done, h + 1)
                    for t, (lo, hi) in enumerate(((0, P), (P, 384))):
                        ins = dve.tensor_scalar(pr[:, h % 2, lo:hi], pr[:, h % 2, lo:hi], rsum[:, h % 2, t:t + 1], None, ALU.mult)
                    ins.then_inc(pn_done, 1)

                scores(0)
                for k in range(n):
                    if k + 1 < n:
                        scores(k + 1)
                    normalise(k)
                    if k >= 1:
                        copy_out(k - 1)
                copy_out(n - 1)

            def moba_out(h):
                dve.wait_ge(oh_done, h + 1)
                dve.tensor_tensor(a_lo[:, h, :], bank[4 + h % 2][:, 0:256], a_hi[:, h, :].bitcast(F32), ALU.subtract).then_inc(o_done, 1)
                if steps[0] < 8 * MOD_GROUPS:
                    mod(*((G_A1, 7) if h == 0 else (G_B1, h - 1)))

            dve.wait_ge(s_bias, 32)
            attention(list(range(HEADS)), lambda k: bias[:, k, :], moba_out)
            mod(G_B1, 7)
            assert steps[0] == 8 * MOD_GROUPS
            mod_columns(G_A1, 0)
            mod_columns(G_B1, 1)
            scale_of(4, G_B1, 0, COL_AT["norm_ffn"] + CH)
            split_to(B_FFN1 + 2)
            add_gated(2, B_O + 3, lambda c: modcol(G_A1, c))
            root(N_FFN1, 2, D)
            dve.wait_ge(scale_ready, 5)
            normed(A_FFN1, N_FFN1, x_src, lambda c: scale1[:, 4 * CH + c:4 * CH + c + 1], a_h, a_l, lambda c: modcol(G_A1, CH + c))
            split_to(B_FFN1 + 3)
            ffn(1, B_FFN1)
            split_to(B_L2 + 2)
            add_gated(3, B_FFN1 + 3 * FJ - 1, lambda c: modcol(G_B1, CH + c))
            root(N_FIN, 0, D)
            for c in range(CH):
                dve.scalar_tensor_tensor(out=x[:, c, :], in0=x[:, c, :], scalar=col("final_norm", c), in1=rstd[:, N_FIN % 2, :],
                                         op0=ALU.mult, op1=ALU.mult).then_inc(x_ready, 1)

            def take_sums(l, k, phase, slab):
                for b4 in range(4):
                    bank_sums(phase, b4, slab)
                    dve.tensor_copy(f[:, 2 * b4:2 * b4 + 2, :].rearrange("p c s -> p (c s)"), bank[4 + b4][:, :]).then_inc(f_ready, 1)

            def post(l, k, n, b, gain):
                root(n, b, D)
                p = 4 * l + k

                def add(c):
                    dve.wait_ge(f_scaled, CH * p + c + 1)
                    dve.tensor_tensor(x[:, c, :], x[:, c, :], f[:, c, :], ALU.add).then_inc(x_ready, 1)

                for c in range(CH):
                    dve.scalar_tensor_tensor(out=f[:, c, :], in0=f[:, c, :], scalar=gain(c), in1=rstd[:, n % 2, :],
                                             op0=ALU.mult, op1=ALU.mult).then_inc(f_scaled, 1)
                    if c:
                        add(c - 1)
                add(CH - 1)

            def gain2(l, k):
                return lambda c: col("gains2", 64 * l + CH * k + c)

            def link(ins):
                trig[0] += 1
                ins.then_inc(trig_step, 1)
                dve.wait_ge(trig_step, trig[0])

            def rope_tables():
                dve.wait_ge(s_late, 48)
                link(dve.tensor_copy(pos_f, pos_i))
                for kind, inv in enumerate(("inv_mla", "inv_dil")):
                    link(dve.tensor_scalar(ang, pos_f, col(inv, 0), None, ALU.mult))
                    for k in range(2):
                        r, t = red[:, k, :], turn[:, k, :]
                        if kind:
                            dve.wait_ge(trig_act, k + 1)
                        link(dve.tensor_scalar(t, ang, 1.0 / TWO_PI, 0.25 if k == 0 else 0.0, ALU.mult, ALU.add))
                        link(dve.tensor_scalar(t, t, MAGIC, -MAGIC, ALU.add, ALU.add))
                        link(dve.scalar_tensor_tensor(out=r, in0=t, scalar=-C1, in1=ang, op0=ALU.mult, op1=ALU.add))
                        link(dve.scalar_tensor_tensor(out=r, in0=t, scalar=-C2, in1=r, op0=ALU.mult, op1=ALU.add))
                        link(dve.scalar_tensor_tensor(out=r, in0=t, scalar=-C3, in1=r, op0=ALU.mult, op1=ALU.add))
                        link(dve.tensor_scalar(r, r, math.pi / 2 if k == 0 else 0.0, PI_SAFE, ALU.add, ALU.min))
                        link(dve.tensor_scalar(r, r, -PI_SAFE, None, ALU.max))
                        assert trig[0] == TRIG_AT[2 * kind + k]
                dve.wait_ge(trig_act, 4)
                dve.tensor_scalar(rope[:, 1, :], rope[:, 1, :], col("sign_mla", 0), None, ALU.mult).then_inc(rope_ready, 1)

            n_rope = [0]

            def rlink(ins):
                n_rope[0] += 1
                ins.then_inc(rope_step, 1)
                return n_rope[0]

            def scaled(out, src, scale, table):
                return rlink(dve.scalar_tensor_tensor(out=out, in0=src, scalar=scale, in1=table, op0=ALU.mult, op1=ALU.mult))

            def place_free(taken):
                if n_rope[0]:
                    dve.wait_ge(rope_step, n_rope[0])
                    dve.wait_ge(qkv_dve, taken)

            def rope_dilated(dst, g, sums, scale, taken):
                va, vb = sums[:, 0:S], sums[:, S:2 * S]
                place_free(taken)
                scaled(rt[:, 0, :], va, scale, rope[:, 2, :])
                scaled(rt[:, 1, :], vb, scale, rope[:, 3, :])
                n = scaled(rt[:, 2, :], vb, scale, rope[:, 2, :])
                n = scaled(rt[:, 3, :], va, scale, rope[:, 3, :])
                dve.wait_ge(rope_step, n - 2)
                rlink(dve.tensor_tensor(dst[:, 2 * g, :], rt[:, 0, :], rt[:, 1, :], ALU.subtract))
                dve.wait_ge(rope_step, n)
                dve.tensor_tensor(dst[:, 2 * g + 1, :], rt[:, 2, :], rt[:, 3, :], ALU.add).then_inc(qkv_dve, 1)

            for l in range(LAYERS2):
                root(norm2(l, L_PRE1), 1, D)
                normed(apply2(l, LA_PRE1), norm2(l, L_PRE1), x_src, gain2(l, 0), a_h, a_l)
                split_to(base2(l) + 3)
                if l == 0:
                    rope_tables()
                ffn(2 + 2 * l, base2(l))
                b = base2(l, M_MIX)
                split_to(b + 2)
                take_sums(l, 0, 4 + 3 * l, b - 1)
                dve.wait_ge(half_ready, 2 * LAYERS2)
                post(l, 0, norm2(l, L_POST1), 0, lambda c: half_g[:, 16 * l + c:16 * l + c + 1])
                root(norm2(l, L_PREMIX), 1, D)
                normed(apply2(l, LA_PREMIX), norm2(l, L_PREMIX), x_src, gain2(l, 2), a_h, a_l)
                split_to(b + 3)
                d0 = 8 * l
                dve.wait_ge(rope_ready, 1)
                dve.wait_ge(slab_done, b + 1)
                dve.tensor_copy(q_lat[:, :, :].rearrange("p c s -> p (c s)"), bank[0][:, :]).then_inc(qkv_dve, 1)
                split_to(b + 4)
                dve.wait_ge(slab_done, b + 2)
                scaled(kr, bank[1][:, S:2 * S], 1.0, rope[:, 0, :])
                dve.tensor_copy(kv_lat[:, 0, :], bank[1][:, 0:S]).then_inc(qkv_dve, 1)
                split_to(b + 5)
                for i in range(4):
                    dve.wait_ge(slab_done, b + 3 + i)
                    rope_dilated(q_dil if i < 2 else k_dil, i % 2, bank[(2 + i) % 4], 64 ** -0.5 if i < 2 else 1.0, d0 + 2 + i)
                    split_to(b + 6 + i)
                root(norm2(l, L_QLAT), 6, 256)
                normed(apply2(l, LA_QLAT), norm2(l, L_QLAT), lambda c: q_lat[:, c, :], lambda c: col("q_norm2", 2 * l + c),
                       lambda c: a_hi[:, 8 + c, :], lambda c: a_lo[:, 8 + c, :])
                split_to(b + 10)
                root(norm2(l, L_KVLAT), 7, P)
                normed(apply2(l, LA_KVLAT), norm2(l, L_KVLAT), lambda c: kv_lat[:, c, :], lambda c: col("kv_norm2", l + c),
                       lambda c: hid_hi[:, 0, 0, :], lambda c: hid_lo[:, 0, 0, :], None, 2)
                split_to(b + 11)
                dve.wait_ge(up_done, UP2 * l + 1)
                place_free(d0 + 6)
                n = scaled(rt[:, 0, :], bank[0][:, 0:S], 1.0, rope[:, 1, :])
                dve.wait_ge(rope_step, n)
                dve.tensor_tensor(kr, kr, rt[:, 0, :], ALU.add).then_inc(qkv_dve, 1)
                split_to(b + 12)
                dve.wait_ge(slab_done, b + 10)
                place_free(d0 + 7)
                for m in range(2):
                    scaled(rt[:, m, :], bank[7][:, m * S:(m + 1) * S], 96 ** -0.5, rope[:, 0, :])
                for m in range(2):
                    n = scaled(rt[:, 2 + m, :], bank[0][:, m * S:(m + 1) * S], 96 ** -0.5, rope[:, 1, :])
                dve.wait_ge(rope_step, n)
                dve.tensor_tensor(q_rope[:, :, :], rt[:, 0:2, :], rt[:, 2:4, :], ALU.add).then_inc(qkv_dve, 1)
                split_to(b + 13)

                def pair_out(k):
                    if k % 2:
                        h = HEADS + 16 * l + k
                        dve.wait_ge(pv_done, h + 1)
                        dve.tensor_copy(f[:, (k // 2 + 4) % 8, :], bank[4 + (k // 2) % 2][:, 0:256]).then_inc(o_done, 1)

                attention([HEADS + 16 * l + k for k in range(16)], lambda k: mask[:, 1 if k < HEADS else 0, :], pair_out)
                root(norm2(l, L_GMLA), 0, 512)
                root(norm2(l, L_GDIL), 1, 512)
                normed(apply2(l, LA_GMLA), norm2(l, L_GMLA), lambda c: f[:, c, :], lambda c: col("group2", CH * l + c), a_h, a_l)
                normed(apply2(l, LA_GDIL), norm2(l, L_GDIL), lambda c: f[:, 4 + c, :], lambda c: col("group2", CH * l + 4 + c),
                       lambda c: a_hi[:, 4 + c, :], lambda c: a_lo[:, 4 + c, :], None, 4)
                bf = base2(l, M_FFN)
                split_to(bf + 2)
                take_sums(l, 1, 5 + 3 * l, bf - 1)
                post(l, 1, norm2(l, L_POSTMIX), 0, gain2(l, 3))
                root(norm2(l, L_PRE2), 1, D)
                normed(apply2(l, LA_PRE2), norm2(l, L_PRE2), x_src, gain2(l, 4), a_h, a_l)
                split_to(bf + 3)
                ffn(3 + 2 * l, bf)
                dve.wait_ge(ph_ready, l + 1)
                dve.tensor_tensor(hid_lo[:, 1], ptok[:, l], hid_hi[:, 1].bitcast(F32), ALU.subtract).then_inc(pl_ready, 1)
                split_to(bf + 3 * FJ + 3)
                take_sums(l, 2, 6 + 3 * l, bf + 3 * FJ - 1)
                post(l, 2, norm2(l, L_POST2), 0, lambda c: half_g[:, 16 * l + CH + c:16 * l + CH + c + 1])
                root(norm2(l, L_PREPLE), 1, D)
                normed(apply2(l, LA_PREPLE), norm2(l, L_PREPLE), x_src, gain2(l, 6), a_h, a_l)
                split_to(bf + 3 * FJ + 4)
                for i in range(4):
                    dve.wait_ge(pg_ready, 4 * l + i + 1)
                    dve.tensor_tensor(f[:, 2 * i:2 * i + 2, :].rearrange("p c s -> p (c s)"), bank[4 + i][:, :], gate_s[:, i % 2, :],
                                      ALU.mult).then_inc(f_ready, 1)
                    split_to(base2(l, M_PGATE) + i + 4)
                post(l, 3, norm2(l, L_POSTPLE), 0, gain2(l, 7))


def rope_slot(h):
    return h % 4 // 2 + 2 * (h % 2)


GATE_ENDS = (1, 3, 4)
ATANH_LAST = 17
LAM_STEPS = 5 + (ATANH_LAST - 3) // 2 + 5
TRIG_AT = [9, 16, 24, 31]
UP2 = 6


def conv_count(i, k, m):
    return 5 * i + 2 * k + m + 1


def wide(w):
    return w.reshape(-1, P, w.shape[1]).transpose(1, 0, 2).reshape(P, -1)


def stream_slabs(a):
    win = a["lru_w_in"][0]
    for at in (LRU, 0):
        for i in range(5):
            yield wide(win[:, at + 256 * i:at + 256 * (i + 1)])
    g = a["lru_w_gates"][0]
    for i in range(0, LHEADS, 2):
        yield np.concatenate([wide(g[h]) if h < LHEADS else np.zeros((P, 1024), np.float32) for h in (i, i + 1)], axis=1)
    yield from tall(a["lru_w_out"][0])
    yield from ffn_slabs(a["ffn_w_gate"][0], a["ffn_w_up"][0], a["ffn_w_down"][0])
    for w in (a["w_kv"], a["attn_w_q"][0]):
        for i in range(4):
            yield wide(w[:, 256 * i:256 * (i + 1)])
    yield from tall(a["attn_w_o"][0])
    yield from ffn_slabs(a["ffn_w_gate"][1], a["ffn_w_up"][1], a["ffn_w_down"][1])
    for l in range(LAYERS2):
        yield from ffn_slabs(a["ffn_gate_2"][l, 0], a["ffn_up_2"][l, 0], a["ffn_down_2"][l, 0])
        w = a["w_in_2"][l]
        kr, rot = w[:, 384:416], np.concatenate([w[:, 400:416], w[:, 384:400]], axis=1)
        yield wide(w[:, 0:256])
        yield wide(np.concatenate([w[:, 256:384]] + [kr] * 4, axis=1))
        for part in range(2):
            v = w[:, 416 + 512 * part:416 + 512 * (part + 1)].reshape(D, 2, 4, 2, 32)
            for g in range(2):
                yield wide(v[:, g].transpose(0, 2, 1, 3).reshape(D, 256))
        for i in range(2):
            yield wide(w[:, 1440 + 256 * i:1440 + 256 * (i + 1)])
        up = a["w_kv_up_2"][l].reshape(P, HEADS, 2, 64).transpose(0, 2, 1, 3).reshape(P, 1024)
        yield np.concatenate([wide(np.concatenate([rot] * 4, axis=1)), up], axis=1)
        q = a["w_q_up_2"][l].reshape(256, HEADS, 96)
        slots = [4 * c + next(h for h in range(4) if rope_slot(h) == s) for c in range(2) for s in range(4)]
        pairs = q[:, slots, 64:]
        turned = np.concatenate([pairs[:, :, 16:], pairs[:, :, :16]], axis=2)
        yield wide(np.concatenate([q[:, :, :64].reshape(256, 512), pairs.reshape(256, 256), turned.reshape(256, 256)], axis=1))
        yield from tall(a["w_out_2"][l])
        yield from ffn_slabs(a["ffn_gate_2"][l, 1], a["ffn_up_2"][l, 1], a["ffn_down_2"][l, 1])
        yield from tall(a["w_ple_2"][l])
        w = a["w_ple_gate_2"][l]
        for i in range(4):
            yield wide(w[:, 256 * i:256 * (i + 1)])


def tall(w):
    for i in range(0, w.shape[0], 256):
        yield wide(w[i:i + 256])


def ffn_slabs(gate, up, down):
    d = list(tall(down))
    for j in range(FJ):
        yield wide(gate[:, 256 * j:256 * (j + 1)])
        yield wide(up[:, 256 * j:256 * (j + 1)])
        if j:
            yield d[j - 1]
    yield d[FJ - 1]


def mod_slabs(a):
    m, kv = a["mod_w"], a["kv_mod_w"]
    groups = [m[0][:, 0:2048], m[0][:, 2048:4096], m[0][:, 4096:6144], kv, m[1][:, 0:2048], m[1][:, 2048:4096], m[1][:, 4096:6144]]
    for pair in ([0], [1], [2], [3, 4], [5], [6]):
        for k in range(8):
            for g in pair:
                yield groups[g][P * k:P * (k + 1)]


def columns(a):
    def cut(v):
        return v.reshape(-1, P).T
    inv_m = (10000.0 ** (-np.arange(0, 32, 2, dtype=np.float32) / np.float32(32))).astype(np.float32)
    inv_d = (10000.0 ** (-np.arange(0, 64, 2, dtype=np.float32) / np.float32(64))).astype(np.float32)
    parts = {
        "c": cut(a["c"]), "norm_mix": cut(a["norm_mix"]), "norm_ffn": cut(a["norm_ffn"]), "kv_norm": cut(a["kv_norm"]),
        "final_norm": cut(a["final_norm"]), "gains2": cut(a["norm_gains_2"]), "q_norm2": cut(a["q_norm_2"]),
        "kv_norm2": cut(a["kv_norm_2"]), "group2": cut(a["group_out_norm_2"]), "conv_w": cut(a["lru_conv_w"]),
        "conv_b": cut(a["lru_conv_b"]), "b_gates": cut(a["lru_b_gates"]), "lambda": cut(a["lru_lambda"]),
        "mod_b": np.concatenate([cut(a["mod_b"][0]), cut(a["kv_mod_b"]), cut(a["mod_b"][1])], axis=1),
        "inv_mla": np.tile(inv_m, 8)[:, None], "inv_dil": np.tile(inv_d, 4)[:, None],
        "sign_mla": np.tile(np.repeat(np.array([-1.0, 1.0], np.float32), 16), 4)[:, None],
    }
    for n, k in COLS:
        assert parts[n].shape == (P, k), (n, parts[n].shape, k)
    return np.ascontiguousarray(np.concatenate([parts[n] for n, _ in COLS], axis=1))


def bucket(dist):
    if dist < 16:
        return dist
    return min(16 + int(math.log(dist / 16) / math.log(8) * 16 + 1e-9), 31)


def shape_constants():
    onehot = np.zeros((33, 512), np.float32)
    for y in range(512):
        if y <= 255:
            onehot[bucket(255 - y), y] = 1.0
        else:
            onehot[32, y] = NEG
    q, k = np.arange(S)[:, None], np.arange(S)[None, :]
    dist = q - k
    causal = np.where(dist >= 0, 0.0, NEG)
    times = (dist >= 0) * sum(((dist % d == 0) & (dist <= w)).astype(int) for w, d in ((128, 1), (512, 4), (2048, 16)))
    dilated = np.where(times > 0, np.log(np.maximum(times, 1)), NEG)
    masks = np.stack([np.concatenate([m[:P, :P], m[P:, :]], axis=1) for m in (causal, dilated)]).astype(np.float32)
    return onehot, masks


def kernel(**inputs):
    import concourse.bacc as bacc
    from concourse.bass_utils import run_bass_kernel_spmd

    a = {k: np.asarray(v) for k, v in inputs.items()}
    onehot, masks = shape_constants()
    stream = np.empty((SLABS, P, DINNER), np.float32)
    n = 0
    for slab in stream_slabs(a):
        stream[n] = slab
        n += 1
    assert n == SLABS
    mods = np.empty((8 * MOD_GROUPS, P, DINNER), np.float32)
    for n, slab in enumerate(mod_slabs(a)):
        mods[n] = slab
    arrays = {
        "stream": stream, "mods": mods,
        "x_t": np.ascontiguousarray(a["x"][0].T),
        "cols": columns(a),
        "onehot": onehot,
        "rb_t": np.ascontiguousarray(a["rel_bias"].T),
        "masks": masks,
        "pos": np.ascontiguousarray(np.broadcast_to(a["positions_2"], (P, S))),
        "p_t": np.ascontiguousarray(a["p_2"][:, 0].transpose(0, 2, 1)),
    }
    nc = bacc.Bacc("TRN2", target_bir_lowering=False, num_devices=1)
    args = {k: nc.dram_tensor("in_" + k, v.shape, mybir.dt.from_np(v.dtype), kind="ExternalInput").ap() for k, v in arrays.items()}
    out_t = nc.dram_tensor("out_t", (D, S), F32, kind="ExternalOutput").ap()
    build(nc, args["stream"], args["mods"], args["x_t"], args["cols"], args["onehot"], args["rb_t"], args["masks"], args["pos"],
          args["p_t"], out_t)
    r = run_bass_kernel_spmd(nc, [{"in_" + k: v for k, v in arrays.items()}], core_ids=[0])
    return np.ascontiguousarray(r.results[0]["out_t"].T)[None]
```

```python
import math
from contextlib import ExitStack

import numpy as np

import concourse.bass as bass
from concourse import mybir

F32 = mybir.dt.float32
F32R = mybir.dt.float32r
I32 = mybir.dt.int32
ALU = mybir.AluOpType
ACT = mybir.ActivationFunctionType

P = 128
S = 256
D = 1024
CH = D // P
DFF = 2816
FJ = DFF // 256
LRU = 1280
LCH = LRU // P
LHEADS = 5
HEADS = 8
KVH = 4
LAYERS2 = 2
DINNER = 2048
EPS = 1e-6
NEG = -1e30
MAGIC = 12582912.0
TWO_PI = 2.0 * math.pi
C1 = 6.28125
C2 = float(np.float32(np.round((TWO_PI - C1) * 2**21) / 2**21))
C3 = TWO_PI - C1 - C2
PI_SAFE = 3.1415925

B_WIN = 0
B_GATE = B_WIN + 10
B_LOUT = B_GATE + 3
B_FFN0 = B_LOUT + 5
B_KV = B_FFN0 + 3 * FJ
B_Q = B_KV + 4
B_O = B_Q + 4
B_FFN1 = B_O + 4
B_L2 = B_FFN1 + 3 * FJ
M_MIX = 3 * FJ
M_OUT = M_MIX + 10
M_FFN = M_OUT + 4
M_PLE = M_FFN + 3 * FJ
M_PGATE = M_PLE + 1
PER_L2 = M_PGATE + 4
SLABS = B_L2 + LAYERS2 * PER_L2
RING = 3

MOD_GROUPS = 7
MOD_RING = 2
G_MIX0, G_A0, G_B0, G_KV, G_MIX1, G_A1, G_B1 = range(MOD_GROUPS)

N_MIX0, N_FFN0, N_KV, N_FFN1, N_FIN = range(5)
L_PRE1, L_POST1, L_PREMIX, L_QLAT, L_KVLAT, L_GDIL, L_GMLA, L_POSTMIX, L_PRE2, L_POST2, L_PREPLE, L_POSTPLE = range(12)
NORM_CHUNKS = [CH] * 5 + [8, 8, 8, 2, 1, 4, 4, 8, 8, 8, 8, 8] * LAYERS2
A_MIX0, A_FFN0, A_KV, A_MIX1, A_FFN1 = range(5)
LA_PRE1, LA_PREMIX, LA_QLAT, LA_KVLAT, LA_GDIL, LA_GMLA, LA_PRE2, LA_PREPLE = range(8)
APPLY_CHUNKS = [CH] * 5 + [8, 8, 2, 1, 4, 4, 8, 8] * LAYERS2


DEFERRED = (LA_PRE1, LA_PREMIX, LA_PRE2, LA_PREPLE)
TURNED_CHUNKS = [CH] * 5 + [0 if k in DEFERRED else APPLY_CHUNKS[5 + k] for k in range(8)] * LAYERS2
SUM_ALL = (L_PRE1, L_PREMIX, L_PRE2, L_PREPLE)
SUM_SIX = (L_POST1, L_POSTMIX, L_POST2, L_POSTPLE)


def before(counts, n):
    return sum(counts[:n])


def summed(n):
    if n < 5:
        return 6 if n in (N_FFN1, N_FIN) else 0
    k = (n - 5) % 12
    return CH if k in SUM_ALL else 6 if k in SUM_SIX else 0


SUMMED = [n for n in range(len(NORM_CHUNKS)) if summed(n)]


def stat_bank(n):
    if n < 5:
        return {N_MIX0: 6, N_FFN1: 2}.get(n, 0)
    return {L_PRE1: 4, L_PREMIX: 4, L_QLAT: 6, L_KVLAT: 7, L_GDIL: 6, L_PRE2: 4, L_PREPLE: 3}.get((n - 5) % 12, 0)


def norm2(l, k):
    return 5 + 12 * l + k


def apply2(l, k):
    return 5 + 8 * l + k


def norm_at(n):
    return {L_KVLAT: 2, L_GDIL: 4}.get((n - 5) % 12, 0) if n >= 5 else 0


def base2(l, k=0):
    return B_L2 + l * PER_L2 + k


COLS = [("c", CH), ("norm_mix", 2 * CH), ("norm_ffn", 2 * CH), ("kv_norm", CH), ("final_norm", CH),
        ("gains2", LAYERS2 * 8 * CH), ("q_norm2", LAYERS2 * 2), ("kv_norm2", LAYERS2), ("group2", LAYERS2 * CH),
        ("conv_w", 4 * LCH), ("conv_b", LCH), ("b_gates", 2 * LCH), ("lambda", LCH), ("mod_b", MOD_GROUPS * 16),
        ("inv_mla", 1), ("inv_dil", 1), ("sign_mla", 1), ("sign_dil", 1)]
COL_AT = {}
_n = 0
for _name, _k in COLS:
    COL_AT[_name] = _n
    _n += _k
NCOLS = _n


def build(nc, stream, mods, x_t, cols_d, onehot, rb_t, masks, pos, p_t, out_t):
    scratch = nc.dram_tensor("bias_rows", (HEADS, P, 512), F32, kind="Internal").ap()
    with ExitStack() as ctx:
        def sb(name, shape, dt=F32):
            return ctx.enter_context(nc.sbuf_tensor(name, shape, dt))

        def sem(name):
            return ctx.enter_context(nc.semaphore(name))

        bank = [ctx.enter_context(nc.psum_tensor(f"bank{i}", [P, 512], F32)) for i in range(8)]

        raw = sb("raw", [P, RING, DINNER])
        w_hi = sb("w_hi", [P, RING, DINNER], F32R)
        w_lo = sb("w_lo", [P, RING, DINNER], F32R)
        x = sb("x", [P, CH, S])
        a_hi = sb("a_hi", [P, LCH, S], F32R)
        a_lo = sb("a_lo", [P, LCH, S], F32R)
        hid_hi = sb("hid_hi", [P, 2, 2, S], F32R)
        hid_lo = sb("hid_lo", [P, 2, 2, S], F32R)
        sq = sb("sq", [P, CH, S])
        rs0 = sb("rs0", [P, S])
        nwt = sb("nwt", [P, S])
        rstd = sb("rstd", [P, 2, S])
        ones = sb("ones", [P, P])
        ident = sb("ident", [P, P])
        cols = sb("cols", [P, NCOLS])
        modc = sb("modc", [P, MOD_GROUPS * 16])
        cs = sb("cs", [P, CH])
        scale1 = sb("scale1", [P, 5 * CH])
        half_g = sb("half_g", [P, LAYERS2 * 2 * CH])
        lam = sb("lam", [P, 8, LCH])
        shared = sb("shared", [P, 4 * 2048])
        mod_raw = shared[:, 0:4096].rearrange("p (r n) -> p r n", r=2)
        mod_acc = shared[:, 4096:8192].rearrange("p (r n) -> p r n", r=2)
        f = shared[:, 0:2048].rearrange("p (c s) -> p c s", c=CH)
        rope = shared[:, 2048:3072].rearrange("p (k s) -> p k s", k=4)
        mask = shared[:, 3072:3840].rearrange("p (k s) -> p k s", k=2)
        ptok = shared[:, 3840:4864].rearrange("p (l c s) -> p l c s", l=2, c=2)
        kr_m = shared[:, 4864:5888].rearrange("p (h s) -> p h s", h=4)
        q_dil = shared[:, 6144:8192].rearrange("p (h s) -> p h s", h=HEADS)
        work = sb("work", [P, 10752])

        def area(at, *shape):
            n = int(np.prod(shape))
            v = work[:, at:at + n]
            if len(shape) == 2:
                v = v.rearrange("p (a b) -> p a b", a=shape[0])
            elif len(shape) == 3:
                v = v.rearrange("p (a b c) -> p a b c", a=shape[0], b=shape[1])
            return v

        y_br = area(0, LCH, S)
        xc = area(2560, LCH, S)
        r_g = area(5120, LCH, S)
        i_g = area(7680, LCH, S)
        mod_more = area(0, 2, 2048)
        mod_third = area(6400, 2048)
        rbb = area(5120, HEADS, P)
        bias_rows = area(6144, HEADS, 512)
        onehot_sb = area(10240, 512)
        gate_s = area(0, 2, 512)
        hid = area(1024, 2, 512)
        q_a = area(0, CH, S)
        k_a = area(2048, KVH, S)
        v_a = area(3072, 2, 512)
        bias = area(7168, HEADS, 384)
        k_dil = area(0, 4, S)
        k_nope = area(1024, 4, S)
        v_dil = area(2048, 2, 512)
        v_mla = area(3072, 2, 512)
        q_lat = area(6400, 2, S)
        kv_lat = area(6912, 1, S)
        kr = area(7168, S)
        q_nope = area(7424, HEADS, S)
        q_rope = area(9472, 2, S)
        swap = area(9984, 512)
        sc = area(4096, 2, 384)
        prob = area(4864, 2, 384)
        prob_t = area(5632, 2, 384)
        rt = area(4096, 4, S)
        pos_i = area(4096, S).bitcast(I32)
        pos_f = area(4352, S)
        ang = area(4608, S)
        turn = area(4864, 2, S)
        red = area(5376, 2, S)
        nmax = sb("nmax", [P, 2, 2])
        ssum = sb("ssum", [P, 2, 2])
        rsum = sb("rsum", [P, 2, 2])
        xp_all = sb("xp", [P, 4 * (S + 3)])
        xp = xp_all[:, :].rearrange("p (b c s) -> p b c s", b=2, c=2)
        rope_r = xp_all[:, 0:4 * S].rearrange("p (k s) -> p k s", k=4)
        rcol = sb("rcol", [P, 2])
        eps = sb("eps", [P, 1])
        warm = sb("warm", [P, 1])
        rb_sb = sb("rb_sb", [32, HEADS])

        def col(name, k):
            return cols[:, COL_AT[name] + k:COL_AT[name] + k + 1]

        def modcol(g, k):
            return modc[:, 16 * g + k:16 * g + k + 1]

        s_cols, s_x, s_rb, s_oh = sem("cols_landed"), sem("x_landed"), sem("rb_landed"), sem("onehot_landed")
        landed = [sem(f"slab_landed{r}") for r in range(RING)]
        mod_landed = [sem(f"mod_landed{r}") for r in range(2 * MOD_RING)]
        s_late = sem("late_landed")
        s_rows = sem("bias_rows_stored")
        s_bias = sem("bias_landed")
        s_out = sem("out_stored")
        hi_ready, lo_ready, slab_done = sem("hi_ready"), sem("lo_ready"), sem("slab_done")
        bank_done = sem("bank_done")
        sq_ready, stat_ready, rs0_ready = sem("sq_ready"), sem("stat_ready"), sem("rs0_ready")
        sum_step, sum_ready = sem("sum_step"), sem("squares_summed")
        newton, rstd_ready = sem("newton"), sem("rstd_ready")
        nt_ready, nh_ready, nl_ready = sem("normed_ready"), sem("normed_hi_ready"), sem("normed_lo_ready")
        x_ready, f_ready, f_scaled = sem("x_ready"), sem("f_ready"), sem("f_scaled")
        silu_done, hid_done, hh_ready, hl_ready = sem("silu_done"), sem("hid_done"), sem("hid_hi_ready"), sem("hid_lo_ready")
        const_ready = sem("const_ready")
        ident0 = sem("ident_zeroed")
        rbb_ready = sem("rbb_ready")
        row_mm, row_ev = sem("bias_row_made"), sem("bias_row_copied")
        cs_ready = sem("cs_ready")
        mod_step, mod_red, modc_ready = sem("mod_step"), sem("mod_reduced"), sem("modc_ready")
        acc_zero = sem("acc_zero")

        mod_slots = [mod_raw[:, 0, :], mod_raw[:, 1, :], mod_more[:, 0, :], mod_more[:, 1, :]]

        def mod_slot(s):
            return (s % 4, s // 4 + 1) if s < 8 else (s % 2, s // 2 - 1)

        def mod_sums(g):
            return mod_third if g == G_A1 else mod_acc[:, g % 2, :]


        scale_ready = sem("scale_ready")
        half_ready = sem("half_ready")
        lam_act, lam_dve = sem("lambda_act"), sem("lambda_dve")
        pad_zero = sem("pad_zero")
        xbr_ready, conv_step, conv_done, y_ready = sem("xbr_copied"), sem("conv_step"), sem("conv_done"), sem("gelu_ready")
        xch_ready, xcl_ready = sem("conv_hi_ready"), sem("conv_lo_ready")
        gate_done, gates_ready = sem("gates_made"), sem("gates_ready")
        bi_ready, decay_ready = sem("gated_input_ready"), sem("decay_ready")
        mult2_step, mult2_ready, mult_ready = sem("mult2_step"), sem("mult2_ready"), sem("mult_ready")
        scan_step, z_ready, zh_ready, zl_ready = sem("scan_step"), sem("z_ready"), sem("z_hi_ready"), sem("z_lo_ready")
        qkv_act, qkv_dve, rope_step = sem("qkv_copied_act"), sem("qkv_copied_dve"), sem("rope_step")
        qk_done, sc_done, exp_done, rs_done, pn_done = sem("qk_done"), sem("scores_done"), sem("exp_done"), sem("rsum_done"), sem("probs_done")
        tr_done, pt_done, pv_done, o_done, oh_done = sem("probs_turned"), sem("probs_t_done"), sem("pv_done"), sem("o_done"), sem("o_hi_done")
        rows_zero, swap_ready = sem("rows_zeroed"), sem("halves_exchanged")
        up_done = sem("latent_up_done")
        trig_step, trig_act, rope_ready = sem("trig_step"), sem("trig_act"), sem("rope_ready")
        ph_ready, pl_ready = sem("p_hi_ready"), sem("p_lo_ready")
        pg_scaled, pg_ready = sem("ple_gate_scaled"), sem("ple_gate_ready")
        gate_scaled, up_scaled = sem("gate_scaled"), sem("up_scaled")
        table_ready, rturn_done, rcol_ready = sem("rope_over_rms_ready"), sem("rms_turned"), sem("rms_column_ready")
        eps_ready, warmed = sem("eps_ready"), sem("table_warmed")

        block = ctx.enter_context(nc.Block())

        U_LRU, U_FFN0, U_MOBA, U_FFN1, U_FIN = range(5)

        def u2(l, k):
            return 5 + 4 * l + k

        U_LAST = u2(LAYERS2 - 1, 3)

        @block.sync
        def _(sp):
            sp.dma_start(cols[:, :], cols_d).then_inc(s_cols, 16)
            sp.dma_start(x[:, :, :], x_t.rearrange("(c p) s -> p c s", p=P)).then_inc(s_x, 16)
            for s in range(RING):
                sp.dma_start(raw[:, s, :], stream[s]).then_inc(landed[s], 16)
            with sp.Fori(1, SLABS // RING) as i:
                for r in range(RING):
                    src = stream[bass.ds(i * RING + r, 1)].rearrange("a p n -> p (a n)")
                    split = sp.snap(i * RING + (r - RING + 1))
                    sp.wait_ge(lo_ready, split)
                    sp.dma_start(raw[:, r, :], src).then_inc(landed[r], 16)
            for s in range(SLABS // RING * RING, SLABS):
                sp.wait_ge(lo_ready, s - RING + 1)
                sp.dma_start(raw[:, s % RING, :], stream[s]).then_inc(landed[s % RING], 16)
            for c in range(CH):
                sp.wait_ge(x_ready, CH * U_LAST + c + 1)
                sp.dma_start(out_t[c * P:(c + 1) * P, :], x[:, c, :]).then_inc(s_out, 16)
            sp.wait_ge(s_out, 16 * CH)

        @block.gpsimd
        def _(pool):
            pool.dma_start(rb_sb[:, :], rb_t).then_inc(s_rb, 16)
            pool.dma_start(onehot_sb[0:33, :], onehot).then_inc(s_oh, 16)
            for s in range(4):
                pool.dma_start(mod_slots[s], mods[s]).then_inc(mod_landed[s], 16)
            nc.gpsimd.memset(eps[:, :], EPS).then_inc(eps_ready, 1)
            nc.gpsimd.memset(ident[:, :], 0.0).then_inc(ident0, 1)
            pool.wait_ge(ident0, 1)
            nc.gpsimd.affine_select(out=ident[:, :], in_=ident[:, :], compare_op=ALU.not_equal, fill=1.0, base=0,
                                    pattern=[[-1, P]], channel_multiplier=1)
            nc.gpsimd.memset(ones[:, :], 1.0).then_inc(const_ready, 1)
            for s in range(4, 10):
                r = s % 4 if s < 8 else s % 2
                pool.wait_ge(mod_step, s - 3)
                pool.dma_start(mod_slots[r], mods[s]).then_inc(mod_landed[r], 16)
            with pool.Fori(0, (8 * MOD_GROUPS - 10) // 2) as i:
                for r in range(2):
                    src = mods[bass.ds(i * 2 + (10 + r), 1)].rearrange("a p n -> p (a n)")
                    used = pool.snap(i * 2 + (9 + r))
                    pool.wait_ge(mod_step, used)
                    pool.dma_start(mod_slots[r], src).then_inc(mod_landed[r], 16)
            pool.wait_ge(mod_red, MOD_GROUPS)
            pool.dma_start(mask, masks.rearrange("k p s -> p k s")).then_inc(s_late, 16)
            pool.dma_start(ptok, p_t.rearrange("l (c p) s -> p l c s", p=P)).then_inc(s_late, 16)
            pool.wait_ge(o_done, HEADS)
            pool.dma_start(pos_i, pos).then_inc(s_late, 16)
            for zeroed in (kr_m, q_dil, q_nope):
                nc.gpsimd.memset(zeroed, 0.0).then_inc(rows_zero, 1)
            added = 0
            for i, n in enumerate(SUMMED):
                for c in range(2, summed(n), 2):
                    if c > 2:
                        pool.wait_ge(sum_step, added)
                    pool.wait_ge(sq_ready, before(NORM_CHUNKS, n) + c + 2)
                    ins = nc.gpsimd.tensor_tensor(out=sq[:, 0:2, :], in0=sq[:, 0:2, :], in1=sq[:, c:c + 2, :], op=ALU.add)
                    if c + 2 < summed(n):
                        ins.then_inc(sum_step, 1)
                        added += 1
                ins.then_inc(sum_ready, 1)

        @block.tensor
        def _(pe):
            def product(out, w_h, w_l, v_h, v_l, start, stop):
                pe.matmul(out, w_h, v_h, start=start, stop=False, skip_group_check=True)
                pe.matmul(out, w_h, v_l, start=False, stop=False, skip_group_check=True)
                return pe.matmul(out, w_l, v_h, start=False, stop=stop, skip_group_check=True)

            def weights(s, lo, n):
                return w_hi[:, s % RING, lo:lo + n], w_lo[:, s % RING, lo:lo + n]

            def need_slab(s):
                pe.wait_ge(lo_ready, s + 1)

            def feature_slab(slot, out, chunk_ready=None, m_chunks=2, width=256):
                for c in range(CH):
                    if chunk_ready is not None:
                        pe.wait_ge(nl_ready, chunk_ready + c + 1)
                    for m in range(m_chunks):
                        mm = product(out[:, m * S:(m + 1) * S], *weights(slot, c * width + m * P, P), a_hi[:, c, :], a_lo[:, c, :],
                                     start=(c == 0 and m == 0), stop=(c == CH - 1))
                return mm

            def token_slab(slot, out, chunks=CH):
                for c in range(chunks):
                    for t in range(2):
                        wh, wl = weights(slot, c * 256, 256)
                        o = out[:, t * 256:(t + 1) * 256]
                        lh, ll = a_hi[:, c, t * P:(t + 1) * P], a_lo[:, c, t * P:(t + 1) * P]
                        pe.matmul(o, lh, wh, start=(c == 0 and t == 0), stop=False, skip_group_check=True)
                        pe.matmul(o, ll, wh, start=False, stop=False, skip_group_check=True)
                        mm = pe.matmul(o, lh, wl, start=False, stop=(c == chunks - 1), skip_group_check=True)
                return mm

            def sums_slab(slot, v_h, v_l, first, last):
                def one(k, m):
                    return product(bank[4 + m // 2][:, (m % 2) * S:(m % 2 + 1) * S], *weights(slot, k * D + m * P, P),
                                   v_h[:, k, :], v_l[:, k, :], start=(first and k == 0 and m % 2 == 0), stop=(last and k == 1))
                if not last:
                    for k in range(2):
                        for m in range(CH):
                            mm = one(k, m)
                    return mm
                for m in range(CH):
                    for k in range(2):
                        mm = one(k, m)
                    if m in (1, 3, 5):
                        mm.then_inc(bank_done, 1)
                return mm

            def norm_stat(n):
                at, total = norm_at(n), NORM_CHUNKS[n]
                done = before(NORM_CHUNKS, n)
                chunks = list(range(total))
                if summed(n):
                    pe.wait_ge(sum_ready, SUMMED.index(n) + 1)
                    chunks = [0, 1] + chunks[summed(n):]
                for c in chunks:
                    if not summed(n) or c > 1:
                        pe.wait_ge(sq_ready, done + c + 1)
                    mm = pe.matmul(bank[stat_bank(n)][:, 0:S], ones[:, :], sq[:, at + c, :], start=(c == 0), stop=(c == chunks[-1]))
                mm.then_inc(stat_ready, 1)

            def keep_warm(n):
                for _ in range(n):
                    pe.matmul(bank[1][:, 0:P], ones[:, :], ident[:, :], start=True, stop=True)

            def norm_between(n, first=WARM_BEFORE, then=WARM_AFTER):
                keep_warm(first)
                norm_stat(n)
                keep_warm(then)

            def slab_pair(slots, outs, chunk_ready):
                for c in range(CH):
                    pe.wait_ge(nl_ready, chunk_ready + c + 1)
                    for slot, out in zip(slots, outs):
                        for m in range(2):
                            mm = product(out[:, m * S:(m + 1) * S], *weights(slot, c * 256 + m * P, P), a_hi[:, c, :], a_lo[:, c, :],
                                         start=(c == 0 and m == 0), stop=(c == CH - 1))
                        if c == CH - 1:
                            mm.then_inc(slab_done, 1)

            def mod_reduce(g, b):
                pe.wait_ge(mod_step, MOD_LAST[g])
                for m in range(16):
                    mm = pe.matmul(bank[b][:, m:m + 1], mod_sums(g)[:, m * P:(m + 1) * P], ones[:, 0:1],
                                   start=True, stop=True)
                mm.then_inc(mod_red, 1)

            def ffn(i, b, ap, stat=None):
                f0 = FJ * i

                def group(j, ready, slot, chunk_ready=None, j_par=None):
                    par = j_par
                    for k, out in enumerate((bank[par], bank[2 + par])):
                        pe.wait_ge(lo_ready, ready + k)
                        if j is not None:
                            pe.wait_ge(hid_done, j + (f0 - 1))
                        feature_slab(slot + k, out, chunk_ready if k == 0 else None).then_inc(slab_done, 1)

                def down(j, ready, slot, par, first=False, last=False):
                    pe.wait_ge(lo_ready, ready)
                    pe.wait_ge(hl_ready, j + (f0 + 1))
                    sums_slab(slot, hid_hi[:, par], hid_lo[:, par], first, last).then_inc(slab_done, 1)

                pe.wait_ge(lo_ready, b + 2)
                slab_pair((b, b + 1), (bank[0], bank[2]), before(APPLY_CHUNKS, ap))
                if stat is not None:
                    norm_stat(stat)
                group(None, b + 3, b + 2, None, 1)
                down(0, b + 5, b + 4, 0, first=True)
                with pe.Fori(0, (FJ - 3) // 2) as k:
                    for h in range(2):
                        group(2 * k + (2 + h), 6 * k + (b + 6 + 3 * h), b + 5 + 3 * h, None, h)
                        down(2 * k + (1 + h), 6 * k + (b + 8 + 3 * h), b + 7 + 3 * h, (1 + h) % 2)
                j = FJ - 1
                group(j, b + 3 * j, b + 3 * j - 1, None, j % 2)
                down(j - 1, b + 3 * j + 2, b + 3 * j + 1, (j - 1) % 2)
                down(j, b + 3 * j + 3, b + 3 * j + 2, j % 2, last=True)

            def attention(heads, qk, pv, between=None):
                n = len(heads)

                def score(k):
                    if k >= 2:
                        pe.wait_ge(sc_done, heads[k] - 1)
                    for t in range(2):
                        out = bank[k % 2][:, 0:P] if t == 0 else bank[k % 2][:, P:384]
                        parts = qk(k, t)
                        for i, (lhs, rhs) in enumerate(parts):
                            mm = pe.matmul(out, lhs, rhs, start=(t == 0 and i == 0), stop=(i == len(parts) - 1), skip_group_check=True)
                    mm.then_inc(qk_done, 1)

                def turn(k):
                    pe.wait_ge(pn_done, heads[k] + 1)
                    if k >= 2:
                        pe.wait_ge(pt_done, heads[k] - 1)
                    pr = prob[:, heads[k] % 2]
                    for t in range(3):
                        mm = pe.transpose(bank[2 + k % 2][:, t * P:(t + 1) * P], pr[:, t * P:(t + 1) * P], ident[:, :])
                    mm.then_inc(tr_done, 1)

                def weigh(k):
                    pe.wait_ge(pt_done, heads[k] + 1)
                    lhs, out, gate = pv(k)
                    if gate is not None:
                        pe.wait_ge(o_done, gate)
                    pt = prob_t[:, heads[k] % 2]
                    pe.matmul(out[:, 0:256], lhs(0), pt[:, 0:256], start=True, stop=False, skip_group_check=True)
                    pe.matmul(out[:, 128:256], lhs(1), pt[:, 256:384], start=False, stop=True, skip_group_check=True).then_inc(pv_done, 1)

                for k in range(-3, n + 1):
                    if 0 <= k < n:
                        turn(k)
                    if k >= 1:
                        weigh(k - 1)
                    if k + 3 < n:
                        score(k + 3)
                    if between is not None and k == NORM_STEP:
                        between()

            pe.wait_ge(const_ready, 1)
            pe.wait_ge(rbb_ready, 2)
            pe.wait_ge(s_oh, 16)
            for h in range(HEADS):
                if h >= 2:
                    pe.wait_ge(row_ev, h - 1)
                pe.matmul(bank[h % 2][:, :], rbb[0:33, h, :], onehot_sb[0:33, :], start=True, stop=True).then_inc(row_mm, 1)
            norm_stat(N_MIX0)
            mod_reduce(G_MIX0, 7)

            pe.wait_ge(row_ev, HEADS)
            need_slab(B_WIN + 1)
            slab_pair((B_WIN, B_WIN + 1), (bank[0], bank[1]), before(APPLY_CHUNKS, A_MIX0))
            for i in range(2, 10):
                s = B_WIN + i
                need_slab(s)
                if 4 <= i < 9:
                    pe.wait_ge(xbr_ready, i - 3)
                if i == 9:
                    pe.wait_ge(y_ready, 1)
                feature_slab(s, bank[i % 4]).then_inc(slab_done, 1)
            for hd in range(LHEADS):
                s = B_GATE + hd // 2
                if hd % 2 == 0:
                    need_slab(s)
                pe.wait_ge(xcl_ready, hd + 1)
                for k in range(2):
                    b = (2 * hd + k) % 4
                    if hd >= 2:
                        pe.wait_ge(gates_ready, 2 * (hd - 2) + k + 1)
                    for c in range(2):
                        for m in range(2):
                            mm = product(bank[b][:, m * S:(m + 1) * S], *weights(s, (hd % 2) * 1024 + c * 512 + k * 256 + m * P, P),
                                         a_hi[:, 2 * hd + c, :], a_lo[:, 2 * hd + c, :], start=(c == 0 and m == 0), stop=(c == 1))
                    mm.then_inc(slab_done if k == 1 and hd in GATE_ENDS else gate_done, 1)
            pe.wait_ge(gates_ready, 2 * LHEADS)
            mod_reduce(G_A0, 2)
            for i in range(LHEADS):
                need_slab(B_LOUT + i)
                pe.wait_ge(zl_ready, i + 1)
                sums_slab(B_LOUT + i, a_hi[:, 2 * i:2 * i + 2], a_lo[:, 2 * i:2 * i + 2], i == 0, i == LHEADS - 1).then_inc(slab_done, 1)
            mod_reduce(G_B0, 3)
            norm_between(N_FFN0)
            ffn(0, B_FFN0, A_FFN0)

            mod_reduce(G_KV, 2)
            norm_stat(N_KV)
            mod_reduce(G_MIX1, 3)
            keep_warm(4)
            need_slab(B_KV + 1)
            slab_pair((B_KV, B_KV + 1), (bank[0], bank[1]), before(APPLY_CHUNKS, A_KV))
            for i in range(2, 4):
                need_slab(B_KV + i)
                pe.wait_ge(modc_ready, i + 2)
                token_slab(B_KV + i, bank[i]).then_inc(slab_done, 1)
            mod_reduce(G_A1, 4)
            for i in range(4):
                need_slab(B_Q + i)
                pe.wait_ge(qkv_act, i + 1)
                feature_slab(B_Q + i, bank[i], before(APPLY_CHUNKS, A_MIX1) if i == 0 else None).then_inc(slab_done, 1)
            pe.wait_ge(qkv_act, 8)
            pe.wait_ge(modc_ready, G_A1 + 1)
            attention(list(range(HEADS)),
                      lambda k, t: [(q_a[:, k, t * P:(t + 1) * P], k_a[:, k // 2, 0:P * (t + 1)])],
                      lambda k: (lambda kt: v_a[:, kt, (k // 2) * P:(k // 2 + 1) * P], bank[4 + k % 2][:, 0:256], k - 1 if k >= 2 else None))
            for i in range(4):
                need_slab(B_O + i)
                pe.wait_ge(o_done, 2 * i + 2 if i else HEADS)
                sums_slab(B_O + i, a_hi[:, 2 * i:2 * i + 2], a_lo[:, 2 * i:2 * i + 2], i == 0, i == 3).then_inc(slab_done, 1)
                if i == 2:
                    mod_reduce(G_B1, 0)
            norm_between(N_FFN1)
            ffn(1, B_FFN1, A_FFN1)
            norm_between(N_FIN)

            for l in range(LAYERS2):
                ffn(2 + 2 * l, base2(l), apply2(l, LA_PRE1), norm2(l, L_PRE1))
                norm_between(norm2(l, L_POST1))
                b = base2(l, M_MIX)
                d0, c0 = 8 * l, 8 + 8 * l
                need_slab(b + 1)
                slab_pair((b, b + 1), (bank[0], bank[1]), before(APPLY_CHUNKS, apply2(l, LA_PREMIX)))
                norm_stat(norm2(l, L_PREMIX))
                for i in range(2, 8):
                    need_slab(b + i)
                    if i in (4, 5, 6, 7):
                        pe.wait_ge(qkv_dve, d0 + i - 3)
                    if i < 6:
                        mm = feature_slab(b + i, bank[i % 4])
                    else:
                        mm = token_slab(b + i, bank[i % 4])
                    mm.then_inc(slab_done, 1)
                    if i == 3:
                        pe.wait_ge(rstd_ready, norm2(l, L_PREMIX) + 1)
                        for t in range(2):
                            mm = pe.transpose(bank[5][:, t * P:(t + 1) * P], rstd[:, norm2(l, L_PREMIX) % 2, t * P:(t + 1) * P], ident[:, :])
                        mm.then_inc(rturn_done, 1)
                    if i == 5:
                        norm_stat(norm2(l, L_QLAT))
                    if i == 6:
                        norm_stat(norm2(l, L_KVLAT))
                sC, sQ = b + 8, b + 9
                need_slab(sC)
                pe.wait_ge(qkv_dve, d0 + 5)
                feature_slab(sC, bank[0], None, 1, P).then_inc(up_done, 1)
                at = before(APPLY_CHUNKS, apply2(l, LA_KVLAT))
                pe.wait_ge(nl_ready, at + 1)
                pe.wait_ge(qkv_dve, d0 + 6)
                lat_h, lat_l = hid_hi[:, 0, 0, :], hid_lo[:, 0, 0, :]
                for k in range(2):
                    if k == 1:
                        pe.wait_ge(qkv_act, c0 + 1)
                    for m in range(2):
                        mm = product(bank[1 + k][:, m * S:(m + 1) * S], *weights(sC, 1024 + (2 * k + m) * P, P), lat_h, lat_l,
                                     start=(m == 0), stop=True)
                    mm.then_inc(up_done, 1)
                for t in range(2):
                    wh, wl = weights(sC, 1024 + 512, 512)
                    tk = slice(t * P, (t + 1) * P)
                    mm = product(bank[4 + t][:, :], lat_h[:, tk], lat_l[:, tk], wh, wl, start=True, stop=True)
                    if t == 0:
                        mm.then_inc(up_done, 1)
                mm.then_inc(slab_done, 1)
                need_slab(sQ)
                at = before(APPLY_CHUNKS, apply2(l, LA_QLAT))
                pe.wait_ge(nl_ready, at + 2)
                pe.wait_ge(qkv_act, c0 + 2)
                for k, out in enumerate((bank[3], bank[6], bank[7], bank[0])):
                    if k == 3:
                        pe.wait_ge(qkv_dve, d0 + 7)
                    for c in range(2):
                        for m in range(2):
                            mm = product(out[:, m * S:(m + 1) * S], *weights(sQ, c * 1024 + (2 * k + m) * P, P),
                                         a_hi[:, 8 + c, :], a_lo[:, 8 + c, :], start=(c == 0 and m == 0), stop=(c == 1))
                    if k < 2:
                        mm.then_inc(up_done, 1)
                mm.then_inc(slab_done, 1)
                pe.wait_ge(qkv_act, c0 + 8)
                pe.wait_ge(qkv_dve, d0 + 8)

                def qk(k, t):
                    tk, keys = slice(t * P, (t + 1) * P), slice(0, P * (t + 1))
                    h = k % HEADS
                    if k < HEADS:
                        return [(q_dil[:, h, tk], k_dil[:, h // 2, keys])]
                    return [(q_nope[:, h, tk], k_nope[:, h // 2, keys]), (q_rope[:, h // 4, tk], kr_m[:, rope_slot(h), keys])]

                def pv(k):
                    h = k % HEADS
                    v = v_dil if k < HEADS else v_mla
                    r = slice(64 * (h % 2), 64 * (h % 2) + 64)
                    gate = 8 + 8 * l + k // 2 - 1 if k >= 4 and k % 2 == 0 else None
                    return lambda kt: v[:, kt, h * 64:(h + 1) * 64], bank[4 + (k // 2) % 2][r, 0:256], gate

                attention([HEADS + 16 * l + k for k in range(16)], qk, pv, lambda: norm_stat(norm2(l, L_GDIL)))
                pe.wait_ge(o_done, 8 + 8 * l + 8)
                for i, g in enumerate(OUT_ORDER):
                    need_slab(base2(l, M_OUT) + i)
                    pe.wait_ge(nl_ready, before(APPLY_CHUNKS, apply2(l, LA_GDIL)) + 2 * i + 2)
                    sums_slab(base2(l, M_OUT) + i, a_hi[:, 2 * g:2 * g + 2], a_lo[:, 2 * g:2 * g + 2], i == 0, i == 3).then_inc(slab_done, 1)
                    if i == 0:
                        norm_stat(norm2(l, L_GMLA))
                norm_between(norm2(l, L_POSTMIX))
                ffn(3 + 2 * l, base2(l, M_FFN), apply2(l, LA_PRE2), norm2(l, L_PRE2))
                norm_between(norm2(l, L_POST2), WARM_BEFORE, 0)
                need_slab(base2(l, M_PLE))
                pe.wait_ge(pl_ready, l + 1)
                pe.wait_ge(f_ready, 4 * (4 * l + 2) + 4)
                for m in range(CH):
                    for k in range(2):
                        mm = product(bank[4 + m // 2][:, (m % 2) * S:(m % 2 + 1) * S], *weights(base2(l, M_PLE), k * D + m * P, P),
                                     hid_hi[:, 1, k, :], hid_lo[:, 1, k, :], start=(k == 0 and m % 2 == 0), stop=(k == 1))
                mm.then_inc(slab_done, 1)
                need_slab(base2(l, M_PGATE) + 1)
                slab_pair((base2(l, M_PGATE), base2(l, M_PGATE) + 1), (bank[0], bank[1]), before(APPLY_CHUNKS, apply2(l, LA_PREPLE)))
                norm_stat(norm2(l, L_PREPLE))
                for i in (2, 3):
                    need_slab(base2(l, M_PGATE) + i)
                    if i == 3:
                        pe.wait_ge(rstd_ready, norm2(l, L_PREPLE) + 1)
                    feature_slab(base2(l, M_PGATE) + i, bank[i]).then_inc(slab_done, 1)
                pe.wait_ge(pg_scaled, 4 * l + 2)
                norm_between(norm2(l, L_POSTPLE), WARM_BEFORE + 6, WARM_AFTER if l + 1 < LAYERS2 else 0)

        @block.scalar
        def _(act):
            made = [0]

            def split_to(n):
                for s in range(made[0], min(n, SLABS)):
                    act.wait_ge(landed[s % RING], 16 * (s // RING + 1))
                    if s >= RING:
                        act.wait_ge(slab_done, s - RING + 1)
                    act.copy(w_hi[:, s % RING, :], raw[:, s % RING, :]).then_inc(hi_ready, 1)
                made[0] = max(made[0], min(n, SLABS))

            def squares(n, src, ready):
                for c in range(NORM_CHUNKS[n]):
                    ready(c)
                    act.activation(sq[:, norm_at(n) + c, :], src(c), ACT.Square).then_inc(sq_ready, 1)

            def rsqrt(n, features):
                act.wait_ge(stat_ready, n + 1)
                if n:
                    act.wait_ge(rstd_ready, n)
                act.activation(rs0[:, :], bank[stat_bank(n)][:, 0:S], ACT.Abs_reciprocal_sqrt, scale=1.0 / features,
                               bias=eps[:, :]).then_inc(rs0_ready, 1)

            def warm_up():
                act.activation(warm[:, :], eps[:, :], ACT.Abs_reciprocal_sqrt)

            def deferred_hi(u, gain):
                for c in range(CH):
                    act.wait_ge(x_ready, CH * u + c + 1)
                    act.activation(a_hi[:, c, :], x[:, c, :], ACT.Copy, scale=gain(c)).then_inc(nh_ready, 1)
                    if c % 2:
                        act.activation(sq[:, c - 1:c + 1, :], x[:, c - 1:c + 1, :], ACT.Square).then_inc(sq_ready, 2)

            def gain2(l, k):
                return lambda c: col("gains2", 64 * l + CH * k + c)

            def normed_hi(ap, out, shift=None, free=None, at=0):
                if free is not None:
                    act.wait_ge(slab_done, free)
                for c in range(APPLY_CHUNKS[ap]):
                    act.wait_ge(nt_ready, before(TURNED_CHUNKS, ap) + c + 1)
                    if shift is None:
                        ins = act.copy(out(c), sq[:, at + c, :])
                    else:
                        ins = act.activation(out(c), sq[:, c, :], ACT.Identity, bias=shift(c))
                    ins.then_inc(nh_ready, 1)

            def residual(u):
                return lambda c: act.wait_ge(x_ready, CH * u + c + 1)

            def x_norm(n, u):
                warm_up()
                squares(n, lambda c: x[:, c, :], residual(u))
                rsqrt(n, D)

            def a_out(c):
                return a_hi[:, c, :]

            def ffn(i, b):
                f0 = FJ * i

                def silu(j, par, done):
                    if i >= 2:
                        act.wait_ge(gate_scaled, (j if j is not None else par) + (FJ * (i - 2) + 1))
                        act.activation(gate_s[:, par, :], gate_s[:, par, :], ACT.Silu).then_inc(silu_done, 1)
                        return
                    act.wait_ge(slab_done, done)
                    if j is not None:
                        act.wait_ge(hid_done, j + (f0 - 1))
                    act.activation(gate_s[:, par, :], bank[par][:, :], ACT.Silu).then_inc(silu_done, 1)

                def hidden_hi(j, par, done):
                    act.wait_ge(hid_done, j + (f0 + 1))
                    if done is not None:
                        act.wait_ge(slab_done, done)
                    act.copy(hid_hi[:, par].rearrange("p c s -> p (c s)"), hid[:, par, :]).then_inc(hh_ready, 1)

                def high(count, land, slot):
                    act.wait_ge(landed[slot], land)
                    act.wait_ge(slab_done, count)
                    act.copy(w_hi[:, slot, :], raw[:, slot, :]).then_inc(hi_ready, 1)

                def sine(k):
                    if i == 1:
                        act.wait_ge(trig_step, TRIG_AT[k])
                        act.activation(rope[:, k, :], red[:, k % 2, :], ACT.Sin).then_inc(trig_act, 1)

                silu(None, 0, b + 1)
                split_to(b + 5)
                hidden_hi(0, 0, None)
                sine(0)
                silu(None, 1, b + 3)
                split_to(b + 7)
                sine(1)
                hidden_hi(1, 1, None)
                split_to(b + 8)
                sine(2)
                sine(3)
                with act.Fori(0, (FJ - 3) // 2) as k:
                    for h in range(2):
                        g = b + 5 + 3 * h
                        silu(2 * k + (2 + h), h, 6 * k + (g + 1))
                        for d in (0, 1):
                            high(6 * k + (g + d + 1), 32 * k + 16 * ((g + d + 3) // RING + 1), (g + d) % RING)
                        hidden_hi(2 * k + (2 + h), h, 6 * k + (b + 5 + 3 * h))
                        high(6 * k + (g + 3), 32 * k + 16 * ((g + 5) // RING + 1), (g + 2) % RING)
                made[0] = b + 3 * (FJ - 2) + 5
                j = FJ - 1
                silu(j, j % 2, b + 3 * j)
                split_to(b + 3 * j + 4)
                hidden_hi(j, j % 2, b + 3 * j - 1)
                split_to(b + 3 * j + 5)

            act.wait_ge(s_cols, 16)
            act.activation(cs[:, :], cols[:, COL_AT["c"]:COL_AT["c"] + CH], ACT.Silu).then_inc(cs_ready, 1)
            lam_c = cols[:, COL_AT["lambda"]:COL_AT["lambda"] + LCH]
            act.activation(lam[:, 0, :], lam_c, ACT.Abs).then_inc(lam_act, 1)
            act.wait_ge(lam_act, 1)
            act.activation(lam[:, 1, :], lam[:, 0, :], ACT.Exp, scale=-1.0).then_inc(lam_act, 1)
            act.wait_ge(eps_ready, 1)
            act.wait_ge(s_x, 16)
            squares(N_MIX0, lambda c: x[:, c, :], lambda c: None)
            for h in range(HEADS):
                act.wait_ge(row_mm, h + 1)
                act.copy(bias_rows[:, h, :], bank[h % 2][:, :]).then_inc(row_ev, 1)
            act.wait_ge(row_ev, HEADS)
            act.dma_start(scratch.rearrange("h p s -> p h s"), bias_rows).then_inc(s_rows, 16)
            split_to(RING)
            rsqrt(N_MIX0, D)
            normed_hi(A_MIX0, a_out, lambda c: modcol(G_MIX0, c))

            for i in range(5):
                s = B_WIN + i
                act.wait_ge(slab_done, s + 1)
                if i == 0:
                    act.wait_ge(pad_zero, 1)
                if i >= 2:
                    act.wait_ge(conv_done, i - 1)
                sums = bank[i % 4]
                act.copy(xp[:, i % 2, :, 3:S + 3], sums[:, :].rearrange("p (c s) -> p c s", c=2))
                for m in range(2):
                    c = 2 * i + m
                    ins = act.activation(xc[:, c, :], sums[:, m * S:(m + 1) * S], ACT.Identity,
                                         scale=col("conv_w", 3 * LCH + c), bias=col("conv_b", c))
                ins.then_inc(xbr_ready, 1)
                split_to(s + 4)
            for i in range(5):
                s = B_WIN + 5 + i
                act.wait_ge(slab_done, s + 1)
                act.activation(y_br[:, 2 * i:2 * i + 2, :].rearrange("p c s -> p (c s)"), bank[(5 + i) % 4][:, :],
                               ACT.Gelu_apprx_tanh).then_inc(y_ready, 1)
                split_to(s + 4)
            act.wait_ge(slab_done, B_GATE)
            for hd in range(LHEADS):
                act.wait_ge(conv_done, hd + 1)
                act.copy(a_hi[:, 2 * hd:2 * hd + 2, :], xc[:, 2 * hd:2 * hd + 2, :]).then_inc(xch_ready, 1)
            act.wait_ge(s_rows, 16)
            for hd in range(LHEADS):
                for k, dst in enumerate((r_g, i_g)):
                    if k == 1 and hd in GATE_ENDS:
                        act.wait_ge(slab_done, B_GATE + hd // 2 + 1)
                    else:
                        act.wait_ge(gate_done, 2 * hd + k + 1 - sum(h < hd for h in GATE_ENDS))
                    for m in range(2):
                        c = 2 * hd + m
                        ins = act.activation(dst[:, c, :], bank[(2 * hd + k) % 4][:, m * S:(m + 1) * S], ACT.Sigmoid,
                                             bias=col("b_gates", k * LCH + c))
                    ins.then_inc(gates_ready, 1)
                if hd == 2:
                    split_to(B_LOUT + 1)
            split_to(B_LOUT + 2)
            act.wait_ge(lam_dve, LAM_STEPS)
            for hd in range(LHEADS):
                act.wait_ge(bi_ready, hd + 1)
                for c in (2 * hd, 2 * hd + 1):
                    act.activation(xc[:, c, :], r_g[:, c, :], ACT.Exp, scale=lam[:, 6, c:c + 1])
                    ins = act.activation(r_g[:, c, :], r_g[:, c, :], ACT.Tanh, scale=lam[:, 7, c:c + 1])
                ins.then_inc(decay_ready, 1)
            split_to(B_LOUT + 3)
            for hd in range(LHEADS):
                act.wait_ge(mult2_ready, hd + 1)
                v = r_g[:, 2 * hd:2 * hd + 2, :]
                act.activation(v, v, ACT.Sqrt).then_inc(mult_ready, 1)
            for hd in range(LHEADS):
                act.wait_ge(z_ready, hd + 1)
                act.copy(a_hi[:, 2 * hd:2 * hd + 2, :], i_g[:, 2 * hd:2 * hd + 2, :]).then_inc(zh_ready, 1)
                if hd == 2:
                    split_to(B_LOUT + 4)
            split_to(B_FFN0 + 2)
            x_norm(N_FFN0, U_LRU)
            normed_hi(A_FFN0, a_out, lambda c: modcol(G_A0, CH + c))
            split_to(B_FFN0 + 3)
            ffn(0, B_FFN0)

            split_to(B_KV + 2)
            x_norm(N_KV, U_FFN0)
            normed_hi(A_KV, a_out, lambda c: modcol(G_KV, c))
            split_to(B_KV + 3)
            for i in range(4):
                act.wait_ge(slab_done, B_KV + i + 1)
                dst = k_a[:, 2 * i:2 * i + 2, :] if i < 2 else v_a[:, :, 256 * (i - 2):256 * (i - 1)]
                act.copy(dst, bank[i][:, :].rearrange("p (c s) -> p c s", c=2)).then_inc(qkv_act, 1)
                if i == 3:
                    normed_hi(A_MIX1, a_out, lambda c: modcol(G_MIX1, c), B_Q)
                split_to(B_KV + i + 4)
            act.wait_ge(mod_red, G_A1 + 1)
            for t, n in ((0, P), (1, 256)):
                skew = bass.AP(tensor=scratch.tensor, offset=255 - P * t, ap=[[511, P], [512 * P, HEADS], [1, n]])
                act.dma_start(bias[:, :, P * t:P * t + n], skew).then_inc(s_bias, 16)
            for i in range(4):
                act.wait_ge(slab_done, B_Q + i + 1)
                act.activation(q_a[:, 2 * i:2 * i + 2, :], bank[i][:, :].rearrange("p (c s) -> p c s", c=2), ACT.Copy,
                               scale=P ** -0.5).then_inc(qkv_act, 1)
                split_to(B_Q + i + 4)

            def attention(heads, copy_out=None, norm_squares=None, norm=None):
                n = len(heads)

                def exps(k):
                    h = heads[k]
                    act.wait_ge(sc_done, h + 1)
                    if k >= 2:
                        act.wait_ge(tr_done, h - 1)
                    src, dst = sc, prob
                    for t, (lo, hi) in enumerate(((0, P), (P, 384))):
                        ins = act.activation(dst[:, h % 2, lo:hi], src[:, h % 2, lo:hi], ACT.Exp, scale=-1.0,
                                             bias=nmax[:, h % 2, t:t + 1], accum_out=ssum[:, h % 2, t:t + 1])
                    ins.then_inc(exp_done, 1)

                def turned(k):
                    h = heads[k]
                    act.wait_ge(tr_done, h + 1)
                    if k >= 2:
                        act.wait_ge(pv_done, h - 1)
                    act.copy(prob_t[:, h % 2, :], bank[2 + k % 2][:, 0:384]).then_inc(pt_done, 1)

                for k in range(-2, n + 1):
                    if 0 <= k < n:
                        turned(k)
                    if k + 2 < n:
                        exps(k + 2)
                    if copy_out is not None and k >= 1:
                        copy_out(k - 1)
                    if norm is not None and k == NORM_STEP:
                        norm_squares()
                    if norm is not None and k == NORM_STEP + 1:
                        norm()

            def moba_out(h):
                act.wait_ge(pv_done, h + 1)
                act.copy(a_hi[:, h, :], bank[4 + h % 2][:, 0:256]).then_inc(oh_done, 1)

            attention(list(range(HEADS)), moba_out)
            split_to(B_FFN1 + 2)
            x_norm(N_FFN1, U_MOBA)
            normed_hi(A_FFN1, a_out, lambda c: modcol(G_A1, CH + c))
            split_to(B_FFN1 + 3)
            ffn(1, B_FFN1)
            split_to(B_L2 + 2)
            x_norm(N_FIN, U_FFN1)

            def post(l, k, n, phase=None, slab=None):
                warm_up()
                for b4 in range(4):
                    if k == 3:
                        act.wait_ge(f_ready, 4 * (4 * l + k) + b4 + 1)
                        src = f[:, 2 * b4:2 * b4 + 2, :]
                    else:
                        if b4 < 3:
                            act.wait_ge(bank_done, 3 * phase + b4 + 1)
                        else:
                            act.wait_ge(slab_done, slab + 1)
                        src = bank[4 + b4][:, :].rearrange("p (c s) -> p c s", c=2)
                    act.activation(sq[:, 2 * b4:2 * b4 + 2, :], src, ACT.Square).then_inc(sq_ready, 2)
                if k == 3:
                    split_to(base2(l + 1) + 2)
                rsqrt(n, D)

            for l in range(LAYERS2):
                deferred_hi(U_FIN if l == 0 else u2(l - 1, 3), gain2(l, 0))
                split_to(base2(l) + 4)
                rsqrt(norm2(l, L_PRE1), D)
                ffn(2 + 2 * l, base2(l))
                b = base2(l, M_MIX)
                split_to(b + 2)
                post(l, 0, norm2(l, L_POST1), 4 + 3 * l, b - 1)
                deferred_hi(u2(l, 0), gain2(l, 2))
                c0, d0 = 8 + 8 * l, 8 * l
                split_to(b + 4)
                rsqrt(norm2(l, L_PREMIX), D)

                def values(i):
                    for t in range(2):
                        ins = act.activation(v_dil[:, t, 256 * i:256 * (i + 1)], bank[2 + i][:, 256 * t:256 * (t + 1)], ACT.Copy,
                                             scale=rcol[:, t:t + 1])
                    ins.then_inc(qkv_act, 1)

                squares(norm2(l, L_QLAT), lambda c: q_lat[:, c, :], lambda c: act.wait_ge(qkv_dve, d0 + 1))
                split_to(b + 5)
                squares(norm2(l, L_KVLAT), lambda c: kv_lat[:, c, :], lambda c: act.wait_ge(qkv_dve, d0 + 2))
                for i in range(4):
                    act.wait_ge(slab_done, b + 3 + i)
                    if i:
                        act.wait_ge(qkv_dve, d0 + 2 + i)
                    for q in range(4):
                        ins = act.copy(swap[32 * (q ^ 1):32 * (q ^ 1) + 32, :], bank[(2 + i) % 4][32 * q:32 * q + 32, :])
                    ins.then_inc(swap_ready, 1)
                    split_to(b + 6 + i)
                rsqrt(norm2(l, L_QLAT), 256)
                normed_hi(apply2(l, LA_QLAT), lambda c: a_hi[:, 8 + c, :])
                act.wait_ge(rows_zero, 3)
                act.wait_ge(slab_done, b + 7)
                act.wait_ge(rcol_ready, l + 1)
                values(0)
                split_to(b + 10)
                rsqrt(norm2(l, L_KVLAT), P)
                normed_hi(apply2(l, LA_KVLAT), lambda c: hid_hi[:, 0, 0, :], at=2)
                act.wait_ge(slab_done, b + 8)
                values(1)
                split_to(b + 11)
                for k in range(2):
                    act.wait_ge(up_done, UP2 * l + 2 + k)
                    act.copy(k_nope[:, 2 * k:2 * k + 2, :], bank[1 + k][:, :].rearrange("p (c s) -> p c s", c=2)).then_inc(qkv_act, 1)
                act.wait_ge(up_done, UP2 * l + 4)
                act.copy(v_mla[:, 0, :], bank[4][:, :]).then_inc(qkv_act, 1)
                act.wait_ge(slab_done, b + 9)
                act.copy(v_mla[:, 1, :], bank[5][:, :]).then_inc(qkv_act, 1)
                split_to(b + 12)
                for k, src in enumerate((bank[3], bank[6])):
                    act.wait_ge(up_done, UP2 * l + 5 + k)
                    for m in range(2):
                        ins = act.activation(q_nope[64 * m:64 * m + 64, 4 * k + m:4 * k + 4:2, :],
                                             src[64 * m:64 * m + 64, :].rearrange("p (c s) -> p c s", c=2), ACT.Copy, scale=96 ** -0.5)
                    ins.then_inc(qkv_act, 1)
                act.wait_ge(slab_done, b + 10)
                split_to(b + 13)
                o0 = 8 + 8 * l

                def dilated_squares():
                    act.wait_ge(o_done, o0 + 4)
                    squares(norm2(l, L_GDIL), lambda c: f[:, 4 + c, :], lambda c: None)

                def dilated_norm():
                    rsqrt(norm2(l, L_GDIL), 512)
                    normed_hi(apply2(l, LA_GDIL), lambda c: a_hi[:, 4 + c, :], at=4)

                attention([HEADS + 16 * l + k for k in range(16)], None, dilated_squares, dilated_norm)
                warm_up()
                squares(norm2(l, L_GMLA), lambda c: f[:, c, :], lambda c: act.wait_ge(o_done, o0 + 5 + c))
                rsqrt(norm2(l, L_GMLA), 512)
                normed_hi(apply2(l, LA_GMLA), a_out)
                bf = base2(l, M_FFN)
                split_to(bf + 2)
                post(l, 1, norm2(l, L_POSTMIX), 5 + 3 * l, bf - 1)
                deferred_hi(u2(l, 1), gain2(l, 4))
                split_to(bf + 4)
                rsqrt(norm2(l, L_PRE2), D)
                ffn(3 + 2 * l, bf)
                act.wait_ge(slab_done, bf + 3 * FJ)
                act.copy(hid_hi[:, 1], ptok[:, l]).then_inc(ph_ready, 1)
                split_to(bf + 3 * FJ + 3)
                post(l, 2, norm2(l, L_POST2), 6 + 3 * l, bf + 3 * FJ - 1)
                deferred_hi(u2(l, 2), gain2(l, 6))
                split_to(bf + 3 * FJ + 5)
                rsqrt(norm2(l, L_PREPLE), D)
                for i in range(4):
                    act.wait_ge(pg_scaled, 4 * l + i + 1)
                    act.activation(gate_s[:, i % 2, :], gate_s[:, i % 2, :], ACT.Sigmoid).then_inc(pg_ready, 1)
                    if i == 1:
                        split_to(base2(l + 1) + 1)
                post(l, 3, norm2(l, L_POSTPLE))

        @block.vector
        def _(dve):
            made = [0]
            trig = [0]

            def split_to(n):
                for s in range(made[0], min(n, SLABS)):
                    dve.wait_ge(hi_ready, s + 1)
                    dve.tensor_tensor(w_lo[:, s % RING, :], raw[:, s % RING, :], w_hi[:, s % RING, :].bitcast(F32),
                                      ALU.subtract).then_inc(lo_ready, 1)
                made[0] = max(made[0], min(n, SLABS))

            steps = [0]

            def mod(g, kc):
                s = steps[0]
                slot, landings = mod_slot(s)
                dve.wait_ge(mod_landed[slot], 16 * landings)
                acc = mod_sums(g)
                if kc == 0:
                    if g in (G_B0, G_KV, G_MIX1, G_B1):
                        dve.wait_ge(mod_red, g - 1)
                    ins = dve.tensor_scalar(acc, mod_slots[slot], cs[:, 0:1], None, ALU.mult)
                else:
                    dve.wait_ge(mod_step, s)
                    ins = dve.scalar_tensor_tensor(out=acc, in0=mod_slots[slot], scalar=cs[:, kc:kc + 1], in1=acc,
                                                   op0=ALU.mult, op1=ALU.add)
                ins.then_inc(mod_step, 1)
                steps[0] += 1

            def mod_columns(g, b):
                dve.wait_ge(mod_red, g + 1)
                at = COL_AT["mod_b"] + 16 * g
                dve.tensor_tensor(modc[:, 16 * g:16 * g + 16], bank[b][:, 0:16], cols[:, at:at + 16], ALU.add).then_inc(modc_ready, 1)

            def scale_of(k, g, at, gain):
                dve.wait_ge(modc_ready, g + 1)
                dve.scalar_tensor_tensor(out=scale1[:, CH * k:CH * k + CH], in0=modc[:, 16 * g + at:16 * g + at + CH], scalar=1.0,
                                         in1=cols[:, gain:gain + CH], op0=ALU.add, op1=ALU.mult).then_inc(scale_ready, 1)

            def root(n, features):
                dve.wait_ge(rs0_ready, n + 1)
                dve.scalar_tensor_tensor(out=nwt[:, :], in0=rs0[:, :], scalar=-0.5 / features, in1=rs0[:, :], op0=ALU.mult, op1=ALU.mult).then_inc(newton, 1)
                dve.wait_ge(newton, 2 * n + 1)
                dve.scalar_tensor_tensor(out=nwt[:, :], in0=bank[stat_bank(n)][:, 0:S], scalar=EPS * features, in1=nwt[:, :],
                                         op0=ALU.add, op1=ALU.mult).then_inc(newton, 1)
                dve.wait_ge(newton, 2 * n + 2)
                dve.scalar_tensor_tensor(out=rstd[:, n % 2, :], in0=nwt[:, :], scalar=1.5, in1=rs0[:, :], op0=ALU.add, op1=ALU.mult).then_inc(rstd_ready, 1)
                dve.wait_ge(rstd_ready, n + 1)

            def over_rms(n):
                return rstd[:, n % 2:n % 2 + 1, :].to_broadcast([P, 2, S])

            def pair(v):
                return v.rearrange("p (c s) -> p c s", c=2)

            def deferred_low(ap, c, gain):
                dve.wait_ge(nh_ready, before(APPLY_CHUNKS, ap) + c + 1)
                dve.scalar_tensor_tensor(out=a_lo[:, c, :], in0=x[:, c, :], scalar=gain(c), in1=a_hi[:, c, :].bitcast(F32),
                                         op0=ALU.mult, op1=ALU.subtract).then_inc(nl_ready, 1)

            def normed(ap, n, src, gain, hi, lo, shift=None, at=0):
                a0, m = before(APPLY_CHUNKS, ap), APPLY_CHUNKS[ap]

                def low(c):
                    dve.wait_ge(nh_ready, a0 + c + 1)
                    if shift is None:
                        ins = dve.tensor_tensor(lo(c), sq[:, at + c, :], hi(c).bitcast(F32), ALU.subtract)
                    else:
                        ins = dve.scalar_tensor_tensor(out=lo(c), in0=sq[:, at + c, :], scalar=shift(c), in1=hi(c).bitcast(F32),
                                                       op0=ALU.add, op1=ALU.subtract)
                    ins.then_inc(nl_ready, 1)

                for c in range(m):
                    dve.scalar_tensor_tensor(out=sq[:, at + c, :], in0=src(c), scalar=gain(c), in1=rstd[:, n % 2, :],
                                             op0=ALU.mult, op1=ALU.mult).then_inc(nt_ready, 1)
                    if c >= 1:
                        low(c - 1)
                low(m - 1)

            def x_src(c):
                return x[:, c, :]

            def a_h(c):
                return a_hi[:, c, :]

            def a_l(c):
                return a_lo[:, c, :]

            def bank_sums(phase, b4, slab):
                if b4 < 3:
                    dve.wait_ge(bank_done, 3 * phase + b4 + 1)
                else:
                    dve.wait_ge(slab_done, slab + 1)

            def add_gated(phase, slab, gate):
                for c in range(CH):
                    if c % 2 == 0:
                        bank_sums(phase, c // 2, slab)
                    dve.scalar_tensor_tensor(out=x[:, c, :], in0=bank[4 + c // 2][:, (c % 2) * S:(c % 2 + 1) * S], scalar=gate(c),
                                             in1=x[:, c, :], op0=ALU.mult, op1=ALU.add).then_inc(x_ready, 1)

            def link(ins):
                trig[0] += 1
                ins.then_inc(trig_step, 1)
                dve.wait_ge(trig_step, trig[0])

            def rope_angle(part):
                kind, k = part // 2, part % 2
                if part == 0:
                    dve.wait_ge(s_late, 48)
                    link(dve.tensor_copy(pos_f, pos_i))
                if k == 0:
                    link(dve.tensor_scalar(ang, pos_f, col("inv_dil" if kind else "inv_mla", 0), None, ALU.mult))
                r, t = red[:, k, :], turn[:, k, :]
                if kind:
                    dve.wait_ge(trig_act, k + 1)
                link(dve.tensor_scalar(t, ang, 1.0 / TWO_PI, 0.25 if k == 0 else 0.0, ALU.mult, ALU.add))
                link(dve.tensor_scalar(t, t, MAGIC, -MAGIC, ALU.add, ALU.add))
                link(dve.scalar_tensor_tensor(out=r, in0=t, scalar=-C1, in1=ang, op0=ALU.mult, op1=ALU.add))
                link(dve.scalar_tensor_tensor(out=r, in0=t, scalar=-C2, in1=r, op0=ALU.mult, op1=ALU.add))
                link(dve.scalar_tensor_tensor(out=r, in0=t, scalar=-C3, in1=r, op0=ALU.mult, op1=ALU.add))
                link(dve.tensor_scalar(r, r, math.pi / 2 if k == 0 else 0.0, PI_SAFE, ALU.add, ALU.min))
                link(dve.tensor_scalar(r, r, -PI_SAFE, None, ALU.max))
                assert trig[0] == TRIG_AT[part]

            def ffn(i, b):
                def early(kc):
                    if i == 0:
                        mod(G_A1, kc)

                def angle(part):
                    if i == 1:
                        rope_angle(part)

                f0 = FJ * i

                n = None if i < 2 else norm2((i - 2) // 2, L_PRE1 if i % 2 == 0 else L_PRE2)

                def gate(j, par, done, first=False):
                    if i < 2:
                        return
                    dve.wait_ge(slab_done, done)
                    if not first:
                        dve.wait_ge(hid_done, j + (f0 - 1))
                    dve.tensor_tensor(pair(gate_s[:, par, :]), pair(bank[par][:, :]), over_rms(n), ALU.mult).then_inc(gate_scaled, 1)

                def hidden(j, par, up, first=False):
                    if i >= 2:
                        dve.wait_ge(slab_done, up)
                        if not first:
                            dve.wait_ge(hl_ready, j + (f0 - 1))
                        dve.tensor_tensor(pair(hid[:, par, :]), pair(bank[2 + par][:, :]), over_rms(n), ALU.mult).then_inc(up_scaled, 1)
                        dve.wait_ge(up_scaled, j + (FJ * (i - 2) + 1))
                        dve.wait_ge(silu_done, j + (f0 + 1))
                        dve.tensor_tensor(hid[:, par, :], hid[:, par, :], gate_s[:, par, :], ALU.mult).then_inc(hid_done, 1)
                        return
                    dve.wait_ge(silu_done, j + (f0 + 1))
                    dve.wait_ge(slab_done, up)
                    dve.tensor_tensor(hid[:, par, :], bank[2 + par][:, :], gate_s[:, par, :], ALU.mult).then_inc(hid_done, 1)

                def hidden_lo(j, par):
                    dve.wait_ge(hh_ready, j + (f0 + 1))
                    dve.tensor_tensor(hid_lo[:, par].rearrange("p c s -> p (c s)"), hid[:, par, :],
                                      hid_hi[:, par].rearrange("p c s -> p (c s)").bitcast(F32), ALU.subtract).then_inc(hl_ready, 1)

                def low(count, slot):
                    dve.wait_ge(hi_ready, count)
                    dve.tensor_tensor(w_lo[:, slot, :], raw[:, slot, :], w_hi[:, slot, :].bitcast(F32), ALU.subtract).then_inc(lo_ready, 1)

                split_to(b + 4)
                gate(0, 0, b + 1, True)
                hidden(0, 0, b + 2, True)
                split_to(b + 5)
                angle(0)
                early(0)
                hidden_lo(0, 0)
                gate(1, 1, b + 3, True)
                split_to(b + 6)
                angle(1)
                early(1)
                hidden(1, 1, b + 4, True)
                split_to(b + 7)
                angle(2)
                early(2)
                hidden_lo(1, 1)
                split_to(b + 8)
                angle(3)
                early(3)
                if i == 0:
                    for g in (G_KV, G_MIX1):
                        dve.wait_ge(mod_red, g - 1)
                        dve.memset(mod_sums(g), 0.0).then_inc(acc_zero, 1)
                    dve.wait_ge(acc_zero, 2)
                s0 = steps[0]
                with dve.Fori(0, (FJ - 3) // 2) as k:
                    for h in range(2):
                        g = b + 5 + 3 * h
                        gate(2 * k + (2 + h), h, 6 * k + (g + 1))
                        low(6 * k + (g + 4), g % RING)
                        hidden(2 * k + (2 + h), h, 6 * k + (g + 2))
                        low(6 * k + (g + 5), (g + 1) % RING)
                        hidden_lo(2 * k + (2 + h), h)
                        low(6 * k + (g + 6), (g + 2) % RING)
                        if i == 0:
                            for m, gr in enumerate((G_KV, G_MIX1)):
                                e = 2 * h + m
                                slot, landings = mod_slot(s0 + e)
                                dve.wait_ge(mod_landed[slot], 32 * k + 16 * landings)
                                dve.wait_ge(mod_step, 4 * k + (s0 + e - 1))
                                acc = mod_sums(gr)
                                dve.scalar_tensor_tensor(out=acc, in0=mod_slots[slot], scalar=cs[:, bass.ds(2 * k + h, 1)],
                                                         in1=acc, op0=ALU.mult, op1=ALU.add).then_inc(mod_step, 1)
                if i == 0:
                    steps[0] += 16
                made[0] = b + 3 * (FJ - 2) + 5
                j = FJ - 1
                gate(j, j % 2, b + 3 * j)
                split_to(b + 3 * j + 3)
                hidden(j, j % 2, b + 3 * j + 1)
                if i == 0:
                    mod(G_A1, 4)
                split_to(b + 3 * j + 4)
                hidden_lo(j, j % 2)
                if i == 0:
                    mod(G_A1, 5)
                split_to(b + 3 * j + 5)

            dve.wait_ge(s_rb, 16)
            dve.tensor_copy(rbb[0:32, :, :], rb_sb[:, :].unsqueeze(2).to_broadcast([32, HEADS, P])).then_inc(rbb_ready, 1)
            dve.memset(rbb[32:33, :, :], 1.0).then_inc(rbb_ready, 1)
            dve.memset(xp[:, :, :, 0:3], 0.0).then_inc(pad_zero, 1)
            dve.wait_ge(lam_act, 2)
            lam_n = [0]

            def lam_link(ins):
                lam_n[0] += 1
                ins.then_inc(lam_dve, 1)
                dve.wait_ge(lam_dve, lam_n[0])

            u, s1, s2, v = lam[:, 1, :], lam[:, 2, :], lam[:, 3, :], lam[:, 4, :]
            lam_link(dve.tensor_scalar(v, u, 2.0, None, ALU.add))
            lam_link(dve.reciprocal(s2, v))
            lam_link(dve.tensor_tensor(s1, u, s2, ALU.mult))
            lam_link(dve.tensor_tensor(s2, s1, s1, ALU.mult))
            lam_link(dve.tensor_scalar(v, s2, 1.0 / ATANH_LAST, None, ALU.mult))
            for d in range(ATANH_LAST - 2, 1, -2):
                lam_link(dve.scalar_tensor_tensor(out=v, in0=v, scalar=1.0 / d, in1=s2, op0=ALU.add, op1=ALU.mult))
            lam_link(dve.scalar_tensor_tensor(out=v, in0=v, scalar=1.0, in1=s1, op0=ALU.add, op1=ALU.mult))
            at = COL_AT["lambda"]
            lam_link(dve.tensor_scalar(lam[:, 5, :], cols[:, at:at + LCH], -1.0, 0.0, ALU.mult, ALU.max))
            lam_link(dve.scalar_tensor_tensor(out=v, in0=v, scalar=2.0, in1=lam[:, 5, :], op0=ALU.mult, op1=ALU.add))
            lam_link(dve.tensor_scalar(lam[:, 6, :], v, -8.0, None, ALU.mult))
            lam_link(dve.tensor_scalar(lam[:, 7, :], v, 8.0, None, ALU.mult))
            assert lam_n[0] == LAM_STEPS
            for l in range(LAYERS2):
                for k in range(2):
                    at = COL_AT["gains2"] + 64 * l + CH * (1 + 4 * k)
                    dve.tensor_scalar(half_g[:, 16 * l + CH * k:16 * l + CH * k + CH], cols[:, at:at + CH], 0.5, None, ALU.mult).then_inc(half_ready, 1)
            dve.wait_ge(cs_ready, 1)
            for kc in range(8):
                mod(G_MIX0, kc)
                if 4 <= kc < 7:
                    split_to(kc - 3)
                if kc == 6:
                    root(N_MIX0, D)
            mod_columns(G_MIX0, 7)
            scale_of(0, G_MIX0, CH, COL_AT["norm_mix"])
            dve.wait_ge(scale_ready, 1)
            normed(A_MIX0, N_MIX0, x_src, lambda c: scale1[:, c:c + 1], a_h, a_l, lambda c: modcol(G_MIX0, c))

            for i in range(5):
                s = B_WIN + i
                dve.wait_ge(xbr_ready, i + 1)
                for k in range(3):
                    for m in range(2):
                        c = 2 * i + m
                        if k:
                            dve.wait_ge(conv_step, conv_count(i, k - 1, m))
                        ins = dve.scalar_tensor_tensor(out=xc[:, c, :], in0=xp[:, i % 2, m, k:k + S], scalar=col("conv_w", k * LCH + c),
                                                       in1=xc[:, c, :], op0=ALU.mult, op1=ALU.add)
                        ins.then_inc(conv_done if (k, m) == (2, 1) else conv_step, 1)
                split_to(s + 4)
            for i in range(5):
                split_to(B_WIN + 8 + i)
                mod(G_A0, i)
            for hd in range(LHEADS):
                dve.wait_ge(xch_ready, hd + 1)
                dve.tensor_tensor(a_lo[:, 2 * hd:2 * hd + 2, :], xc[:, 2 * hd:2 * hd + 2, :], a_hi[:, 2 * hd:2 * hd + 2, :].bitcast(F32),
                                  ALU.subtract).then_inc(xcl_ready, 1)
            split_to(B_GATE + 3)
            for hd in range(LHEADS):
                h2 = slice(2 * hd, 2 * hd + 2)
                dve.wait_ge(gates_ready, 2 * hd + 2)
                dve.tensor_tensor(i_g[:, h2, :], i_g[:, h2, :], xc[:, h2, :], ALU.mult).then_inc(bi_ready, 1)
                if hd < 3:
                    mod(G_A0, 5 + hd)
                if hd == 2:
                    split_to(B_LOUT + 1)
            split_to(B_LOUT + 2)
            for hd in range(LHEADS):
                h2, tmp = slice(2 * hd, 2 * hd + 2), sq[:, 2 * (hd % 4):2 * (hd % 4) + 2, :]
                dve.wait_ge(decay_ready, hd + 1)
                dve.tensor_tensor(tmp, xc[:, h2, :], xc[:, h2, :], ALU.mult).then_inc(mult2_step, 1)
                dve.wait_ge(mult2_step, hd + 1)
                dve.scalar_tensor_tensor(out=r_g[:, h2, :], in0=tmp, scalar=1.0, in1=r_g[:, h2, :], op0=ALU.add, op1=ALU.mult).then_inc(mult2_ready, 1)
                if hd in (0, 2):
                    mod(G_B0, hd // 2)
            split_to(B_LOUT + 3)

            def z_low(hd):
                h2 = slice(2 * hd, 2 * hd + 2)
                dve.wait_ge(zh_ready, hd + 1)
                dve.tensor_tensor(a_lo[:, h2, :], i_g[:, h2, :], a_hi[:, h2, :].bitcast(F32), ALU.subtract).then_inc(zl_ready, 1)

            for hd in range(LHEADS):
                h2 = slice(2 * hd, 2 * hd + 2)
                dve.wait_ge(mult_ready, hd + 1)
                dve.tensor_tensor(i_g[:, h2, :], i_g[:, h2, :], r_g[:, h2, :], ALU.mult).then_inc(scan_step, 1)
                dve.wait_ge(scan_step, 2 * hd + 1)
                for c in (2 * hd, 2 * hd + 1):
                    ins = dve.tensor_tensor_scan(r_g[:, c, :], xc[:, c, :], i_g[:, c, :], 0.0, ALU.mult, ALU.add)
                ins.then_inc(scan_step, 1)
                dve.wait_ge(scan_step, 2 * hd + 2)
                dve.tensor_tensor(i_g[:, h2, :], r_g[:, h2, :], y_br[:, h2, :], ALU.mult).then_inc(z_ready, 1)
                if hd:
                    z_low(hd - 1)
                if hd in (1, 2):
                    mod(G_B0, 1 + hd)
                if hd == 3:
                    split_to(B_LOUT + 4)
            z_low(LHEADS - 1)
            for kc in range(4, 6):
                mod(G_B0, kc)
            split_to(B_LOUT + 5)
            for kc in range(6, 8):
                mod(G_B0, kc)
            split_to(B_LOUT + 7)
            mod_columns(G_A0, 2)
            mod_columns(G_B0, 3)
            scale_of(1, G_B0, 0, COL_AT["norm_ffn"])
            split_to(B_FFN0 + 2)
            add_gated(0, B_LOUT + 4, lambda c: modcol(G_A0, c))
            root(N_FFN0, D)
            dve.wait_ge(scale_ready, 2)
            normed(A_FFN0, N_FFN0, x_src, lambda c: scale1[:, CH + c:CH + c + 1], a_h, a_l, lambda c: modcol(G_A0, CH + c))
            split_to(B_FFN0 + 3)
            ffn(0, B_FFN0)

            split_to(B_KV + 2)
            mod_columns(G_KV, 2)
            scale_of(2, G_KV, CH, COL_AT["kv_norm"])
            add_gated(1, B_FFN0 + 3 * FJ - 1, lambda c: modcol(G_B0, CH + c))
            root(N_KV, D)
            dve.wait_ge(scale_ready, 3)
            normed(A_KV, N_KV, x_src, lambda c: scale1[:, 2 * CH + c:2 * CH + c + 1], a_h, a_l, lambda c: modcol(G_KV, c))
            split_to(B_KV + 3)
            mod_columns(G_MIX1, 3)
            scale_of(3, G_MIX1, CH, COL_AT["norm_mix"] + CH)
            split_to(B_KV + 4)
            for kc in (6, 7):
                mod(G_A1, kc)
            split_to(B_KV + 5)
            split_to(B_KV + 6)
            dve.wait_ge(scale_ready, 4)
            normed(A_MIX1, N_KV, x_src, lambda c: scale1[:, 3 * CH + c:3 * CH + c + 1], a_h, a_l, lambda c: modcol(G_MIX1, c))
            split_to(B_KV + 7)
            mod(G_B1, 0)
            mod_columns(G_A1, 4)
            for i in range(3):
                split_to(B_Q + i + 4)
                mod(G_B1, 1 + i)
            split_to(B_Q + 7)

            def attention(heads, add, copy_out, norm=None):
                n = len(heads)

                def scores(k):
                    h = heads[k]
                    dve.wait_ge(qk_done, h + 1)
                    if k >= 2:
                        dve.wait_ge(exp_done, h - 1)
                    dst = sc
                    for t, (lo, hi) in enumerate(((0, P), (P, 384))):
                        ins = dve.tensor_tensor_reduce(dst[:, h % 2, lo:hi], bank[k % 2][:, lo:hi], add(k)[:, lo:hi], -1.0, 3.0e38,
                                                       ALU.add, ALU.min, nmax[:, h % 2, t:t + 1])
                    ins.then_inc(sc_done, 1)

                def normalise(k):
                    h = heads[k]
                    pr = prob
                    dve.wait_ge(exp_done, h + 1)
                    dve.reciprocal(rsum[:, h % 2, :], ssum[:, h % 2, :]).then_inc(rs_done, 1)
                    dve.wait_ge(rs_done, h + 1)
                    for t, (lo, hi) in enumerate(((0, P), (P, 384))):
                        ins = dve.tensor_scalar(pr[:, h % 2, lo:hi], pr[:, h % 2, lo:hi], rsum[:, h % 2, t:t + 1], None, ALU.mult)
                    ins.then_inc(pn_done, 1)

                for k in range(-3, n + 1):
                    if 0 <= k + 1 < n:
                        normalise(k + 1)
                    if k + 3 < n:
                        scores(k + 3)
                    if k >= 1:
                        copy_out(k - 1)
                    if norm is not None and k == NORM_STEP + 1:
                        norm()

            def moba_out(h):
                if h % 2:
                    mod(G_B1, 4 + h // 2)
                dve.wait_ge(oh_done, h + 1)
                dve.tensor_tensor(a_lo[:, h, :], bank[4 + h % 2][:, 0:256], a_hi[:, h, :].bitcast(F32), ALU.subtract).then_inc(o_done, 1)

            dve.wait_ge(s_bias, 32)
            attention(list(range(HEADS)), lambda k: bias[:, k, :], moba_out)
            assert steps[0] == 8 * MOD_GROUPS
            split_to(B_FFN1 + 2)
            mod_columns(G_B1, 0)
            scale_of(4, G_B1, 0, COL_AT["norm_ffn"] + CH)
            add_gated(2, B_O + 3, lambda c: modcol(G_A1, c))
            root(N_FFN1, D)
            dve.wait_ge(scale_ready, 5)
            normed(A_FFN1, N_FFN1, x_src, lambda c: scale1[:, 4 * CH + c:4 * CH + c + 1], a_h, a_l, lambda c: modcol(G_A1, CH + c))
            split_to(B_FFN1 + 3)
            ffn(1, B_FFN1)
            split_to(B_L2 + 2)
            add_gated(3, B_FFN1 + 3 * FJ - 1, lambda c: modcol(G_B1, CH + c))
            root(N_FIN, D)
            for c in range(CH):
                dve.scalar_tensor_tensor(out=x[:, c, :], in0=x[:, c, :], scalar=col("final_norm", c), in1=rstd[:, N_FIN % 2, :],
                                         op0=ALU.mult, op1=ALU.mult).then_inc(x_ready, 1)
                if c >= 2:
                    deferred_low(apply2(0, LA_PRE1), c - 2, lambda k: col("gains2", k))
            for c in (CH - 2, CH - 1):
                deferred_low(apply2(0, LA_PRE1), c, lambda k: col("gains2", k))

            def take_sums(l, k, n, phase, slab, gain):
                for b4 in range(4):
                    bank_sums(phase, b4, slab)
                    dve.wait_ge(sq_ready, before(NORM_CHUNKS, n) + 2 * b4 + 2)
                    for m in range(2):
                        c = 2 * b4 + m
                        ins = dve.tensor_scalar(f[:, c, :], bank[4 + b4][:, m * S:(m + 1) * S], gain(c), None, ALU.mult)
                    ins.then_inc(f_ready, 1)

            def post(l, k, n, gain=None, then=None):
                root(n, D)
                p = 4 * (4 * l + k)

                def scale(q):
                    c2 = slice(2 * q, 2 * q + 2)
                    dve.wait_ge(f_ready, p + q + 1)
                    if gain is None:
                        dve.tensor_tensor(f[:, c2, :], f[:, c2, :], over_rms(n), ALU.mult).then_inc(f_scaled, 1)
                        return
                    for c in (2 * q, 2 * q + 1):
                        ins = dve.scalar_tensor_tensor(out=f[:, c, :], in0=f[:, c, :], scalar=gain(c), in1=rstd[:, n % 2, :],
                                                       op0=ALU.mult, op1=ALU.mult)
                    ins.then_inc(f_scaled, 1)

                def add(q):
                    c2 = slice(2 * q, 2 * q + 2)
                    dve.wait_ge(f_scaled, p + q + 1)
                    dve.tensor_tensor(x[:, c2, :], x[:, c2, :], f[:, c2, :], ALU.add).then_inc(x_ready, 2)

                def low(q):
                    if then is not None:
                        for c in (2 * q, 2 * q + 1):
                            deferred_low(then[0], c, then[1])

                scale(0)
                for q in range(4):
                    if q < 3:
                        scale(q + 1)
                    add(q)
                    if q:
                        low(q - 1)
                low(3)

            def gain2(l, k):
                return lambda c: col("gains2", 64 * l + CH * k + c)

            n_rope = [0]

            def rlink(ins):
                n_rope[0] += 1
                ins.then_inc(rope_step, 1)
                return n_rope[0]

            def scaled(out, src, scale, table):
                return rlink(dve.scalar_tensor_tensor(out=out, in0=src, scalar=scale, in1=table, op0=ALU.mult, op1=ALU.mult))

            def place_free(taken):
                if n_rope[0]:
                    dve.wait_ge(rope_step, n_rope[0])
                    dve.wait_ge(qkv_dve, taken)

            def rope_dilated(dst, g, sums, scale, taken, swaps):
                both = lambda k: rope_r[:, k:k + 1, :].to_broadcast([P, 2, S])
                place_free(taken)
                dve.wait_ge(swap_ready, swaps)
                scaled(rt[:, 0:2, :], pair(sums[:, :]), scale, both(2))
                n = scaled(rt[:, 2:4, :], pair(swap), scale, both(3))
                dve.wait_ge(rope_step, n)
                if dst is k_dil:
                    dve.tensor_tensor(dst[:, 2 * g:2 * g + 2, :], rt[:, 0:2, :], rt[:, 2:4, :], ALU.add).then_inc(qkv_dve, 1)
                    return
                for m in range(2):
                    r = slice(64 * m, 64 * m + 64)
                    ins = dve.tensor_tensor(dst[r, 4 * g + m:4 * g + 4:2, :], rt[r, 0:2, :], rt[r, 2:4, :], ALU.add)
                ins.then_inc(qkv_dve, 1)

            for l in range(LAYERS2):
                split_to(base2(l) + 4)
                root(norm2(l, L_PRE1), D)
                ffn(2 + 2 * l, base2(l))
                if l == 0:
                    dve.wait_ge(trig_act, 4)
                    dve.tensor_scalar(rope[:, 1, :], rope[:, 1, :], col("sign_mla", 0), None, ALU.mult).then_inc(rope_ready, 1)
                    dve.tensor_scalar(rope[:, 3, :], rope[:, 3, :], col("sign_dil", 0), None, ALU.mult).then_inc(rope_ready, 1)
                b = base2(l, M_MIX)
                split_to(b + 2)
                dve.wait_ge(half_ready, 2 * LAYERS2)
                take_sums(l, 0, norm2(l, L_POST1), 4 + 3 * l, b - 1, lambda c: half_g[:, 16 * l + c:16 * l + c + 1])
                post(l, 0, norm2(l, L_POST1), None, (apply2(l, LA_PREMIX), gain2(l, 2)))
                split_to(b + 4)
                root(norm2(l, L_PREMIX), D)
                d0 = 8 * l
                dve.wait_ge(rope_ready, 2)
                if l:
                    place_free(d0)
                dve.tensor_tensor(rope_r[:, :, :], rope[:, :, :], rstd[:, norm2(l, L_PREMIX) % 2:norm2(l, L_PREMIX) % 2 + 1, :].to_broadcast([P, 4, S]),
                                  ALU.mult).then_inc(table_ready, 1)
                dve.wait_ge(rows_zero, 3)
                dve.wait_ge(slab_done, b + 1)
                dve.tensor_tensor(q_lat[:, :, :], pair(bank[0][:, :]), over_rms(norm2(l, L_PREMIX)), ALU.mult).then_inc(qkv_dve, 1)
                dve.wait_ge(slab_done, b + 2)
                dve.wait_ge(table_ready, l + 1)
                scaled(kr, bank[1][:, S:2 * S], 1.0, rope_r[:, 0, :])
                dve.tensor_tensor(kv_lat[:, 0, :], bank[1][:, 0:S], rstd[:, norm2(l, L_PREMIX) % 2, :], ALU.mult).then_inc(qkv_dve, 1)
                split_to(b + 5)
                for i in range(4):
                    dve.wait_ge(slab_done, b + 3 + i)
                    rope_dilated(q_dil if i < 2 else k_dil, i % 2, bank[(2 + i) % 4], 64 ** -0.5 if i < 2 else 1.0, d0 + 2 + i, 4 * l + i + 1)
                    split_to(b + 6 + i)
                    if i == 0:
                        dve.wait_ge(rturn_done, l + 1)
                        dve.tensor_copy(rcol[:, :], bank[5][:, 0:256:P]).then_inc(rcol_ready, 1)
                root(norm2(l, L_QLAT), 256)
                normed(apply2(l, LA_QLAT), norm2(l, L_QLAT), lambda c: q_lat[:, c, :], lambda c: col("q_norm2", 2 * l + c),
                       lambda c: a_hi[:, 8 + c, :], lambda c: a_lo[:, 8 + c, :])
                split_to(b + 10)
                root(norm2(l, L_KVLAT), P)
                normed(apply2(l, LA_KVLAT), norm2(l, L_KVLAT), lambda c: kv_lat[:, c, :], lambda c: col("kv_norm2", l + c),
                       lambda c: hid_hi[:, 0, 0, :], lambda c: hid_lo[:, 0, 0, :], None, 2)
                split_to(b + 11)
                dve.wait_ge(up_done, UP2 * l + 1)
                place_free(d0 + 6)
                n = scaled(rt[:, 0, :], bank[0][:, 0:S], 1.0, rope_r[:, 1, :])
                dve.wait_ge(rope_step, n)
                for h in range(4):
                    r = slice(32 * h, 32 * h + 32)
                    ins = dve.tensor_tensor(kr_m[r, h, :], kr[r, :], rt[r, 0, :], ALU.add)
                ins.then_inc(qkv_dve, 1)
                split_to(b + 12)
                dve.wait_ge(slab_done, b + 10)
                place_free(d0 + 7)
                for m in range(2):
                    scaled(rt[:, m, :], bank[7][:, m * S:(m + 1) * S], 96 ** -0.5, rope[:, 0, :])
                for m in range(2):
                    n = scaled(rt[:, 2 + m, :], bank[0][:, m * S:(m + 1) * S], 96 ** -0.5, rope[:, 1, :])
                dve.wait_ge(rope_step, n)
                dve.tensor_tensor(q_rope[:, :, :], rt[:, 0:2, :], rt[:, 2:4, :], ALU.add).then_inc(qkv_dve, 1)
                split_to(b + 13)

                def pair_out(k):
                    if k % 2:
                        h = HEADS + 16 * l + k
                        dve.wait_ge(pv_done, h + 1)
                        dve.tensor_copy(f[:, (k // 2 + 4) % 8, :], bank[4 + (k // 2) % 2][:, 0:256]).then_inc(o_done, 1)

                def dilated_norm():
                    root(norm2(l, L_GDIL), 512)
                    normed(apply2(l, LA_GDIL), norm2(l, L_GDIL), lambda c: f[:, 4 + c, :], lambda c: col("group2", CH * l + 4 + c),
                           lambda c: a_hi[:, 4 + c, :], lambda c: a_lo[:, 4 + c, :], None, 4)

                attention([HEADS + 16 * l + k for k in range(16)], lambda k: mask[:, 1 if k < HEADS else 0, :], pair_out, dilated_norm)
                root(norm2(l, L_GMLA), 512)
                normed(apply2(l, LA_GMLA), norm2(l, L_GMLA), lambda c: f[:, c, :], lambda c: col("group2", CH * l + c), a_h, a_l)
                bf = base2(l, M_FFN)
                split_to(bf + 2)
                take_sums(l, 1, norm2(l, L_POSTMIX), 5 + 3 * l, bf - 1, gain2(l, 3))
                post(l, 1, norm2(l, L_POSTMIX), None, (apply2(l, LA_PRE2), gain2(l, 4)))
                split_to(bf + 4)
                root(norm2(l, L_PRE2), D)
                ffn(3 + 2 * l, bf)
                dve.wait_ge(ph_ready, l + 1)
                dve.tensor_tensor(hid_lo[:, 1], ptok[:, l], hid_hi[:, 1].bitcast(F32), ALU.subtract).then_inc(pl_ready, 1)
                split_to(bf + 3 * FJ + 3)
                take_sums(l, 2, norm2(l, L_POST2), 6 + 3 * l, bf + 3 * FJ - 1, lambda c: half_g[:, 16 * l + CH + c:16 * l + CH + c + 1])
                post(l, 2, norm2(l, L_POST2), None, (apply2(l, LA_PREPLE), gain2(l, 6)))
                split_to(bf + 3 * FJ + 5)
                n = norm2(l, L_PREPLE)
                root(n, D)

                def embed(i):
                    dve.wait_ge(pg_ready, 4 * l + i + 1)
                    dve.tensor_tensor(f[:, 2 * i:2 * i + 2, :], pair(bank[4 + i][:, :]), pair(gate_s[:, i % 2, :]), ALU.mult).then_inc(f_ready, 1)

                for i in range(4):
                    dve.wait_ge(slab_done, base2(l, M_PGATE) + i + 1)
                    if i >= 2:
                        dve.wait_ge(f_ready, 4 * (4 * l + 3) + i - 1)
                    dve.tensor_tensor(pair(gate_s[:, i % 2, :]), pair(bank[i][:, :]), over_rms(n), ALU.mult).then_inc(pg_scaled, 1)
                    if i:
                        embed(i - 1)
                    if i == 1:
                        split_to(base2(l + 1) + 1)
                embed(3)
                split_to(base2(l + 1) + 2)
                then = (apply2(l + 1, LA_PRE1), gain2(l + 1, 0)) if l + 1 < LAYERS2 else None
                post(l, 3, norm2(l, L_POSTPLE), gain2(l, 7), then)


def rope_slot(h):
    return h % 4


GATE_ENDS = (1, 3, 4)
ATANH_LAST = 17
LAM_STEPS = 5 + (ATANH_LAST - 3) // 2 + 5
TRIG_AT = [9, 16, 24, 31]
MOD_ORDER = ([(g, k) for g in (G_MIX0, G_A0, G_B0) for k in range(8)] + [(G_A1, k) for k in range(4)]
             + [(g, k) for k in range(8) for g in (G_KV, G_MIX1)] + [(G_A1, k) for k in range(4, 8)] + [(G_B1, k) for k in range(8)])
MOD_LAST = [max(i for i, (h, _) in enumerate(MOD_ORDER) if h == g) + 1 for g in range(MOD_GROUPS)]
UP2 = 6
WARM_BEFORE, WARM_AFTER = 10, 14
NORM_STEP = 9
OUT_ORDER = (2, 3, 0, 1)


def conv_count(i, k, m):
    return 5 * i + 2 * k + m + 1


def wide(w):
    return w.reshape(-1, P, w.shape[1]).transpose(1, 0, 2).reshape(P, -1)


def stream_slabs(a):
    win = a["lru_w_in"][0]
    for at in (LRU, 0):
        for i in range(5):
            yield wide(win[:, at + 256 * i:at + 256 * (i + 1)])
    g = a["lru_w_gates"][0]
    for i in range(0, LHEADS, 2):
        yield np.concatenate([wide(g[h]) if h < LHEADS else np.zeros((P, 1024), np.float32) for h in (i, i + 1)], axis=1)
    yield from tall(a["lru_w_out"][0])
    yield from ffn_slabs(a["ffn_w_gate"][0], a["ffn_w_up"][0], a["ffn_w_down"][0])
    for w in (a["w_kv"], a["attn_w_q"][0]):
        for i in range(4):
            yield wide(w[:, 256 * i:256 * (i + 1)])
    yield from tall(a["attn_w_o"][0])
    yield from ffn_slabs(a["ffn_w_gate"][1], a["ffn_w_up"][1], a["ffn_w_down"][1])
    for l in range(LAYERS2):
        yield from ffn_slabs(a["ffn_gate_2"][l, 0], a["ffn_up_2"][l, 0], a["ffn_down_2"][l, 0])
        w = a["w_in_2"][l]
        kr, rot = w[:, 384:416], np.concatenate([w[:, 400:416], w[:, 384:400]], axis=1)
        yield wide(w[:, 0:256])
        yield wide(np.concatenate([w[:, 256:384]] + [kr] * 4, axis=1))
        for part in range(2):
            for g in range(2):
                yield wide(w[:, 416 + 512 * part + 256 * g:416 + 512 * part + 256 * (g + 1)])
        for i in range(2):
            yield wide(w[:, 1440 + 256 * i:1440 + 256 * (i + 1)])
        up = a["w_kv_up_2"][l].reshape(P, HEADS, 2, 64).transpose(0, 2, 1, 3).reshape(P, 1024)
        yield np.concatenate([wide(np.concatenate([rot] * 4, axis=1)), up], axis=1)
        q = a["w_q_up_2"][l].reshape(256, HEADS, 96)
        slots = [4 * c + next(h for h in range(4) if rope_slot(h) == s) for c in range(2) for s in range(4)]
        pairs = q[:, slots, 64:]
        turned = np.concatenate([pairs[:, :, 16:], pairs[:, :, :16]], axis=2)
        yield wide(np.concatenate([q[:, :, :64].reshape(256, 512), pairs.reshape(256, 256), turned.reshape(256, 256)], axis=1))
        out = list(tall(a["w_out_2"][l]))
        yield from (out[i] for i in OUT_ORDER)
        yield from ffn_slabs(a["ffn_gate_2"][l, 1], a["ffn_up_2"][l, 1], a["ffn_down_2"][l, 1])
        yield from tall(a["w_ple_2"][l])
        w = a["w_ple_gate_2"][l]
        for i in range(4):
            yield wide(w[:, 256 * i:256 * (i + 1)])


def tall(w):
    for i in range(0, w.shape[0], 256):
        yield wide(w[i:i + 256])


def ffn_slabs(gate, up, down):
    d = list(tall(down))
    for j in range(FJ):
        yield wide(gate[:, 256 * j:256 * (j + 1)])
        yield wide(up[:, 256 * j:256 * (j + 1)])
        if j:
            yield d[j - 1]
    yield d[FJ - 1]


def mod_slabs(a):
    m, kv = a["mod_w"], a["kv_mod_w"]
    groups = [m[0][:, 0:2048], m[0][:, 2048:4096], m[0][:, 4096:6144], kv, m[1][:, 0:2048], m[1][:, 2048:4096], m[1][:, 4096:6144]]
    for g, k in MOD_ORDER:
        yield groups[g][P * k:P * (k + 1)]


def columns(a):
    def cut(v):
        return v.reshape(-1, P).T
    inv_m = (10000.0 ** (-np.arange(0, 32, 2, dtype=np.float32) / np.float32(32))).astype(np.float32)
    inv_d = (10000.0 ** (-np.arange(0, 64, 2, dtype=np.float32) / np.float32(64))).astype(np.float32)
    parts = {
        "c": cut(a["c"]), "norm_mix": cut(a["norm_mix"]), "norm_ffn": cut(a["norm_ffn"]), "kv_norm": cut(a["kv_norm"]),
        "final_norm": cut(a["final_norm"]), "gains2": cut(a["norm_gains_2"]), "q_norm2": cut(a["q_norm_2"]),
        "kv_norm2": cut(a["kv_norm_2"]), "group2": cut(a["group_out_norm_2"]), "conv_w": cut(a["lru_conv_w"]),
        "conv_b": cut(a["lru_conv_b"]), "b_gates": cut(a["lru_b_gates"]), "lambda": cut(a["lru_lambda"]),
        "mod_b": np.concatenate([cut(a["mod_b"][0]), cut(a["kv_mod_b"]), cut(a["mod_b"][1])], axis=1),
        "inv_mla": np.tile(inv_m, 8)[:, None], "inv_dil": np.tile(inv_d, 4)[:, None],
        "sign_mla": np.tile(np.repeat(np.array([-1.0, 1.0], np.float32), 16), 4)[:, None],
        "sign_dil": np.tile(np.repeat(np.array([-1.0, 1.0], np.float32), 32), 2)[:, None],
    }
    for n, k in COLS:
        assert parts[n].shape == (P, k), (n, parts[n].shape, k)
    return np.ascontiguousarray(np.concatenate([parts[n] for n, _ in COLS], axis=1))


def bucket(dist):
    if dist < 16:
        return dist
    return min(16 + int(math.log(dist / 16) / math.log(8) * 16 + 1e-9), 31)


def shape_constants():
    onehot = np.zeros((33, 512), np.float32)
    for y in range(512):
        if y <= 255:
            onehot[bucket(255 - y), y] = 1.0
        else:
            onehot[32, y] = NEG
    q, k = np.arange(S)[:, None], np.arange(S)[None, :]
    dist = q - k
    causal = np.where(dist >= 0, 0.0, NEG)
    times = (dist >= 0) * sum(((dist % d == 0) & (dist <= w)).astype(int) for w, d in ((128, 1), (512, 4), (2048, 16)))
    dilated = np.where(times > 0, np.log(np.maximum(times, 1)), NEG)
    masks = np.stack([np.concatenate([m[:P, :P], m[P:, :]], axis=1) for m in (causal, dilated)]).astype(np.float32)
    return onehot, masks


def kernel(**inputs):
    import concourse.bacc as bacc
    from concourse.bass_utils import run_bass_kernel_spmd

    a = {k: np.asarray(v) for k, v in inputs.items()}
    onehot, masks = shape_constants()
    stream = np.empty((SLABS, P, DINNER), np.float32)
    n = 0
    for slab in stream_slabs(a):
        stream[n] = slab
        n += 1
    assert n == SLABS
    mods = np.empty((8 * MOD_GROUPS, P, DINNER), np.float32)
    for n, slab in enumerate(mod_slabs(a)):
        mods[n] = slab
    arrays = {
        "stream": stream, "mods": mods,
        "x_t": np.ascontiguousarray(a["x"][0].T),
        "cols": columns(a),
        "onehot": onehot,
        "rb_t": np.ascontiguousarray(a["rel_bias"].T),
        "masks": masks,
        "pos": np.ascontiguousarray(np.broadcast_to(a["positions_2"], (P, S))),
        "p_t": np.ascontiguousarray(a["p_2"][:, 0].transpose(0, 2, 1)),
    }
    nc = bacc.Bacc("TRN2", target_bir_lowering=False, num_devices=1)
    args = {k: nc.dram_tensor("in_" + k, v.shape, mybir.dt.from_np(v.dtype), kind="ExternalInput").ap() for k, v in arrays.items()}
    out_t = nc.dram_tensor("out_t", (D, S), F32, kind="ExternalOutput").ap()
    build(nc, args["stream"], args["mods"], args["x_t"], args["cols"], args["onehot"], args["rb_t"], args["masks"], args["pos"],
          args["p_t"], out_t)
    r = run_bass_kernel_spmd(nc, [{"in_" + k: v for k, v in arrays.items()}], core_ids=[0])
    return np.ascontiguousarray(r.results[0]["out_t"].T)[None]
```

```python
import math
from contextlib import ExitStack

import numpy as np

import concourse.bass as bass
from concourse import mybir

F32 = mybir.dt.float32
F32R = mybir.dt.float32r
I32 = mybir.dt.int32
ALU = mybir.AluOpType
ACT = mybir.ActivationFunctionType

P = 128
S = 256
D = 1024
CH = D // P
DFF = 2816
FJ = DFF // 256
LRU = 1280
LCH = LRU // P
LHEADS = 5
HEADS = 8
KVH = 4
LAYERS2 = 2
DINNER = 2048
EPS = 1e-6
NEG = -1e30
MAGIC = 12582912.0
TWO_PI = 2.0 * math.pi
C1 = 6.28125
C2 = float(np.float32(np.round((TWO_PI - C1) * 2**21) / 2**21))
C3 = TWO_PI - C1 - C2
PI_SAFE = 3.1415925

B_WIN = 0
B_GATE = B_WIN + 10
B_LOUT = B_GATE + 3
B_FFN0 = B_LOUT + 5
B_KV = B_FFN0 + 3 * FJ
B_Q = B_KV + 4
B_O = B_Q + 4
B_FFN1 = B_O + 4
B_L2 = B_FFN1 + 3 * FJ
M_MIX = 3 * FJ
M_OUT = M_MIX + 10
M_FFN = M_OUT + 4
M_PLE = M_FFN + 3 * FJ
M_PGATE = M_PLE + 1
PER_L2 = M_PGATE + 4
SLABS = B_L2 + LAYERS2 * PER_L2
RING = 3

MOD_GROUPS = 7
MOD_RING = 4
MOD_HALF = DINNER // 2
G_MIX0, G_A0, G_B0, G_KV, G_MIX1, G_A1, G_B1 = range(MOD_GROUPS)

N_MIX0, N_FFN0, N_KV, N_FFN1, N_FIN = range(5)
L_PRE1, L_POST1, L_PREMIX, L_QLAT, L_KVLAT, L_GDIL, L_GMLA, L_POSTMIX, L_PRE2, L_POST2, L_PREPLE, L_POSTPLE = range(12)
NORM_CHUNKS = [CH] * 5 + [8, 8, 8, 2, 1, 4, 4, 8, 8, 8, 8, 8] * LAYERS2
A_MIX0, A_FFN0, A_KV, A_MIX1, A_FFN1 = range(5)
LA_PRE1, LA_PREMIX, LA_QLAT, LA_KVLAT, LA_GDIL, LA_GMLA, LA_PRE2, LA_PREPLE = range(8)
APPLY_CHUNKS = [CH] * 5 + [8, 8, 2, 1, 4, 4, 8, 8] * LAYERS2


DEFERRED = (LA_PRE1, LA_PREMIX, LA_PRE2, LA_PREPLE)
TURNED_CHUNKS = [CH] * 5 + [0 if k in DEFERRED else APPLY_CHUNKS[5 + k] for k in range(8)] * LAYERS2
SUM_ALL = (L_PRE1, L_PREMIX, L_PRE2, L_PREPLE)
SUM_SIX = (L_POST1, L_POSTMIX, L_POST2, L_POSTPLE)


def before(counts, n):
    return sum(counts[:n])


def summed(n):
    if n < 5:
        return 0 if n == N_MIX0 else 6
    k = (n - 5) % 12
    return CH if k in SUM_ALL else 6 if k in SUM_SIX else 0


SUMMED = [n for n in range(len(NORM_CHUNKS)) if summed(n)]


def stat_bank(n):
    if n < 5:
        return {N_MIX0: 6, N_FFN1: 2}.get(n, 0)
    return {L_PRE1: 4, L_PREMIX: 4, L_QLAT: 6, L_KVLAT: 7, L_GDIL: 6, L_PRE2: 4, L_PREPLE: 3}.get((n - 5) % 12, 0)


def norm2(l, k):
    return 5 + 12 * l + k


def apply2(l, k):
    return 5 + 8 * l + k


def norm_at(n):
    return {L_KVLAT: 2, L_GDIL: 4}.get((n - 5) % 12, 0) if n >= 5 else 0


def base2(l, k=0):
    return B_L2 + l * PER_L2 + k


COLS = [("c", CH), ("norm_mix", 2 * CH), ("norm_ffn", 2 * CH), ("kv_norm", CH), ("final_norm", CH),
        ("gains2", LAYERS2 * 8 * CH), ("q_norm2", LAYERS2 * 2), ("kv_norm2", LAYERS2), ("group2", LAYERS2 * CH),
        ("conv_w", 4 * LCH), ("conv_b", LCH), ("b_gates", 2 * LCH), ("lambda", LCH), ("mod_b", MOD_GROUPS * 16),
        ("inv_mla", 1), ("inv_dil", 1), ("sign_mla", 1), ("sign_dil", 1)]
COL_AT = {}
_n = 0
for _name, _k in COLS:
    COL_AT[_name] = _n
    _n += _k
NCOLS = _n


def build(nc, stream, mods, x_t, cols_d, onehot, rb_t, masks, pos, p_t, out_t):
    scratch = nc.dram_tensor("bias_rows", (HEADS, P, 512), F32, kind="Internal").ap()
    with ExitStack() as ctx:
        def sb(name, shape, dt=F32):
            return ctx.enter_context(nc.sbuf_tensor(name, shape, dt))

        def sem(name):
            return ctx.enter_context(nc.semaphore(name))

        bank = [ctx.enter_context(nc.psum_tensor(f"bank{i}", [P, 512], F32)) for i in range(8)]

        raw = sb("raw", [P, RING, DINNER])
        w_hi = sb("w_hi", [P, RING, DINNER], F32R)
        w_lo = sb("w_lo", [P, RING, DINNER], F32R)
        x = sb("x", [P, CH, S])
        a_hi = sb("a_hi", [P, LCH, S], F32R)
        a_lo = sb("a_lo", [P, LCH, S], F32R)
        hid_hi = sb("hid_hi", [P, 2, 2, S], F32R)
        hid_lo = sb("hid_lo", [P, 2, 2, S], F32R)
        sq = sb("sq", [P, CH, S])
        rs0 = sb("rs0", [P, S])
        nwt = sb("nwt", [P, S])
        rstd = sb("rstd", [P, 2, S])
        ones = sb("ones", [P, P])
        ident = sb("ident", [P, P])
        cols = sb("cols", [P, NCOLS])
        modc = sb("modc", [P, MOD_GROUPS * 16])
        cs = sb("cs", [P, CH])
        scale1 = sb("scale1", [P, 5 * CH])
        half_g = sb("half_g", [P, LAYERS2 * 2 * CH])
        lam = sb("lam", [P, 8, LCH])
        shared = sb("shared", [P, 4 * 2048])
        mod_raw = shared[:, 0:4096].rearrange("p (r n) -> p r n", r=2)
        mod_acc = shared[:, 4096:8192].rearrange("p (r n) -> p r n", r=2)
        f = shared[:, 0:2048].rearrange("p (c s) -> p c s", c=CH)
        rope = shared[:, 2048:3072].rearrange("p (k s) -> p k s", k=4)
        mask = shared[:, 3072:3840].rearrange("p (k s) -> p k s", k=2)
        ptok = shared[:, 3840:4864].rearrange("p (l c s) -> p l c s", l=2, c=2)
        k_even = shared[:, 4864:5888].rearrange("p (h s) -> p h s", h=4)
        q_dil = shared[:, 6144:8192].rearrange("p (h s) -> p h s", h=HEADS)
        work = sb("work", [P, 10752])

        def area(at, *shape):
            n = int(np.prod(shape))
            v = work[:, at:at + n]
            if len(shape) == 2:
                v = v.rearrange("p (a b) -> p a b", a=shape[0])
            elif len(shape) == 3:
                v = v.rearrange("p (a b c) -> p a b c", a=shape[0], b=shape[1])
            return v

        y_br = area(0, LCH, S)
        xc = area(2560, LCH, S)
        r_g = area(5120, LCH, S)
        i_g = area(7680, LCH, S)
        mod_more = area(0, 2, 2048)
        mod_third = area(6400, 2048)
        rbb = area(5120, HEADS, P)
        bias_rows = area(6144, HEADS, 512)
        onehot_sb = area(10240, 512)
        gate_s = area(0, 2, 512)
        hid = area(1024, 2, 512)
        q_a = area(0, CH, S)
        k_a = area(2048, KVH, S)
        v_a = area(3072, 2, 512)
        bias = area(7168, HEADS, 384)
        k_dil = area(0, 4, S)
        swap = area(1024, 512)
        v_dil = area(2048, 2, 512)
        v_mla = area(3072, 2, 512)
        q_lat = area(6400, 2, S)
        kv_lat = area(6912, 1, S)
        kr = area(7168, S)
        q_mla = area(7424, HEADS, S)
        k_odd = area(9472, 4, S)
        rt_q = area(6400, 4, S)
        sc = area(4096, 2, 384)
        prob = area(4864, 2, 384)
        prob_t = area(5632, 2, 384)
        rt = area(4096, 4, S)
        pos_i = area(4096, S).bitcast(I32)
        pos_f = area(4352, S)
        ang = area(4608, S)
        turn = area(4864, 2, S)
        red = area(5376, 2, S)
        nmax = sb("nmax", [P, 2, 2])
        ssum = sb("ssum", [P, 2, 2])
        rsum = sb("rsum", [P, 2, 2])
        xp_all = sb("xp", [P, 4 * (S + 3)])
        xp = xp_all[:, :].rearrange("p (b c s) -> p b c s", b=2, c=2)
        rope_r = xp_all[:, 0:4 * S].rearrange("p (k s) -> p k s", k=4)
        rcol = sb("rcol", [P, 2])
        eps = sb("eps", [P, 1])
        warm = sb("warm", [P, 1])
        rb_sb = sb("rb_sb", [32, HEADS])

        def col(name, k):
            return cols[:, COL_AT[name] + k:COL_AT[name] + k + 1]

        def modcol(g, k):
            return modc[:, 16 * g + k:16 * g + k + 1]

        s_cols, s_x, s_rb, s_oh = sem("cols_landed"), sem("x_landed"), sem("rb_landed"), sem("onehot_landed")
        landed = [sem(f"slab_landed{r}") for r in range(RING)]
        mod_landed = [sem(f"mod_landed{r}") for r in range(2 * MOD_RING + len(MOD_AHEAD))]
        s_late = sem("late_landed")
        s_rows = sem("bias_rows_stored")
        s_bias = sem("bias_landed")
        s_out = sem("out_stored")
        hi_ready, lo_ready, slab_done = sem("hi_ready"), sem("lo_ready"), sem("slab_done")
        bank_done = sem("bank_done")
        sq_ready, stat_ready, rs0_ready = sem("sq_ready"), sem("stat_ready"), sem("rs0_ready")
        sum_step, sum_ready = sem("sum_step"), sem("squares_summed")
        newton, rstd_ready = sem("newton"), sem("rstd_ready")
        nt_ready, nh_ready, nl_ready = sem("normed_ready"), sem("normed_hi_ready"), sem("normed_lo_ready")
        x_ready, f_ready, f_scaled = sem("x_ready"), sem("f_ready"), sem("f_scaled")
        silu_done, hid_done, hh_ready, hl_ready = sem("silu_done"), sem("hid_done"), sem("hid_hi_ready"), sem("hid_lo_ready")
        const_ready = sem("const_ready")
        ident0 = sem("ident_zeroed")
        rbb_ready = sem("rbb_ready")
        row_mm, row_ev = sem("bias_row_made"), sem("bias_row_copied")
        cs_ready = sem("cs_ready")
        mod_step, mod_red, modc_ready = sem("mod_step"), sem("mod_reduced"), sem("modc_ready")
        acc_zero = sem("acc_zero")

        mod_slots = [v[:, r, h * MOD_HALF:(h + 1) * MOD_HALF] for v in (mod_raw, mod_more) for r in range(2) for h in range(2)]
        mod_slots += [sq[:, 4:8, :].rearrange("p c s -> p (c s)"), xp_all[:, 0:MOD_HALF]]

        def mod_slot(u):
            n = MOD_RING
            if u in MOD_AHEAD:
                return 2 * n + MOD_AHEAD.index(u), 1
            return (u % (2 * n), u // (2 * n) + 1) if u < 4 * n else (u % n, u // n - 1 - sum(v < u and v % n == u % n for v in MOD_AHEAD))

        def slot_user(u):
            v = u - MOD_RING
            while v in MOD_AHEAD:
                v -= MOD_RING
            return v

        def mod_sums(g):
            return mod_third if g == G_A1 else mod_acc[:, g % 2, :]


        scale_ready = sem("scale_ready")
        half_ready = sem("half_ready")
        lam_act, lam_dve = sem("lambda_act"), sem("lambda_dve")
        pad_zero = sem("pad_zero")
        xbr_ready, conv_step, conv_done, y_ready = sem("xbr_copied"), sem("conv_step"), sem("conv_done"), sem("gelu_ready")
        xch_ready, xcl_ready = sem("conv_hi_ready"), sem("conv_lo_ready")
        gate_done, gates_ready = sem("gates_made"), sem("gates_ready")
        bi_ready, decay_ready = sem("gated_input_ready"), sem("decay_ready")
        mult2_step, mult2_ready, mult_ready = sem("mult2_step"), sem("mult2_ready"), sem("mult_ready")
        scan_step, z_ready, zh_ready, zl_ready = sem("scan_step"), sem("z_ready"), sem("z_hi_ready"), sem("z_lo_ready")
        qkv_act, qkv_dve, rope_step = sem("qkv_copied_act"), sem("qkv_copied_dve"), sem("rope_step")
        qk_done, sc_done, exp_done, rs_done, pn_done = sem("qk_done"), sem("scores_done"), sem("exp_done"), sem("rsum_done"), sem("probs_done")
        tr_done, pt_done, pv_done, o_done, oh_done = sem("probs_turned"), sem("probs_t_done"), sem("pv_done"), sem("o_done"), sem("o_hi_done")
        rows_zero, swap_ready = sem("rows_zeroed"), sem("halves_exchanged")
        up_done = sem("latent_up_done")
        trig_step, trig_act, rope_ready = sem("trig_step"), sem("trig_act"), sem("rope_ready")
        ph_ready, pl_ready = sem("p_hi_ready"), sem("p_lo_ready")
        pg_scaled, pg_ready = sem("ple_gate_scaled"), sem("ple_gate_ready")
        k_roped, q_roped = sem("keys_roped"), sem("queries_roped")
        kv_used = sem("kv_input_used")
        gate_scaled, up_scaled = sem("gate_scaled"), sem("up_scaled")
        table_ready, rturn_done, rcol_ready = sem("rope_over_rms_ready"), sem("rms_turned"), sem("rms_column_ready")
        eps_ready, warmed = sem("eps_ready"), sem("table_warmed")

        block = ctx.enter_context(nc.Block())

        U_LRU, U_FFN0, U_MOBA, U_FFN1, U_FIN = range(5)

        def u2(l, k):
            return 5 + 4 * l + k

        U_LAST = u2(LAYERS2 - 1, 3)

        @block.sync
        def _(sp):
            sp.dma_start(cols[:, :], cols_d).then_inc(s_cols, 16)
            sp.dma_start(x[:, :, :], x_t.rearrange("(c p) s -> p c s", p=P)).then_inc(s_x, 16)
            sp.wait_ge(mod_step, 9)
            for s in range(RING):
                sp.dma_start(raw[:, s, :], stream[s]).then_inc(landed[s], 16)
            with sp.Fori(1, SLABS // RING) as i:
                for r in range(RING):
                    src = stream[bass.ds(i * RING + r, 1)].rearrange("a p n -> p (a n)")
                    split = sp.snap(i * RING + (r - RING + 1))
                    sp.wait_ge(lo_ready, split)
                    sp.dma_start(raw[:, r, :], src).then_inc(landed[r], 16)
            for s in range(SLABS // RING * RING, SLABS):
                sp.wait_ge(lo_ready, s - RING + 1)
                sp.dma_start(raw[:, s % RING, :], stream[s]).then_inc(landed[s % RING], 16)
            for c in range(CH):
                sp.wait_ge(x_ready, CH * U_LAST + c + 1)
                sp.dma_start(out_t[c * P:(c + 1) * P, :], x[:, c, :]).then_inc(s_out, 16)
            sp.wait_ge(s_out, 16 * CH)

        @block.gpsimd
        def _(pool):
            def mod_half(u):
                return mods[u // 2][:, u % 2 * MOD_HALF:(u % 2 + 1) * MOD_HALF]

            pool.dma_start(rb_sb[:, :], rb_t).then_inc(s_rb, 16)
            pool.dma_start(onehot_sb[0:33, :], onehot).then_inc(s_oh, 16)
            for u in range(2 * MOD_RING):
                pool.dma_start(mod_slots[u], mod_half(u)).then_inc(mod_landed[u], 16)
            nc.gpsimd.memset(eps[:, :], EPS).then_inc(eps_ready, 1)
            nc.gpsimd.memset(ident[:, :], 0.0).then_inc(ident0, 1)
            pool.wait_ge(ident0, 1)
            nc.gpsimd.affine_select(out=ident[:, :], in_=ident[:, :], compare_op=ALU.not_equal, fill=1.0, base=0,
                                    pattern=[[-1, P]], channel_multiplier=1)
            nc.gpsimd.memset(ones[:, :], 1.0).then_inc(const_ready, 1)
            for u in range(2 * MOD_RING, 5 * MOD_RING):
                slot, _ = mod_slot(u)
                pool.wait_ge(mod_step, u - 2 * MOD_RING + 1)
                pool.dma_start(mod_slots[slot], mod_half(u)).then_inc(mod_landed[slot], 16)
            def mod_loads(lo, hi):
                with pool.Fori(lo // MOD_RING, hi // MOD_RING) as i:
                    for r in range(MOD_RING):
                        src = mods[bass.ds(i * 2 + r // 2, 1)].rearrange("a p n -> p (a n)")[:, r % 2 * MOD_HALF:(r % 2 + 1) * MOD_HALF]
                        used = pool.snap(i * MOD_RING + (r - MOD_RING + 1))
                        pool.wait_ge(mod_step, used)
                        pool.dma_start(mod_slots[r], src).then_inc(mod_landed[r], 16)

            def mod_load(*halves):
                for u in halves:
                    slot, _ = mod_slot(u)
                    if u not in MOD_AHEAD:
                        pool.wait_ge(mod_step, slot_user(u) + 1)
                    pool.dma_start(mod_slots[slot], mod_half(u)).then_inc(mod_landed[slot], 16)

            def low(s):
                pool.wait_ge(lo_ready, s)
                pool.wait_ge(hi_ready, s + 1)
                nc.gpsimd.tensor_tensor(out=w_lo[:, s % RING, :], in0=raw[:, s % RING, :], in1=w_hi[:, s % RING, :].bitcast(F32),
                                        op=ALU.subtract).then_inc(lo_ready, 1)

            added = [0]

            def sum_squares(n):
                for c in range(2, summed(n), 2):
                    if c > 2:
                        pool.wait_ge(sum_step, added[0])
                    pool.wait_ge(sq_ready, before(NORM_CHUNKS, n) + c + 2)
                    ins = nc.gpsimd.tensor_tensor(out=sq[:, 0:2, :], in0=sq[:, 0:2, :], in1=sq[:, c:c + 2, :], op=ALU.add)
                    if c + 2 < summed(n):
                        ins.then_inc(sum_step, 1)
                        added[0] += 1
                ins.then_inc(sum_ready, 1)

            mod_loads(5 * MOD_RING, 8 * MOD_RING)
            mod_load(32, 33)
            pool.wait_ge(conv_done, 5)
            mod_load(*MOD_AHEAD)
            low(POOL_LOW[0])
            mod_load(38, 39)
            low(POOL_LOW[1])
            mod_load(36, 37, 40, 41)
            low(POOL_LOW[2])
            mod_load(*range(42, 48))
            sum_squares(N_FFN0)
            mod_load(*range(48, 56))
            for g in (G_KV, G_MIX1):
                pool.wait_ge(mod_red, g - 1)
                nc.gpsimd.memset(mod_sums(g), 0.0).then_inc(acc_zero, 1)
            mod_loads(16 * G_KV + 2 * MOD_RING, 16 * G_B1 + MOD_RING)
            sum_squares(N_KV)
            mod_loads(16 * G_B1 + MOD_RING, 16 * MOD_GROUPS)
            def fill_for_block_two():
                pool.wait_ge(mod_red, MOD_GROUPS)
                pool.dma_start(mask, masks.rearrange("k p s -> p k s")).then_inc(s_late, 16)
                pool.dma_start(ptok, p_t.rearrange("l (c p) s -> p l c s", p=P)).then_inc(s_late, 16)
                pool.wait_ge(o_done, HEADS)
                pool.dma_start(pos_i, pos).then_inc(s_late, 16)
                for zeroed in (k_even, k_odd, q_dil, q_mla):
                    nc.gpsimd.memset(zeroed, 0.0).then_inc(rows_zero, 1)

            for n in SUMMED[2:]:
                sum_squares(n)
                if n == N_FFN1:
                    fill_for_block_two()
                for l in range(LAYERS2):
                    if n == norm2(l, L_PREMIX):
                        pool.wait_ge(rope_step, ROPE_STEPS * l + KEY_STEPS)
                        pool.wait_ge(rows_zero, 4)
                        for h in range(4):
                            r = slice(32 * rope_slot(h), 32 * rope_slot(h) + 32)
                            ins = nc.gpsimd.tensor_tensor(out=(k_odd if h % 2 else k_even)[r, h // 2::2, :], in0=kr[r, :].unsqueeze(1).to_broadcast([32, 2, S]),
                                                          in1=rt_q[r, 0:1, :].to_broadcast([32, 2, S]), op=ALU.add)
                        ins.then_inc(k_roped, 1)
                        pool.wait_ge(rope_step, ROPE_STEPS * (l + 1))
                        for h in range(4):
                            r = slice(32 * rope_slot(h), 32 * rope_slot(h) + 32)
                            ins = nc.gpsimd.tensor_tensor(out=q_mla[r, h::4, :], in0=rt_q[r, 0:2, :], in1=rt_q[r, 2:4, :], op=ALU.add)
                        ins.then_inc(q_roped, 1)

        @block.tensor
        def _(pe):
            def product(out, w_h, w_l, v_h, v_l, start, stop):
                pe.matmul(out, w_h, v_h, start=start, stop=False, skip_group_check=True)
                pe.matmul(out, w_h, v_l, start=False, stop=False, skip_group_check=True)
                return pe.matmul(out, w_l, v_h, start=False, stop=stop, skip_group_check=True)

            def weights(s, lo, n):
                return w_hi[:, s % RING, lo:lo + n], w_lo[:, s % RING, lo:lo + n]

            def need_slab(s):
                pe.wait_ge(lo_ready, s + 1)

            def feature_slab(slot, out, chunk_ready=None, m_chunks=2, width=256):
                for c in range(CH):
                    if chunk_ready is not None:
                        pe.wait_ge(nl_ready, chunk_ready + c + 1)
                    for m in range(m_chunks):
                        mm = product(out[:, m * S:(m + 1) * S], *weights(slot, c * width + m * P, P), a_hi[:, c, :], a_lo[:, c, :],
                                     start=(c == 0 and m == 0), stop=(c == CH - 1))
                return mm

            def token_slab(slot, out, used=None):
                for c in range(CH):
                    for t in range(2):
                        wh, wl = weights(slot, c * 256, 256)
                        o = out[:, t * 256:(t + 1) * 256]
                        lh, ll = a_hi[:, c, t * P:(t + 1) * P], a_lo[:, c, t * P:(t + 1) * P]
                        pe.matmul(o, lh, wh, start=(c == 0 and t == 0), stop=False, skip_group_check=True)
                        pe.matmul(o, ll, wh, start=False, stop=False, skip_group_check=True)
                        mm = pe.matmul(o, lh, wl, start=False, stop=(c == CH - 1), skip_group_check=True)
                    if used is not None and c < CH - 1:
                        mm.then_inc(used, 1)
                return mm

            def sums_slab(slot, v_h, v_l, first, last, chunks=range(CH)):
                def one(k, m):
                    return product(bank[4 + m // 2][:, (m % 2) * S:(m % 2 + 1) * S], *weights(slot, k * D + m * P, P),
                                   v_h[:, k, :], v_l[:, k, :], start=(first and k == 0 and m % 2 == 0), stop=(last and k == 1))
                if not last:
                    for k in range(2):
                        for m in chunks:
                            mm = one(k, m)
                    return mm
                for m in range(CH):
                    for k in range(2):
                        mm = one(k, m)
                    if m in (1, 3, 5):
                        mm.then_inc(bank_done, 1)
                return mm

            def norm_stat(n):
                at, total = norm_at(n), NORM_CHUNKS[n]
                done = before(NORM_CHUNKS, n)
                chunks = list(range(total))
                if summed(n):
                    pe.wait_ge(sum_ready, SUMMED.index(n) + 1)
                    chunks = [0, 1] + chunks[summed(n):]
                for c in chunks:
                    if not summed(n) or c > 1:
                        pe.wait_ge(sq_ready, done + c + 1)
                    mm = pe.matmul(bank[stat_bank(n)][:, 0:S], ones[:, :], sq[:, at + c, :], start=(c == 0), stop=(c == chunks[-1]))
                mm.then_inc(stat_ready, 1)

            def keep_warm(n, b=1):
                for _ in range(n):
                    pe.matmul(bank[b][:, 0:P], ones[:, :], ident[:, :], start=True, stop=True)

            def norm_between(n, first=WARM_BEFORE, then=WARM_AFTER):
                keep_warm(first)
                norm_stat(n)
                keep_warm(then)

            def slab_pair(slots, outs, chunk_ready):
                for c in range(CH):
                    pe.wait_ge(nl_ready, chunk_ready + c + 1)
                    for slot, out in zip(slots, outs):
                        for m in range(2):
                            mm = product(out[:, m * S:(m + 1) * S], *weights(slot, c * 256 + m * P, P), a_hi[:, c, :], a_lo[:, c, :],
                                         start=(c == 0 and m == 0), stop=(c == CH - 1))
                        if c == CH - 1:
                            mm.then_inc(slab_done, 1)

            def mod_reduce(g, b):
                pe.wait_ge(mod_step, MOD_LAST[g])
                for m in range(16):
                    n = min(P, 512 - m * 32)
                    mm = pe.matmul(bank[b][:, m * 32:m * 32 + n], mod_sums(g)[:, m * P:(m + 1) * P], ones[:, 0:n],
                                   start=True, stop=True)
                mm.then_inc(mod_red, 1)

            def ffn(i, b, ap, stat=None):
                f0 = FJ * i

                def group(j, ready, slot, chunk_ready=None, j_par=None):
                    par = j_par
                    for k, out in enumerate((bank[par], bank[2 + par])):
                        pe.wait_ge(lo_ready, ready + k)
                        if j is not None:
                            pe.wait_ge(hid_done, j + (f0 - 1))
                        feature_slab(slot + k, out, chunk_ready if k == 0 else None).then_inc(slab_done, 1)

                def down(j, ready, slot, par, first=False, last=False):
                    pe.wait_ge(lo_ready, ready)
                    pe.wait_ge(hl_ready, j + (f0 + 1))
                    sums_slab(slot, hid_hi[:, par], hid_lo[:, par], first, last).then_inc(slab_done, 1)

                pe.wait_ge(lo_ready, b + 2)
                slab_pair((b, b + 1), (bank[0], bank[2]), before(APPLY_CHUNKS, ap))
                if stat is not None:
                    norm_stat(stat)
                group(None, b + 3, b + 2, None, 1)
                down(0, b + 5, b + 4, 0, first=True)
                with pe.Fori(0, (FJ - 3) // 2) as k:
                    for h in range(2):
                        group(2 * k + (2 + h), 6 * k + (b + 6 + 3 * h), b + 5 + 3 * h, None, h)
                        down(2 * k + (1 + h), 6 * k + (b + 8 + 3 * h), b + 7 + 3 * h, (1 + h) % 2)
                j = FJ - 1
                group(j, b + 3 * j, b + 3 * j - 1, None, j % 2)
                down(j - 1, b + 3 * j + 2, b + 3 * j + 1, (j - 1) % 2)
                down(j, b + 3 * j + 3, b + 3 * j + 2, j % 2, last=True)

            def attention(heads, qk, pv, at={}):
                n = len(heads)

                def score(k):
                    if k >= 2:
                        pe.wait_ge(sc_done, heads[k] - 1)
                    for t in range(2):
                        out = bank[k % 2][:, 0:P] if t == 0 else bank[k % 2][:, P:384]
                        parts = qk(k, t)
                        for i, (lhs, rhs) in enumerate(parts):
                            mm = pe.matmul(out, lhs, rhs, start=(t == 0 and i == 0), stop=(i == len(parts) - 1), skip_group_check=True)
                    mm.then_inc(qk_done, 1)

                def turn(k):
                    pe.wait_ge(pn_done, heads[k] + 1)
                    if k >= 2:
                        pe.wait_ge(pt_done, heads[k] - 1)
                    pr = prob[:, heads[k] % 2]
                    for t in range(3):
                        mm = pe.transpose(bank[2 + k % 2][:, t * P:(t + 1) * P], pr[:, t * P:(t + 1) * P], ident[:, :])
                    mm.then_inc(tr_done, 1)

                def weigh(k):
                    pe.wait_ge(pt_done, heads[k] + 1)
                    lhs, out, gate = pv(k)
                    if gate is not None:
                        pe.wait_ge(o_done, gate)
                    pt = prob_t[:, heads[k] % 2]
                    pe.matmul(out[:, 0:256], lhs(0), pt[:, 0:256], start=True, stop=False, skip_group_check=True)
                    pe.matmul(out[:, 128:256], lhs(1), pt[:, 256:384], start=False, stop=True, skip_group_check=True).then_inc(pv_done, 1)

                for k in range(-3, n + 1):
                    if k in at:
                        at[k]()
                    if 0 <= k < n:
                        turn(k)
                    if k >= 1:
                        weigh(k - 1)
                    if k + 3 < n:
                        score(k + 3)

            pe.wait_ge(const_ready, 1)
            pe.wait_ge(rbb_ready, 2)
            pe.wait_ge(s_oh, 16)
            for h in range(HEADS):
                if h >= 2:
                    pe.wait_ge(row_ev, h - 1)
                pe.matmul(bank[h % 2][:, :], rbb[0:33, h, :], onehot_sb[0:33, :], start=True, stop=True).then_inc(row_mm, 1)
            norm_stat(N_MIX0)
            pe.wait_ge(row_ev, HEADS)
            pe.wait_ge(mod_step, 14)
            keep_warm(8)
            mod_reduce(G_MIX0, 7)

            need_slab(B_WIN)
            keep_warm(9)
            need_slab(B_WIN + 1)
            slab_pair((B_WIN, B_WIN + 1), (bank[0], bank[1]), before(APPLY_CHUNKS, A_MIX0))
            for i in range(2, 10):
                s = B_WIN + i
                need_slab(s)
                if 4 <= i < 9:
                    pe.wait_ge(xbr_ready, i - 3)
                if i == 9:
                    pe.wait_ge(y_ready, 1)
                feature_slab(s, bank[i % 4]).then_inc(slab_done, 1)
            keep_warm(14, 5)
            for hd in range(LHEADS):
                s = B_GATE + hd // 2
                if hd % 2 == 0:
                    need_slab(s)
                pe.wait_ge(xcl_ready, hd + 1)
                for k in range(2):
                    b = (2 * hd + k) % 4
                    if hd >= 2:
                        pe.wait_ge(gates_ready, 2 * (hd - 2) + k + 1)
                    for c in range(2):
                        for m in range(2):
                            mm = product(bank[b][:, m * S:(m + 1) * S], *weights(s, (hd % 2) * 1024 + c * 512 + k * 256 + m * P, P),
                                         a_hi[:, 2 * hd + c, :], a_lo[:, 2 * hd + c, :], start=(c == 0 and m == 0), stop=(c == 1))
                    mm.then_inc(slab_done if k == 1 and hd in GATE_ENDS else gate_done, 1)
            pe.wait_ge(gates_ready, 2 * LHEADS)
            pe.wait_ge(decay_ready, 3)
            keep_warm(16)
            mod_reduce(G_A0, 2)
            keep_warm(12)
            for i in range(LHEADS):
                need_slab(B_LOUT + i)
                pe.wait_ge(zl_ready, i + 1)
                sums_slab(B_LOUT + i, a_hi[:, 2 * i:2 * i + 2], a_lo[:, 2 * i:2 * i + 2], i == 0, i == LHEADS - 1).then_inc(slab_done, 1)
            pe.wait_ge(sq_ready, before(NORM_CHUNKS, N_FFN0) + 2)
            keep_warm(8)
            norm_stat(N_FFN0)
            mod_reduce(G_B0, 3)
            keep_warm(8)
            ffn(0, B_FFN0, A_FFN0)

            mod_reduce(G_KV, 1)
            keep_warm(6, 2)
            norm_stat(N_KV)
            mod_reduce(G_MIX1, 3)
            need_slab(B_KV + 1)
            slab_pair((B_KV, B_KV + 1), (bank[0], bank[1]), before(APPLY_CHUNKS, A_KV))
            for i in range(2, 4):
                need_slab(B_KV + i)
                if i == 3:
                    pe.wait_ge(modc_ready, G_MIX1 + 1)
                token_slab(B_KV + i, bank[i], kv_used if i == 3 else None).then_inc(slab_done, 1)

            def queries(i):
                need_slab(B_Q + i)
                pe.wait_ge(qkv_act, i + 1)
                feature_slab(B_Q + i, bank[i], before(APPLY_CHUNKS, A_MIX1) if i == 0 else None).then_inc(slab_done, 1)

            mod_reduce(G_A1, 4)
            for i in range(3):
                queries(i)
            pe.wait_ge(qkv_act, 6)
            pe.wait_ge(modc_ready, G_A1 + 1)

            def out_slab(i, chunks=range(CH)):
                need_slab(B_O + i)
                pe.wait_ge(o_done, 2 * i + 2)
                return sums_slab(B_O + i, a_hi[:, 2 * i:2 * i + 2], a_lo[:, 2 * i:2 * i + 2], i == 0, i == 3, chunks)

            attention(list(range(HEADS)),
                      lambda k, t: [(q_a[:, k, t * P:(t + 1) * P], k_a[:, k // 2, 0:P * (t + 1)])],
                      lambda k: (lambda kt: v_a[:, kt, (k // 2) * P:(k // 2 + 1) * P], bank[4 + k % 2][:, 0:256], k - 1 if k >= 2 else None),
                      {-1: lambda: queries(3), 0: lambda: pe.wait_ge(qkv_act, 8), HEADS: lambda: out_slab(0, range(4, CH))})
            pe.wait_ge(o_done, HEADS - 1)
            out_slab(0, range(2))
            pe.wait_ge(o_done, HEADS)
            out_slab(0, range(2, 4)).then_inc(slab_done, 1)
            for i in range(1, 4):
                out_slab(i).then_inc(slab_done, 1)
            mod_reduce(G_B1, 0)
            norm_between(N_FFN1, 2)
            ffn(1, B_FFN1, A_FFN1)
            norm_between(N_FIN, 14)

            for l in range(LAYERS2):
                ffn(2 + 2 * l, base2(l), apply2(l, LA_PRE1), norm2(l, L_PRE1))
                norm_between(norm2(l, L_POST1))
                b = base2(l, M_MIX)
                d0, c0 = 6 * l, 8 + 8 * l
                need_slab(b + 1)
                slab_pair((b, b + 1), (bank[0], bank[1]), before(APPLY_CHUNKS, apply2(l, LA_PREMIX)))
                norm_stat(norm2(l, L_PREMIX))
                for i in range(2, 8):
                    need_slab(b + i)
                    if i in (4, 5, 6, 7):
                        pe.wait_ge(qkv_dve, d0 + i - 3)
                    if i < 6:
                        mm = feature_slab(b + i, bank[i % 4])
                    else:
                        mm = token_slab(b + i, bank[i % 4])
                    mm.then_inc(slab_done, 1)
                    if i == 3:
                        pe.wait_ge(rstd_ready, norm2(l, L_PREMIX) + 1)
                        for t in range(2):
                            mm = pe.transpose(bank[5][:, t * P:(t + 1) * P], rstd[:, norm2(l, L_PREMIX) % 2, t * P:(t + 1) * P], ident[:, :])
                        mm.then_inc(rturn_done, 1)
                    if i == 4:
                        norm_stat(norm2(l, L_QLAT))
                    if i == 5:
                        norm_stat(norm2(l, L_KVLAT))
                sC, sQ = b + 8, b + 9
                need_slab(sC)
                pe.wait_ge(qkv_dve, d0 + 5)
                feature_slab(sC, bank[0], None, 1, P).then_inc(up_done, 1)
                at = before(APPLY_CHUNKS, apply2(l, LA_KVLAT))
                pe.wait_ge(nl_ready, at + 1)
                pe.wait_ge(qkv_dve, d0 + 6)
                lat_h, lat_l = hid_hi[:, 0, 0, :], hid_lo[:, 0, 0, :]
                for k in range(2):
                    if k == 1:
                        pe.wait_ge(qkv_act, c0 + 1)
                    for m in range(2):
                        mm = product(bank[1 + k][:, m * S:(m + 1) * S], *weights(sC, 1024 + (2 * k + m) * P, P), lat_h, lat_l,
                                     start=(m == 0), stop=True)
                    mm.then_inc(up_done, 1)
                for t in range(2):
                    wh, wl = weights(sC, 1024 + 512, 512)
                    tk = slice(t * P, (t + 1) * P)
                    mm = product(bank[4 + t][:, :], lat_h[:, tk], lat_l[:, tk], wh, wl, start=True, stop=True)
                    if t == 0:
                        mm.then_inc(up_done, 1)
                mm.then_inc(slab_done, 1)

                def queries():
                    need_slab(sQ)
                    pe.wait_ge(nl_ready, before(APPLY_CHUNKS, apply2(l, LA_QLAT)) + 2)
                    for k, out in enumerate((bank[3], bank[2], bank[6], bank[7])):
                        if k == 0:
                            pe.wait_ge(qkv_act, c0 + 4)
                        for c in range(2):
                            for m in range(2):
                                mm = product(out[:, m * S:(m + 1) * S], *weights(sQ, c * 1024 + (2 * k + m) * P, P),
                                             a_hi[:, 8 + c, :], a_lo[:, 8 + c, :], start=(c == 0 and m == 0), stop=(c == 1))
                        if k < 2:
                            mm.then_inc(up_done, 1)
                    mm.then_inc(slab_done, 1)

                def copied():
                    pe.wait_ge(qkv_act, c0 + 8)

                def mla_ready():
                    pe.wait_ge(q_roped, l + 1)

                pe.wait_ge(qkv_dve, d0 + 6)
                pe.wait_ge(rope_step, ROPE_STEPS * l + KEY_STEPS)
                pe.wait_ge(qkv_act, c0 + 3)

                def qk(k, t):
                    tk, keys = slice(t * P, (t + 1) * P), slice(0, P * (t + 1))
                    h = k % HEADS
                    if k < HEADS:
                        return [(q_dil[:, h, tk], k_dil[:, h // 2, keys])]
                    return [(q_mla[:, h, tk], (k_odd if h % 2 else k_even)[:, h // 2, keys])]

                def pv(k):
                    h = k % HEADS
                    v = v_dil if k < HEADS else v_mla
                    r = slice(64 * (h % 2), 64 * (h % 2) + 64)
                    gate = 8 + 8 * l + k // 2 - 1 if k >= 4 and k % 2 == 0 else None
                    return lambda kt: v[:, kt, h * 64:(h + 1) * 64], bank[4 + (k // 2) % 2][r, 0:256], gate

                def out_slab(i, chunks=range(CH)):
                    need_slab(base2(l, M_OUT) + i)
                    pe.wait_ge(nl_ready, before(APPLY_CHUNKS, apply2(l, LA_GDIL)) + 2 * i + 2)
                    g = OUT_ORDER[i]
                    return sums_slab(base2(l, M_OUT) + i, a_hi[:, 2 * g:2 * g + 2], a_lo[:, 2 * g:2 * g + 2], i == 0, i == 3, chunks)

                attention([HEADS + 16 * l + k for k in range(16)], qk, pv,
                          {-1: queries, 0: copied, HEADS - 3: mla_ready, NORM_STEP: lambda: norm_stat(norm2(l, L_GDIL)),
                           16: lambda: out_slab(0, range(4, CH))})
                pe.wait_ge(o_done, 8 + 8 * l + 7)
                out_slab(0, range(2))
                pe.wait_ge(o_done, 8 + 8 * l + 8)
                out_slab(0, range(2, 4)).then_inc(slab_done, 1)
                norm_stat(norm2(l, L_GMLA))
                for i in range(1, 4):
                    out_slab(i).then_inc(slab_done, 1)
                norm_between(norm2(l, L_POSTMIX))
                ffn(3 + 2 * l, base2(l, M_FFN), apply2(l, LA_PRE2), norm2(l, L_PRE2))
                norm_between(norm2(l, L_POST2), WARM_BEFORE, 0)
                need_slab(base2(l, M_PLE))
                pe.wait_ge(pl_ready, l + 1)
                pe.wait_ge(f_ready, 4 * (4 * l + 2) + 4)
                for m in range(CH):
                    for k in range(2):
                        mm = product(bank[4 + m // 2][:, (m % 2) * S:(m % 2 + 1) * S], *weights(base2(l, M_PLE), k * D + m * P, P),
                                     hid_hi[:, 1, k, :], hid_lo[:, 1, k, :], start=(k == 0 and m % 2 == 0), stop=(k == 1))
                mm.then_inc(slab_done, 1)
                need_slab(base2(l, M_PGATE) + 1)
                slab_pair((base2(l, M_PGATE), base2(l, M_PGATE) + 1), (bank[0], bank[1]), before(APPLY_CHUNKS, apply2(l, LA_PREPLE)))
                norm_stat(norm2(l, L_PREPLE))
                for i in (2, 3):
                    need_slab(base2(l, M_PGATE) + i)
                    if i == 3:
                        pe.wait_ge(rstd_ready, norm2(l, L_PREPLE) + 1)
                    feature_slab(base2(l, M_PGATE) + i, bank[i]).then_inc(slab_done, 1)
                pe.wait_ge(pg_scaled, 4 * l + 2)
                norm_between(norm2(l, L_POSTPLE), WARM_BEFORE + 6, WARM_AFTER if l + 1 < LAYERS2 else 0)

        @block.scalar
        def _(act):
            made = [0]

            def split_to(n):
                for s in range(made[0], min(n, SLABS)):
                    act.wait_ge(landed[s % RING], 16 * (s // RING + 1))
                    if s >= RING:
                        act.wait_ge(slab_done, s - RING + 1)
                    act.copy(w_hi[:, s % RING, :], raw[:, s % RING, :]).then_inc(hi_ready, 1)
                made[0] = max(made[0], min(n, SLABS))

            def squares(n, src, ready):
                for c in range(NORM_CHUNKS[n]):
                    ready(c)
                    act.activation(sq[:, norm_at(n) + c, :], src(c), ACT.Square).then_inc(sq_ready, 1)

            def rsqrt(n, features):
                act.wait_ge(stat_ready, n + 1)
                if n:
                    act.wait_ge(rstd_ready, n)
                act.activation(rs0[:, :], bank[stat_bank(n)][:, 0:S], ACT.Abs_reciprocal_sqrt, scale=1.0 / features,
                               bias=eps[:, :]).then_inc(rs0_ready, 1)

            def warm_up():
                act.activation(warm[:, :], eps[:, :], ACT.Abs_reciprocal_sqrt)

            def deferred_hi(u, gain):
                for c in range(CH):
                    act.wait_ge(x_ready, CH * u + c + 1)
                    act.activation(a_hi[:, c, :], x[:, c, :], ACT.Copy, scale=gain(c)).then_inc(nh_ready, 1)
                    if c % 2:
                        act.activation(sq[:, c - 1:c + 1, :], x[:, c - 1:c + 1, :], ACT.Square).then_inc(sq_ready, 2)

            def gain2(l, k):
                return lambda c: col("gains2", 64 * l + CH * k + c)

            def normed_hi(ap, out, shift=None, free=None, at=0, chunks=None):
                for c in chunks or range(APPLY_CHUNKS[ap]):
                    if free is not None:
                        act.wait_ge(*free(c))
                    act.wait_ge(nt_ready, before(TURNED_CHUNKS, ap) + c + 1)
                    if shift is None:
                        ins = act.copy(out(c), sq[:, at + c, :])
                    else:
                        ins = act.activation(out(c), sq[:, c, :], ACT.Identity, bias=shift(c))
                    ins.then_inc(nh_ready, 1)

            def residual(u):
                return lambda c: act.wait_ge(x_ready, CH * u + c + 1)

            def x_norm(n, u):
                warm_up()
                squares(n, lambda c: x[:, c, :], residual(u))
                rsqrt(n, D)

            def a_out(c):
                return a_hi[:, c, :]

            def ffn(i, b):
                f0 = FJ * i

                def silu(j, par, done):
                    if i >= 2:
                        act.wait_ge(gate_scaled, (j if j is not None else par) + (FJ * (i - 2) + 1))
                        act.activation(gate_s[:, par, :], gate_s[:, par, :], ACT.Silu).then_inc(silu_done, 1)
                        return
                    act.wait_ge(slab_done, done)
                    if j is not None:
                        act.wait_ge(hid_done, j + (f0 - 1))
                    act.activation(gate_s[:, par, :], bank[par][:, :], ACT.Silu).then_inc(silu_done, 1)

                def hidden_hi(j, par, done):
                    act.wait_ge(hid_done, j + (f0 + 1))
                    if done is not None:
                        act.wait_ge(slab_done, done)
                    act.copy(hid_hi[:, par].rearrange("p c s -> p (c s)"), hid[:, par, :]).then_inc(hh_ready, 1)

                def high(count, land, slot):
                    act.wait_ge(landed[slot], land)
                    act.wait_ge(slab_done, count)
                    act.copy(w_hi[:, slot, :], raw[:, slot, :]).then_inc(hi_ready, 1)

                def sine(k):
                    if i == 1:
                        act.wait_ge(trig_step, TRIG_AT[k])
                        act.activation(rope[:, k, :], red[:, k % 2, :], ACT.Sin).then_inc(trig_act, 1)

                silu(None, 0, b + 1)
                split_to(b + 5)
                hidden_hi(0, 0, None)
                sine(0)
                silu(None, 1, b + 3)
                split_to(b + 7)
                sine(1)
                hidden_hi(1, 1, None)
                split_to(b + 8)
                sine(2)
                sine(3)
                with act.Fori(0, (FJ - 3) // 2) as k:
                    for h in range(2):
                        g = b + 5 + 3 * h
                        silu(2 * k + (2 + h), h, 6 * k + (g + 1))
                        for d in (0, 1):
                            high(6 * k + (g + d + 1), 32 * k + 16 * ((g + d + 3) // RING + 1), (g + d) % RING)
                        hidden_hi(2 * k + (2 + h), h, 6 * k + (b + 5 + 3 * h))
                        high(6 * k + (g + 3), 32 * k + 16 * ((g + 5) // RING + 1), (g + 2) % RING)
                made[0] = b + 3 * (FJ - 2) + 5
                j = FJ - 1
                silu(j, j % 2, b + 3 * j)
                split_to(b + 3 * j + 4)
                hidden_hi(j, j % 2, b + 3 * j - 1)
                split_to(b + 3 * j + 5)

            act.wait_ge(s_cols, 16)
            act.activation(cs[:, :], cols[:, COL_AT["c"]:COL_AT["c"] + CH], ACT.Silu).then_inc(cs_ready, 1)
            lam_c = cols[:, COL_AT["lambda"]:COL_AT["lambda"] + LCH]
            act.activation(lam[:, 0, :], lam_c, ACT.Abs).then_inc(lam_act, 1)
            act.wait_ge(lam_act, 1)
            act.activation(lam[:, 1, :], lam[:, 0, :], ACT.Exp, scale=-1.0).then_inc(lam_act, 1)
            act.wait_ge(eps_ready, 1)
            act.wait_ge(s_x, 16)
            squares(N_MIX0, lambda c: x[:, c, :], lambda c: None)
            for h in range(HEADS):
                act.wait_ge(row_mm, h + 1)
                act.copy(bias_rows[:, h, :], bank[h % 2][:, :]).then_inc(row_ev, 1)
            rsqrt(N_MIX0, D)
            split_to(RING)
            normed_hi(A_MIX0, a_out, lambda c: modcol(G_MIX0, c))

            for i in range(5):
                s = B_WIN + i
                act.wait_ge(slab_done, s + 1)
                if i == 0:
                    act.wait_ge(pad_zero, 1)
                if i == 2:
                    act.wait_ge(row_ev, HEADS)
                    act.dma_start(scratch.rearrange("h p s -> p h s"), bias_rows).then_inc(s_rows, 16)
                if i >= 2:
                    act.wait_ge(conv_done, i - 1)
                sums = bank[i % 4]
                act.copy(xp[:, i % 2, :, 3:S + 3], sums[:, :].rearrange("p (c s) -> p c s", c=2))
                for m in range(2):
                    c = 2 * i + m
                    ins = act.activation(xc[:, c, :], sums[:, m * S:(m + 1) * S], ACT.Identity,
                                         scale=col("conv_w", 3 * LCH + c), bias=col("conv_b", c))
                ins.then_inc(xbr_ready, 1)
                split_to(s + 4)
            for i in range(5):
                s = B_WIN + 5 + i
                act.wait_ge(slab_done, s + 1)
                act.activation(y_br[:, 2 * i:2 * i + 2, :].rearrange("p c s -> p (c s)"), bank[(5 + i) % 4][:, :],
                               ACT.Gelu_apprx_tanh).then_inc(y_ready, 1)
                split_to(s + 4)
            act.wait_ge(slab_done, B_GATE)
            for hd in range(LHEADS):
                act.wait_ge(conv_done, hd + 1)
                act.copy(a_hi[:, 2 * hd:2 * hd + 2, :], xc[:, 2 * hd:2 * hd + 2, :]).then_inc(xch_ready, 1)
            act.wait_ge(s_rows, 16)
            for hd in range(LHEADS):
                for k, dst in enumerate((r_g, i_g)):
                    if k == 1 and hd in GATE_ENDS:
                        act.wait_ge(slab_done, B_GATE + hd // 2 + 1)
                    else:
                        act.wait_ge(gate_done, 2 * hd + k + 1 - sum(h < hd for h in GATE_ENDS))
                    for m in range(2):
                        c = 2 * hd + m
                        ins = act.activation(dst[:, c, :], bank[(2 * hd + k) % 4][:, m * S:(m + 1) * S], ACT.Sigmoid,
                                             bias=col("b_gates", k * LCH + c))
                    ins.then_inc(gates_ready, 1)
                if hd in (2, 3):
                    split_to(B_LOUT + hd - 1)
            for hd in range(LHEADS):
                act.wait_ge(bi_ready, hd + 1)
                h2 = slice(2 * hd, 2 * hd + 2)
                act.activation(xc[:, h2, :], r_g[:, h2, :], ACT.Exp, scale=-1.0)
                act.activation(r_g[:, h2, :], r_g[:, h2, :], ACT.Tanh).then_inc(decay_ready, 1)
            for hd in range(LHEADS):
                act.wait_ge(mult2_ready, hd + 1)
                v = r_g[:, 2 * hd:2 * hd + 2, :]
                act.activation(v, v, ACT.Sqrt).then_inc(mult_ready, 1)
            split_to(B_LOUT + 3)
            for hd in range(LHEADS):
                act.wait_ge(z_ready, hd + 1)
                act.copy(a_hi[:, 2 * hd:2 * hd + 2, :], i_g[:, 2 * hd:2 * hd + 2, :]).then_inc(zh_ready, 1)
                if hd in (2, 3):
                    split_to(B_LOUT + hd + 2)
            split_to(B_FFN0 + 2)
            x_norm(N_FFN0, U_LRU)
            normed_hi(A_FFN0, a_out, lambda c: modcol(G_A0, CH + c))
            split_to(B_FFN0 + 3)
            ffn(0, B_FFN0)

            split_to(B_KV + 2)
            x_norm(N_KV, U_FFN0)
            normed_hi(A_KV, a_out, lambda c: modcol(G_KV, c))
            split_to(B_KV + 3)
            for i in range(4):
                act.wait_ge(slab_done, B_KV + i + 1)
                dst = k_a[:, 2 * i:2 * i + 2, :] if i < 2 else v_a[:, :, 256 * (i - 2):256 * (i - 1)]
                act.copy(dst, bank[i][:, :].rearrange("p (c s) -> p c s", c=2)).then_inc(qkv_act, 1)
                if i == 2:
                    normed_hi(A_MIX1, a_out, lambda c: modcol(G_MIX1, c), lambda c: (kv_used, c + 1) if c < CH - 1 else (slab_done, B_Q))
                split_to(B_KV + i + 4)
            act.wait_ge(mod_red, G_A1 + 1)
            for t, n in ((0, P), (1, 256)):
                skew = bass.AP(tensor=scratch.tensor, offset=255 - P * t, ap=[[511, P], [512 * P, HEADS], [1, n]])
                act.dma_start(bias[:, :, P * t:P * t + n], skew).then_inc(s_bias, 16)

            def queries(i):
                act.wait_ge(slab_done, B_Q + i + 1)
                act.activation(q_a[:, 2 * i:2 * i + 2, :], bank[i][:, :].rearrange("p (c s) -> p c s", c=2), ACT.Copy,
                               scale=P ** -0.5).then_inc(qkv_act, 1)
                split_to(B_Q + i + 4 if i < 3 else B_Q + 6)

            for i in range(3):
                queries(i)

            def attention(heads, copy_out=None, at={}):
                n = len(heads)

                def exps(k):
                    h = heads[k]
                    act.wait_ge(sc_done, h + 1)
                    if k >= 2:
                        act.wait_ge(tr_done, h - 1)
                    src, dst = sc, prob
                    for t, (lo, hi) in enumerate(((0, P), (P, 384))):
                        ins = act.activation(dst[:, h % 2, lo:hi], src[:, h % 2, lo:hi], ACT.Exp, scale=-1.0,
                                             bias=nmax[:, h % 2, t:t + 1], accum_out=ssum[:, h % 2, t:t + 1])
                    ins.then_inc(exp_done, 1)

                def turned(k):
                    h = heads[k]
                    act.wait_ge(tr_done, h + 1)
                    if k >= 2:
                        act.wait_ge(pv_done, h - 1)
                    act.copy(prob_t[:, h % 2, :], bank[2 + k % 2][:, 0:384]).then_inc(pt_done, 1)

                for k in range(-2, n + 1):
                    if k in at:
                        at[k]()
                    if 0 <= k < n:
                        turned(k)
                    if k + 2 < n:
                        exps(k + 2)
                    if copy_out is not None and k >= 1:
                        copy_out(k - 1)

            def moba_out(h):
                act.wait_ge(pv_done, h + 1)
                act.copy(a_hi[:, h, :], bank[4 + h % 2][:, 0:256]).then_inc(oh_done, 1)

            attention(list(range(HEADS)), moba_out, {0: lambda: queries(3)})
            split_to(B_FFN1 + 2)
            x_norm(N_FFN1, U_MOBA)
            normed_hi(A_FFN1, a_out, lambda c: modcol(G_A1, CH + c))
            split_to(B_FFN1 + 3)
            ffn(1, B_FFN1)
            split_to(B_L2 + 2)
            x_norm(N_FIN, U_FFN1)

            def post(l, k, n, phase=None, slab=None):
                warm_up()
                for b4 in range(4):
                    if k == 3:
                        act.wait_ge(f_ready, 4 * (4 * l + k) + b4 + 1)
                        src = f[:, 2 * b4:2 * b4 + 2, :]
                    else:
                        if b4 < 3:
                            act.wait_ge(bank_done, 3 * phase + b4 + 1)
                        else:
                            act.wait_ge(slab_done, slab + 1)
                        src = bank[4 + b4][:, :].rearrange("p (c s) -> p c s", c=2)
                    act.activation(sq[:, 2 * b4:2 * b4 + 2, :], src, ACT.Square).then_inc(sq_ready, 2)
                if k == 3:
                    split_to(base2(l + 1) + 2)
                rsqrt(n, D)

            for l in range(LAYERS2):
                deferred_hi(U_FIN if l == 0 else u2(l - 1, 3), gain2(l, 0))
                split_to(base2(l) + 4)
                rsqrt(norm2(l, L_PRE1), D)
                ffn(2 + 2 * l, base2(l))
                b = base2(l, M_MIX)
                split_to(b + 2)
                post(l, 0, norm2(l, L_POST1), 4 + 3 * l, b - 1)
                deferred_hi(u2(l, 0), gain2(l, 2))
                c0, d0 = 8 + 8 * l, 6 * l
                split_to(b + 4)
                rsqrt(norm2(l, L_PREMIX), D)

                def values(i):
                    for t in range(2):
                        ins = act.activation(v_dil[:, t, 256 * i:256 * (i + 1)], bank[2 + i][:, 256 * t:256 * (t + 1)], ACT.Copy,
                                             scale=rcol[:, t:t + 1])
                    ins.then_inc(qkv_act, 1)

                squares(norm2(l, L_QLAT), lambda c: q_lat[:, c, :], lambda c: act.wait_ge(qkv_dve, d0 + 1))
                split_to(b + 5)
                squares(norm2(l, L_KVLAT), lambda c: kv_lat[:, c, :], lambda c: act.wait_ge(qkv_dve, d0 + 2))
                for i in range(4):
                    act.wait_ge(slab_done, b + 3 + i)
                    if i:
                        act.wait_ge(qkv_dve, d0 + 2 + i)
                    for q in range(4):
                        ins = act.copy(swap[32 * (q ^ 1):32 * (q ^ 1) + 32, :], bank[(2 + i) % 4][32 * q:32 * q + 32, :])
                    ins.then_inc(swap_ready, 1)
                    split_to(b + 6 + i)
                    if i == 2:
                        rsqrt(norm2(l, L_QLAT), 256)
                        normed_hi(apply2(l, LA_QLAT), lambda c: a_hi[:, 8 + c, :])
                split_to(b + 10)
                rsqrt(norm2(l, L_KVLAT), P)
                normed_hi(apply2(l, LA_KVLAT), lambda c: hid_hi[:, 0, 0, :], at=2)
                act.wait_ge(rows_zero, 4)
                act.wait_ge(slab_done, b + 7)
                act.wait_ge(rcol_ready, l + 1)
                values(0)
                act.wait_ge(slab_done, b + 8)
                values(1)
                for k in range(2):
                    act.wait_ge(up_done, UP2 * l + 2 + k)
                    for r, dst in ((slice(0, 64), k_even), (slice(64, P), k_odd)):
                        ins = act.copy(dst[r, 2 * k:2 * k + 2, :], bank[1 + k][r, :].rearrange("p (c s) -> p c s", c=2))
                    ins.then_inc(qkv_act, 1)
                act.wait_ge(up_done, UP2 * l + 4)
                act.copy(v_mla[:, 0, :], bank[4][:, :]).then_inc(qkv_act, 1)
                act.wait_ge(slab_done, b + 9)
                act.copy(v_mla[:, 1, :], bank[5][:, :]).then_inc(qkv_act, 1)
                split_to(b + 11)

                def queries():
                    for k, src in enumerate((bank[3], bank[2])):
                        act.wait_ge(up_done, UP2 * l + 5 + k)
                        for m in range(2):
                            ins = act.activation(q_mla[64 * m:64 * m + 64, 4 * k + m:4 * k + 4:2, :],
                                                 src[64 * m:64 * m + 64, :].rearrange("p (c s) -> p c s", c=2), ACT.Copy, scale=96 ** -0.5)
                        ins.then_inc(qkv_act, 1)

                o0 = 8 + 8 * l

                def dilated_square(c):
                    act.wait_ge(o_done, o0 + c + 1)
                    act.activation(sq[:, 4 + c, :], f[:, 4 + c, :], ACT.Square).then_inc(sq_ready, 1)

                def dilated_hi(c):
                    normed_hi(apply2(l, LA_GDIL), lambda c: a_hi[:, 4 + c, :], at=4, chunks=[c])

                steps = {0: queries, NORM_STEP + 1: lambda: rsqrt(norm2(l, L_GDIL), 512)}
                steps.update({min(2 * c + 4, NORM_STEP - 1): lambda c=c: dilated_square(c) for c in range(4)})
                steps.update({NORM_STEP + 3 + c: lambda c=c: dilated_hi(c) for c in range(4)})
                attention([HEADS + 16 * l + k for k in range(16)], None, steps)
                warm_up()
                squares(norm2(l, L_GMLA), lambda c: f[:, c, :], lambda c: act.wait_ge(o_done, o0 + 5 + c))
                split_to(b + 13)
                rsqrt(norm2(l, L_GMLA), 512)
                normed_hi(apply2(l, LA_GMLA), a_out)
                bf = base2(l, M_FFN)
                split_to(bf + 2)
                post(l, 1, norm2(l, L_POSTMIX), 5 + 3 * l, bf - 1)
                deferred_hi(u2(l, 1), gain2(l, 4))
                split_to(bf + 4)
                rsqrt(norm2(l, L_PRE2), D)
                ffn(3 + 2 * l, bf)
                act.wait_ge(slab_done, bf + 3 * FJ)
                act.copy(hid_hi[:, 1], ptok[:, l]).then_inc(ph_ready, 1)
                split_to(bf + 3 * FJ + 3)
                post(l, 2, norm2(l, L_POST2), 6 + 3 * l, bf + 3 * FJ - 1)
                deferred_hi(u2(l, 2), gain2(l, 6))
                split_to(bf + 3 * FJ + 5)
                rsqrt(norm2(l, L_PREPLE), D)
                for i in range(4):
                    act.wait_ge(pg_scaled, 4 * l + i + 1)
                    act.activation(gate_s[:, i % 2, :], gate_s[:, i % 2, :], ACT.Sigmoid).then_inc(pg_ready, 1)
                    if i == 1:
                        split_to(base2(l + 1) + 1)
                post(l, 3, norm2(l, L_POSTPLE))

        @block.vector
        def _(dve):
            made = [0]
            trig = [0]

            def split_to(n):
                for s in range(made[0], min(n, SLABS)):
                    if s in POOL_LOW:
                        continue
                    if s - 1 in POOL_LOW:
                        dve.wait_ge(lo_ready, s)
                    dve.wait_ge(hi_ready, s + 1)
                    dve.tensor_tensor(w_lo[:, s % RING, :], raw[:, s % RING, :], w_hi[:, s % RING, :].bitcast(F32),
                                      ALU.subtract).then_inc(lo_ready, 1)
                made[0] = max(made[0], min(n, SLABS))

            steps = [0]

            def mod(g, kc):
                if kc == 0 and g in (G_B0, G_KV, G_MIX1, G_B1):
                    dve.wait_ge(mod_red, g - 1)
                for h in range(2):
                    u = steps[0]
                    slot, landings = mod_slot(u)
                    dve.wait_ge(mod_landed[slot], 16 * landings)
                    acc = mod_sums(g)[:, h * MOD_HALF:(h + 1) * MOD_HALF]
                    if kc == 0:
                        ins = dve.tensor_scalar(acc, mod_slots[slot], cs[:, 0:1], None, ALU.mult)
                    else:
                        dve.wait_ge(mod_step, u - 1)
                        ins = dve.scalar_tensor_tensor(out=acc, in0=mod_slots[slot], scalar=cs[:, kc:kc + 1], in1=acc,
                                                       op0=ALU.mult, op1=ALU.add)
                    ins.then_inc(mod_step, 1)
                    steps[0] += 1

            def mod_columns(g, b):
                dve.wait_ge(mod_red, g + 1)
                at = COL_AT["mod_b"] + 16 * g
                dve.tensor_tensor(modc[:, 16 * g:16 * g + 16], bank[b][:, 0:512:32], cols[:, at:at + 16], ALU.add).then_inc(modc_ready, 1)

            def scale_of(k, g, at, gain):
                dve.wait_ge(modc_ready, g + 1)
                dve.scalar_tensor_tensor(out=scale1[:, CH * k:CH * k + CH], in0=modc[:, 16 * g + at:16 * g + at + CH], scalar=1.0,
                                         in1=cols[:, gain:gain + CH], op0=ALU.add, op1=ALU.mult).then_inc(scale_ready, 1)

            def root(n, features):
                dve.wait_ge(rs0_ready, n + 1)
                dve.scalar_tensor_tensor(out=nwt[:, :], in0=rs0[:, :], scalar=-0.5 / features, in1=rs0[:, :], op0=ALU.mult, op1=ALU.mult).then_inc(newton, 1)
                dve.wait_ge(newton, 2 * n + 1)
                dve.scalar_tensor_tensor(out=nwt[:, :], in0=bank[stat_bank(n)][:, 0:S], scalar=EPS * features, in1=nwt[:, :],
                                         op0=ALU.add, op1=ALU.mult).then_inc(newton, 1)
                dve.wait_ge(newton, 2 * n + 2)
                dve.scalar_tensor_tensor(out=rstd[:, n % 2, :], in0=nwt[:, :], scalar=1.5, in1=rs0[:, :], op0=ALU.add, op1=ALU.mult).then_inc(rstd_ready, 1)
                dve.wait_ge(rstd_ready, n + 1)

            def over_rms(n):
                return rstd[:, n % 2:n % 2 + 1, :].to_broadcast([P, 2, S])

            def pair(v):
                return v.rearrange("p (c s) -> p c s", c=2)

            def deferred_low(ap, c, gain):
                dve.wait_ge(nh_ready, before(APPLY_CHUNKS, ap) + c + 1)
                dve.scalar_tensor_tensor(out=a_lo[:, c, :], in0=x[:, c, :], scalar=gain(c), in1=a_hi[:, c, :].bitcast(F32),
                                         op0=ALU.mult, op1=ALU.subtract).then_inc(nl_ready, 1)

            def normed(ap, n, src, gain, hi, lo, shift=None, at=0, ahead=1):
                a0, m = before(APPLY_CHUNKS, ap), APPLY_CHUNKS[ap]

                def low(c):
                    dve.wait_ge(nh_ready, a0 + c + 1)
                    if shift is None:
                        ins = dve.tensor_tensor(lo(c), sq[:, at + c, :], hi(c).bitcast(F32), ALU.subtract)
                    else:
                        ins = dve.scalar_tensor_tensor(out=lo(c), in0=sq[:, at + c, :], scalar=shift(c), in1=hi(c).bitcast(F32),
                                                       op0=ALU.add, op1=ALU.subtract)
                    ins.then_inc(nl_ready, 1)

                for c in range(m):
                    dve.scalar_tensor_tensor(out=sq[:, at + c, :], in0=src(c), scalar=gain(c), in1=rstd[:, n % 2, :],
                                             op0=ALU.mult, op1=ALU.mult).then_inc(nt_ready, 1)
                    if c >= ahead:
                        low(c - ahead)
                for c in range(max(m - ahead, 0), m):
                    low(c)

            def x_src(c):
                return x[:, c, :]

            def a_h(c):
                return a_hi[:, c, :]

            def a_l(c):
                return a_lo[:, c, :]

            def bank_sums(phase, b4, slab):
                if b4 < 3:
                    dve.wait_ge(bank_done, 3 * phase + b4 + 1)
                else:
                    dve.wait_ge(slab_done, slab + 1)

            def add_gated(phase, slab, gate):
                for c in range(CH):
                    if c % 2 == 0:
                        bank_sums(phase, c // 2, slab)
                    dve.scalar_tensor_tensor(out=x[:, c, :], in0=bank[4 + c // 2][:, (c % 2) * S:(c % 2 + 1) * S], scalar=gate(c),
                                             in1=x[:, c, :], op0=ALU.mult, op1=ALU.add).then_inc(x_ready, 1)

            def link(ins):
                trig[0] += 1
                ins.then_inc(trig_step, 1)
                dve.wait_ge(trig_step, trig[0])

            def rope_angle(part):
                kind, k = part // 2, part % 2
                if part == 0:
                    dve.wait_ge(s_late, 48)
                    link(dve.tensor_copy(pos_f, pos_i))
                if k == 0:
                    link(dve.tensor_scalar(ang, pos_f, col("inv_dil" if kind else "inv_mla", 0), None, ALU.mult))
                r, t = red[:, k, :], turn[:, k, :]
                if kind:
                    dve.wait_ge(trig_act, k + 1)
                link(dve.tensor_scalar(t, ang, 1.0 / TWO_PI, 0.25 if k == 0 else 0.0, ALU.mult, ALU.add))
                link(dve.tensor_scalar(t, t, MAGIC, -MAGIC, ALU.add, ALU.add))
                link(dve.scalar_tensor_tensor(out=r, in0=t, scalar=-C1, in1=ang, op0=ALU.mult, op1=ALU.add))
                link(dve.scalar_tensor_tensor(out=r, in0=t, scalar=-C2, in1=r, op0=ALU.mult, op1=ALU.add))
                link(dve.scalar_tensor_tensor(out=r, in0=t, scalar=-C3, in1=r, op0=ALU.mult, op1=ALU.add))
                link(dve.tensor_scalar(r, r, math.pi / 2 if k == 0 else 0.0, PI_SAFE, ALU.add, ALU.min))
                link(dve.tensor_scalar(r, r, -PI_SAFE, None, ALU.max))
                assert trig[0] == TRIG_AT[part]

            def ffn(i, b):
                def early(kc):
                    if i == 0:
                        mod(G_A1, kc)

                def angle(part):
                    if i == 1:
                        rope_angle(part)

                f0 = FJ * i

                n = None if i < 2 else norm2((i - 2) // 2, L_PRE1 if i % 2 == 0 else L_PRE2)

                def gate(j, par, done, first=False):
                    if i < 2:
                        return
                    dve.wait_ge(slab_done, done)
                    if not first:
                        dve.wait_ge(hid_done, j + (f0 - 1))
                    dve.tensor_tensor(pair(gate_s[:, par, :]), pair(bank[par][:, :]), over_rms(n), ALU.mult).then_inc(gate_scaled, 1)

                def hidden(j, par, up, first=False):
                    if i >= 2:
                        dve.wait_ge(slab_done, up)
                        if not first:
                            dve.wait_ge(hl_ready, j + (f0 - 1))
                        dve.tensor_tensor(pair(hid[:, par, :]), pair(bank[2 + par][:, :]), over_rms(n), ALU.mult).then_inc(up_scaled, 1)
                        dve.wait_ge(up_scaled, j + (FJ * (i - 2) + 1))
                        dve.wait_ge(silu_done, j + (f0 + 1))
                        dve.tensor_tensor(hid[:, par, :], hid[:, par, :], gate_s[:, par, :], ALU.mult).then_inc(hid_done, 1)
                        return
                    dve.wait_ge(silu_done, j + (f0 + 1))
                    dve.wait_ge(slab_done, up)
                    dve.tensor_tensor(hid[:, par, :], bank[2 + par][:, :], gate_s[:, par, :], ALU.mult).then_inc(hid_done, 1)

                def hidden_lo(j, par):
                    dve.wait_ge(hh_ready, j + (f0 + 1))
                    dve.tensor_tensor(hid_lo[:, par].rearrange("p c s -> p (c s)"), hid[:, par, :],
                                      hid_hi[:, par].rearrange("p c s -> p (c s)").bitcast(F32), ALU.subtract).then_inc(hl_ready, 1)

                def low(count, slot):
                    dve.wait_ge(hi_ready, count)
                    dve.tensor_tensor(w_lo[:, slot, :], raw[:, slot, :], w_hi[:, slot, :].bitcast(F32), ALU.subtract).then_inc(lo_ready, 1)

                split_to(b + 4)
                gate(0, 0, b + 1, True)
                hidden(0, 0, b + 2, True)
                split_to(b + 5)
                angle(0)
                early(0)
                early(1)
                hidden_lo(0, 0)
                gate(1, 1, b + 3, True)
                split_to(b + 6)
                angle(1)
                early(2)
                hidden(1, 1, b + 4, True)
                split_to(b + 7)
                angle(2)
                early(3)
                hidden_lo(1, 1)
                split_to(b + 8)
                angle(3)
                early(4)
                early(5)
                if i == 0:
                    dve.wait_ge(acc_zero, 2)
                s0 = steps[0]
                with dve.Fori(0, (FJ - 3) // 2) as k:
                    for h in range(2):
                        g = b + 5 + 3 * h
                        gate(2 * k + (2 + h), h, 6 * k + (g + 1))
                        low(6 * k + (g + 4), g % RING)
                        hidden(2 * k + (2 + h), h, 6 * k + (g + 2))
                        low(6 * k + (g + 5), (g + 1) % RING)
                        hidden_lo(2 * k + (2 + h), h)
                        low(6 * k + (g + 6), (g + 2) % RING)
                        if i == 0:
                            for m, gr in enumerate((G_KV, G_MIX1)):
                                for v in range(2):
                                    u = s0 + 4 * h + 2 * m + v
                                    slot, landings = mod_slot(u)
                                    dve.wait_ge(mod_landed[slot], 32 * k + 16 * landings)
                                    dve.wait_ge(mod_step, 8 * k + (u - 3))
                                    acc = mod_sums(gr)[:, v * MOD_HALF:(v + 1) * MOD_HALF]
                                    dve.scalar_tensor_tensor(out=acc, in0=mod_slots[slot], scalar=cs[:, bass.ds(2 * k + h, 1)],
                                                             in1=acc, op0=ALU.mult, op1=ALU.add).then_inc(mod_step, 1)
                if i == 0:
                    steps[0] += 32
                made[0] = b + 3 * (FJ - 2) + 5
                j = FJ - 1
                gate(j, j % 2, b + 3 * j)
                split_to(b + 3 * j + 3)
                hidden(j, j % 2, b + 3 * j + 1)
                if i == 0:
                    mod(G_A1, 6)
                split_to(b + 3 * j + 4)
                hidden_lo(j, j % 2)
                if i == 0:
                    mod(G_A1, 7)
                split_to(b + 3 * j + 5)

            dve.wait_ge(s_rb, 16)
            dve.tensor_copy(rbb[0:32, :, :], rb_sb[:, :].unsqueeze(2).to_broadcast([32, HEADS, P])).then_inc(rbb_ready, 1)
            dve.memset(rbb[32:33, :, :], 1.0).then_inc(rbb_ready, 1)
            dve.memset(xp[:, :, :, 0:3], 0.0).then_inc(pad_zero, 1)
            dve.wait_ge(lam_act, 2)
            lam_n = [0]

            def lam_link(ins):
                lam_n[0] += 1
                ins.then_inc(lam_dve, 1)
                dve.wait_ge(lam_dve, lam_n[0])

            u, s1, s2, v = lam[:, 1, :], lam[:, 2, :], lam[:, 3, :], lam[:, 4, :]
            lam_link(dve.tensor_scalar(v, u, 2.0, None, ALU.add))
            lam_link(dve.reciprocal(s2, v))
            lam_link(dve.tensor_tensor(s1, u, s2, ALU.mult))
            lam_link(dve.tensor_tensor(s2, s1, s1, ALU.mult))
            lam_link(dve.tensor_scalar(v, s2, 1.0 / ATANH_LAST, None, ALU.mult))
            for d in range(ATANH_LAST - 2, 1, -2):
                lam_link(dve.scalar_tensor_tensor(out=v, in0=v, scalar=1.0 / d, in1=s2, op0=ALU.add, op1=ALU.mult))
            lam_link(dve.scalar_tensor_tensor(out=v, in0=v, scalar=1.0, in1=s1, op0=ALU.add, op1=ALU.mult))
            at = COL_AT["lambda"]
            lam_link(dve.tensor_scalar(lam[:, 5, :], cols[:, at:at + LCH], -1.0, 0.0, ALU.mult, ALU.max))
            lam_link(dve.scalar_tensor_tensor(out=v, in0=v, scalar=2.0, in1=lam[:, 5, :], op0=ALU.mult, op1=ALU.add))
            lam_link(dve.tensor_scalar(lam[:, 7, :], v, 8.0, None, ALU.mult))
            assert lam_n[0] == LAM_STEPS
            for l in range(LAYERS2):
                for k in range(2):
                    at = COL_AT["gains2"] + 64 * l + CH * (1 + 4 * k)
                    dve.tensor_scalar(half_g[:, 16 * l + CH * k:16 * l + CH * k + CH], cols[:, at:at + CH], 0.5, None, ALU.mult).then_inc(half_ready, 1)
            dve.wait_ge(cs_ready, 1)
            for kc in range(8):
                mod(G_MIX0, kc)
            root(N_MIX0, D)
            split_to(1)
            mod_columns(G_MIX0, 7)
            scale_of(0, G_MIX0, CH, COL_AT["norm_mix"])
            split_to(2)
            dve.wait_ge(scale_ready, 1)
            normed(A_MIX0, N_MIX0, x_src, lambda c: scale1[:, c:c + 1], a_h, a_l, lambda c: modcol(G_MIX0, c))
            split_to(RING)

            for i in range(5):
                s = B_WIN + i
                dve.wait_ge(xbr_ready, i + 1)
                for k in range(3):
                    for m in range(2):
                        c = 2 * i + m
                        if k:
                            dve.wait_ge(conv_step, conv_count(i, k - 1, m))
                        ins = dve.scalar_tensor_tensor(out=xc[:, c, :], in0=xp[:, i % 2, m, k:k + S], scalar=col("conv_w", k * LCH + c),
                                                       in1=xc[:, c, :], op0=ALU.mult, op1=ALU.add)
                        ins.then_inc(conv_done if (k, m) == (2, 1) else conv_step, 1)
                split_to(s + 4)
                if i % 2:
                    mod(G_A0, i // 2)
            for i in range(5):
                split_to(B_WIN + 8 + i)
                if i < 4:
                    mod(G_A0, 2 + i)
            for hd in range(LHEADS):
                dve.wait_ge(xch_ready, hd + 1)
                dve.tensor_tensor(a_lo[:, 2 * hd:2 * hd + 2, :], xc[:, 2 * hd:2 * hd + 2, :], a_hi[:, 2 * hd:2 * hd + 2, :].bitcast(F32),
                                  ALU.subtract).then_inc(xcl_ready, 1)
            split_to(B_GATE + 3)
            mod(G_A0, 6)
            for hd in range(LHEADS):
                h2 = slice(2 * hd, 2 * hd + 2)
                dve.wait_ge(gates_ready, 2 * hd + 2)
                for c in (2 * hd, 2 * hd + 1):
                    dve.tensor_scalar(r_g[:, c, :], r_g[:, c, :], lam[:, 7, c:c + 1], None, ALU.mult)
                dve.tensor_tensor(i_g[:, h2, :], i_g[:, h2, :], xc[:, h2, :], ALU.mult).then_inc(bi_ready, 1)
                if hd == 1:
                    split_to(B_LOUT + 1)
            for hd in range(LHEADS):
                h2, tmp = slice(2 * hd, 2 * hd + 2), sq[:, 2 * (hd % 2):2 * (hd % 2) + 2, :]
                dve.wait_ge(decay_ready, hd + 1)
                dve.tensor_tensor(tmp, xc[:, h2, :], xc[:, h2, :], ALU.mult).then_inc(mult2_step, 1)
                dve.wait_ge(mult2_step, hd + 1)
                dve.scalar_tensor_tensor(out=r_g[:, h2, :], in0=tmp, scalar=1.0, in1=r_g[:, h2, :], op0=ALU.add, op1=ALU.mult).then_inc(mult2_ready, 1)
                if hd == 2:
                    mod(G_A0, 7)

            def z_low(hd):
                h2 = slice(2 * hd, 2 * hd + 2)
                dve.wait_ge(zh_ready, hd + 1)
                dve.tensor_tensor(a_lo[:, h2, :], i_g[:, h2, :], a_hi[:, h2, :].bitcast(F32), ALU.subtract).then_inc(zl_ready, 1)

            for hd in range(LHEADS):
                h2 = slice(2 * hd, 2 * hd + 2)
                dve.wait_ge(mult_ready, hd + 1)
                dve.tensor_tensor(i_g[:, h2, :], i_g[:, h2, :], r_g[:, h2, :], ALU.mult).then_inc(scan_step, 1)
                dve.wait_ge(scan_step, 2 * hd + 1)
                for c in (2 * hd, 2 * hd + 1):
                    ins = dve.tensor_tensor_scan(r_g[:, c, :], xc[:, c, :], i_g[:, c, :], 0.0, ALU.mult, ALU.add)
                ins.then_inc(scan_step, 1)
                dve.wait_ge(scan_step, 2 * hd + 2)
                dve.tensor_tensor(i_g[:, h2, :], r_g[:, h2, :], y_br[:, h2, :], ALU.mult).then_inc(z_ready, 1)
                if hd == 0:
                    z_low(0)
                elif hd > 1:
                    z_low(hd - 1)
                if 0 < hd < 4:
                    mod(G_B0, hd - 1)
            z_low(LHEADS - 1)
            mod(G_B0, 3)
            split_to(B_LOUT + 5)
            mod_columns(G_A0, 2)
            mod(G_B0, 4)
            mod(G_B0, 5)
            split_to(B_FFN0 + 1)
            dve.wait_ge(modc_ready, G_A0 + 1)
            add_gated(0, B_LOUT + 4, lambda c: modcol(G_A0, c))
            mod(G_B0, 6)
            mod(G_B0, 7)
            root(N_FFN0, D)
            split_to(B_FFN0 + 2)
            mod_columns(G_B0, 3)
            scale_of(1, G_B0, 0, COL_AT["norm_ffn"])
            dve.wait_ge(scale_ready, 2)
            normed(A_FFN0, N_FFN0, x_src, lambda c: scale1[:, CH + c:CH + c + 1], a_h, a_l, lambda c: modcol(G_A0, CH + c))
            split_to(B_FFN0 + 3)
            ffn(0, B_FFN0)

            split_to(B_KV + 2)
            add_gated(1, B_FFN0 + 3 * FJ - 1, lambda c: modcol(G_B0, CH + c))
            root(N_KV, D)
            mod_columns(G_KV, 1)
            scale_of(2, G_KV, CH, COL_AT["kv_norm"])
            dve.wait_ge(scale_ready, 3)
            normed(A_KV, N_KV, x_src, lambda c: scale1[:, 2 * CH + c:2 * CH + c + 1], a_h, a_l, lambda c: modcol(G_KV, c))
            split_to(B_KV + 3)
            mod_columns(G_MIX1, 3)
            scale_of(3, G_MIX1, CH, COL_AT["norm_mix"] + CH)
            split_to(B_KV + 4)
            mod(G_B1, 0)
            split_to(B_KV + 5)
            mod(G_B1, 1)
            dve.wait_ge(scale_ready, 4)
            normed(A_MIX1, N_KV, x_src, lambda c: scale1[:, 3 * CH + c:3 * CH + c + 1], a_h, a_l, lambda c: modcol(G_MIX1, c), ahead=CH)
            split_to(B_KV + 6)
            mod(G_B1, 2)
            split_to(B_KV + 7)
            mod_columns(G_A1, 4)
            mod(G_B1, 3)
            split_to(B_Q + 4)
            mod(G_B1, 4)

            def attention(heads, add, copy_out, at={}):
                n = len(heads)

                def scores(k):
                    h = heads[k]
                    dve.wait_ge(qk_done, h + 1)
                    if k >= 2:
                        dve.wait_ge(exp_done, h - 1)
                    dst = sc
                    for t, (lo, hi) in enumerate(((0, P), (P, 384))):
                        ins = dve.tensor_tensor_reduce(dst[:, h % 2, lo:hi], bank[k % 2][:, lo:hi], add(k)[:, lo:hi], -1.0, 3.0e38,
                                                       ALU.add, ALU.min, nmax[:, h % 2, t:t + 1])
                    ins.then_inc(sc_done, 1)

                def normalise(k):
                    h = heads[k]
                    pr = prob
                    dve.wait_ge(exp_done, h + 1)
                    dve.reciprocal(rsum[:, h % 2, :], ssum[:, h % 2, :]).then_inc(rs_done, 1)
                    dve.wait_ge(rs_done, h + 1)
                    for t, (lo, hi) in enumerate(((0, P), (P, 384))):
                        ins = dve.tensor_scalar(pr[:, h % 2, lo:hi], pr[:, h % 2, lo:hi], rsum[:, h % 2, t:t + 1], None, ALU.mult)
                    ins.then_inc(pn_done, 1)

                for k in range(-3, n + 1):
                    if k in at:
                        at[k]()
                    if 0 <= k + 1 < n:
                        normalise(k + 1)
                    if k + 3 < n:
                        scores(k + 3)
                    if k >= 1:
                        copy_out(k - 1)

            def moba_out(h):
                dve.wait_ge(oh_done, h + 1)
                dve.tensor_tensor(a_lo[:, h, :], bank[4 + h % 2][:, 0:256], a_hi[:, h, :].bitcast(F32), ALU.subtract).then_inc(o_done, 1)

            dve.wait_ge(s_bias, 32)

            attention(list(range(HEADS)), lambda k: bias[:, k, :], moba_out, {-1: lambda: split_to(B_Q + 6)})
            mod(G_B1, 5)
            split_to(B_Q + 7)
            mod(G_B1, 6)
            mod(G_B1, 7)
            assert steps[0] == 16 * MOD_GROUPS
            split_to(B_FFN1 + 2)
            add_gated(2, B_O + 3, lambda c: modcol(G_A1, c))
            root(N_FFN1, D)
            mod_columns(G_B1, 0)
            scale_of(4, G_B1, 0, COL_AT["norm_ffn"] + CH)
            dve.wait_ge(scale_ready, 5)
            normed(A_FFN1, N_FFN1, x_src, lambda c: scale1[:, 4 * CH + c:4 * CH + c + 1], a_h, a_l, lambda c: modcol(G_A1, CH + c))
            split_to(B_FFN1 + 3)
            ffn(1, B_FFN1)
            split_to(B_L2 + 2)
            add_gated(3, B_FFN1 + 3 * FJ - 1, lambda c: modcol(G_B1, CH + c))
            root(N_FIN, D)
            for c in range(CH):
                dve.scalar_tensor_tensor(out=x[:, c, :], in0=x[:, c, :], scalar=col("final_norm", c), in1=rstd[:, N_FIN % 2, :],
                                         op0=ALU.mult, op1=ALU.mult).then_inc(x_ready, 1)
                if c >= 2:
                    deferred_low(apply2(0, LA_PRE1), c - 2, lambda k: col("gains2", k))
            for c in (CH - 2, CH - 1):
                deferred_low(apply2(0, LA_PRE1), c, lambda k: col("gains2", k))

            def take_sums(l, k, n, phase, slab, gain):
                for b4 in range(4):
                    bank_sums(phase, b4, slab)
                    dve.wait_ge(sq_ready, before(NORM_CHUNKS, n) + 2 * b4 + 2)
                    for m in range(2):
                        c = 2 * b4 + m
                        ins = dve.tensor_scalar(f[:, c, :], bank[4 + b4][:, m * S:(m + 1) * S], gain(c), None, ALU.mult)
                    ins.then_inc(f_ready, 1)

            def post(l, k, n, gain=None, then=None):
                root(n, D)
                p = 4 * (4 * l + k)
                p5 = 5 * (4 * l + k)

                def scale(q):
                    c2 = slice(2 * q, 2 * q + 2)
                    dve.wait_ge(f_ready, p + q + 1)
                    if gain is None:
                        dve.tensor_tensor(f[:, c2, :], f[:, c2, :], over_rms(n), ALU.mult).then_inc(f_scaled, 1)
                        return
                    for c in (2 * q, 2 * q + 1):
                        ins = dve.scalar_tensor_tensor(out=f[:, c, :], in0=f[:, c, :], scalar=gain(c), in1=rstd[:, n % 2, :],
                                                       op0=ALU.mult, op1=ALU.mult)
                    ins.then_inc(f_scaled, 1)

                def add(q):
                    c2 = slice(2 * q, 2 * q + 2)
                    dve.wait_ge(f_scaled, p5 + q + 2)
                    dve.tensor_tensor(x[:, c2, :], x[:, c2, :], f[:, c2, :], ALU.add).then_inc(x_ready, 2)

                def first():
                    dve.wait_ge(f_ready, p + 1)
                    for c in range(2):
                        if gain is None:
                            ins = dve.tensor_tensor(f[:, c, :], f[:, c, :], rstd[:, n % 2, :], ALU.mult)
                        else:
                            ins = dve.scalar_tensor_tensor(out=f[:, c, :], in0=f[:, c, :], scalar=gain(c), in1=rstd[:, n % 2, :],
                                                           op0=ALU.mult, op1=ALU.mult)
                        ins.then_inc(f_scaled, 1)
                    for c in range(2):
                        dve.wait_ge(f_scaled, p5 + c + 1)
                        dve.tensor_tensor(x[:, c, :], x[:, c, :], f[:, c, :], ALU.add).then_inc(x_ready, 1)

                def low(q):
                    if then is not None:
                        for c in (2 * q, 2 * q + 1):
                            deferred_low(then[0], c, then[1])

                first()
                for q in range(1, 4):
                    scale(q)
                    low(q - 1)
                    add(q)
                low(3)

            def gain2(l, k):
                return lambda c: col("gains2", 64 * l + CH * k + c)

            n_rope = [0]

            def rlink(ins):
                n_rope[0] += 1
                ins.then_inc(rope_step, 1)
                return n_rope[0]

            def scaled(out, src, scale, table):
                return rlink(dve.scalar_tensor_tensor(out=out, in0=src, scalar=scale, in1=table, op0=ALU.mult, op1=ALU.mult))

            def place_free(taken):
                if n_rope[0]:
                    dve.wait_ge(rope_step, n_rope[0])
                    dve.wait_ge(qkv_dve, taken)

            def rope_dilated(dst, g, sums, scale, taken, swaps):
                both = lambda k: rope_r[:, k:k + 1, :].to_broadcast([P, 2, S])
                place_free(taken)
                dve.wait_ge(swap_ready, swaps)
                scaled(rt[:, 0:2, :], pair(sums[:, :]), scale, both(2))
                n = scaled(rt[:, 2:4, :], pair(swap), scale, both(3))
                dve.wait_ge(rope_step, n)
                if dst is k_dil:
                    dve.tensor_tensor(dst[:, 2 * g:2 * g + 2, :], rt[:, 0:2, :], rt[:, 2:4, :], ALU.add).then_inc(qkv_dve, 1)
                    return
                for m in range(2):
                    r = slice(64 * m, 64 * m + 64)
                    ins = dve.tensor_tensor(dst[r, 4 * g + m:4 * g + 4:2, :], rt[r, 0:2, :], rt[r, 2:4, :], ALU.add)
                ins.then_inc(qkv_dve, 1)

            for l in range(LAYERS2):
                split_to(base2(l) + 4)
                root(norm2(l, L_PRE1), D)
                ffn(2 + 2 * l, base2(l))
                if l == 0:
                    dve.wait_ge(trig_act, 4)
                    dve.tensor_scalar(rope[:, 1, :], rope[:, 1, :], col("sign_mla", 0), None, ALU.mult).then_inc(rope_ready, 1)
                    dve.tensor_scalar(rope[:, 3, :], rope[:, 3, :], col("sign_dil", 0), None, ALU.mult).then_inc(rope_ready, 1)
                b = base2(l, M_MIX)
                split_to(b + 2)
                dve.wait_ge(half_ready, 2 * LAYERS2)
                take_sums(l, 0, norm2(l, L_POST1), 4 + 3 * l, b - 1, lambda c: half_g[:, 16 * l + c:16 * l + c + 1])
                post(l, 0, norm2(l, L_POST1), None, (apply2(l, LA_PREMIX), gain2(l, 2)))
                split_to(b + 4)
                root(norm2(l, L_PREMIX), D)
                d0 = 6 * l
                dve.wait_ge(rope_ready, 2)
                if l:
                    place_free(d0)
                dve.tensor_tensor(rope_r[:, :, :], rope[:, :, :], rstd[:, norm2(l, L_PREMIX) % 2:norm2(l, L_PREMIX) % 2 + 1, :].to_broadcast([P, 4, S]),
                                  ALU.mult).then_inc(table_ready, 1)
                dve.wait_ge(rows_zero, 4)
                dve.wait_ge(slab_done, b + 1)
                dve.tensor_tensor(q_lat[:, :, :], pair(bank[0][:, :]), over_rms(norm2(l, L_PREMIX)), ALU.mult).then_inc(qkv_dve, 1)
                dve.wait_ge(slab_done, b + 2)
                dve.wait_ge(table_ready, l + 1)
                scaled(kr, bank[1][:, S:2 * S], 1.0, rope_r[:, 0, :])
                dve.tensor_tensor(kv_lat[:, 0, :], bank[1][:, 0:S], rstd[:, norm2(l, L_PREMIX) % 2, :], ALU.mult).then_inc(qkv_dve, 1)
                split_to(b + 5)
                for i in range(4):
                    dve.wait_ge(slab_done, b + 3 + i)
                    rope_dilated(q_dil if i < 2 else k_dil, i % 2, bank[(2 + i) % 4], 64 ** -0.5 if i < 2 else 1.0, d0 + 2 + i, 4 * l + i + 1)
                    split_to(b + 6 + i)
                    if i == 0:
                        dve.wait_ge(rturn_done, l + 1)
                        dve.tensor_copy(rcol[:, :], bank[5][:, 0:256:P]).then_inc(rcol_ready, 1)
                    if i == 2:
                        root(norm2(l, L_QLAT), 256)
                        normed(apply2(l, LA_QLAT), norm2(l, L_QLAT), lambda c: q_lat[:, c, :], lambda c: col("q_norm2", 2 * l + c),
                               lambda c: a_hi[:, 8 + c, :], lambda c: a_lo[:, 8 + c, :])
                root(norm2(l, L_KVLAT), P)
                normed(apply2(l, LA_KVLAT), norm2(l, L_KVLAT), lambda c: kv_lat[:, c, :], lambda c: col("kv_norm2", l + c),
                       lambda c: hid_hi[:, 0, 0, :], lambda c: hid_lo[:, 0, 0, :], None, 2)
                dve.wait_ge(up_done, UP2 * l + 1)
                n = scaled(rt_q[:, 0, :], bank[0][:, 0:S], 1.0, rope_r[:, 1, :])
                assert n == ROPE_STEPS * l + KEY_STEPS
                split_to(b + 10)

                def queries():
                    dve.wait_ge(slab_done, b + 10)
                    dve.wait_ge(k_roped, l + 1)
                    for m in range(2):
                        scaled(rt_q[:, m, :], bank[6][:, m * S:(m + 1) * S], 96 ** -0.5, rope[:, 0, :])
                    for m in range(2):
                        n = scaled(rt_q[:, 2 + m, :], bank[7][:, m * S:(m + 1) * S], 96 ** -0.5, rope[:, 1, :])
                    assert n == ROPE_STEPS * (l + 1)

                def pair_out(k):
                    if k % 2:
                        h = HEADS + 16 * l + k
                        dve.wait_ge(pv_done, h + 1)
                        dve.tensor_copy(f[:, (k // 2 + 4) % 8, :], bank[4 + (k // 2) % 2][:, 0:256]).then_inc(o_done, 1)

                ap, n_dil = apply2(l, LA_GDIL), norm2(l, L_GDIL)

                def dilated(c):
                    if c == -1:
                        root(n_dil, 512)
                        return
                    if c < 4:
                        dve.scalar_tensor_tensor(out=sq[:, 4 + c, :], in0=f[:, 4 + c, :], scalar=col("group2", CH * l + 4 + c),
                                                 in1=rstd[:, n_dil % 2, :], op0=ALU.mult, op1=ALU.mult).then_inc(nt_ready, 1)
                    if c >= 2:
                        dve.wait_ge(nh_ready, before(APPLY_CHUNKS, ap) + c - 1)
                        dve.tensor_tensor(a_lo[:, 2 + c, :], sq[:, 2 + c, :], a_hi[:, 2 + c, :].bitcast(F32), ALU.subtract).then_inc(nl_ready, 1)

                steps_at = {-1: lambda: split_to(b + 11), 1: queries}
                steps_at.update({NORM_STEP + 2 + c: lambda c=c: dilated(c) for c in range(-1, 5)})
                attention([HEADS + 16 * l + k for k in range(16)], lambda k: mask[:, 1 if k < HEADS else 0, :], pair_out,
                          steps_at)
                dilated(5)
                split_to(b + 13)
                root(norm2(l, L_GMLA), 512)
                normed(apply2(l, LA_GMLA), norm2(l, L_GMLA), lambda c: f[:, c, :], lambda c: col("group2", CH * l + c), a_h, a_l)
                bf = base2(l, M_FFN)
                split_to(bf + 2)
                take_sums(l, 1, norm2(l, L_POSTMIX), 5 + 3 * l, bf - 1, gain2(l, 3))
                post(l, 1, norm2(l, L_POSTMIX), None, (apply2(l, LA_PRE2), gain2(l, 4)))
                split_to(bf + 4)
                root(norm2(l, L_PRE2), D)
                ffn(3 + 2 * l, bf)
                dve.wait_ge(ph_ready, l + 1)
                dve.tensor_tensor(hid_lo[:, 1], ptok[:, l], hid_hi[:, 1].bitcast(F32), ALU.subtract).then_inc(pl_ready, 1)
                split_to(bf + 3 * FJ + 3)
                take_sums(l, 2, norm2(l, L_POST2), 6 + 3 * l, bf + 3 * FJ - 1, lambda c: half_g[:, 16 * l + CH + c:16 * l + CH + c + 1])
                post(l, 2, norm2(l, L_POST2), None, (apply2(l, LA_PREPLE), gain2(l, 6)))
                split_to(bf + 3 * FJ + 5)
                n = norm2(l, L_PREPLE)
                root(n, D)

                def embed(i):
                    dve.wait_ge(pg_ready, 4 * l + i + 1)
                    dve.tensor_tensor(f[:, 2 * i:2 * i + 2, :], pair(bank[4 + i][:, :]), pair(gate_s[:, i % 2, :]), ALU.mult).then_inc(f_ready, 1)

                for i in range(4):
                    dve.wait_ge(slab_done, base2(l, M_PGATE) + i + 1)
                    if i >= 2:
                        dve.wait_ge(f_ready, 4 * (4 * l + 3) + i - 1)
                    dve.tensor_tensor(pair(gate_s[:, i % 2, :]), pair(bank[i][:, :]), over_rms(n), ALU.mult).then_inc(pg_scaled, 1)
                    if i:
                        embed(i - 1)
                    if i == 1:
                        split_to(base2(l + 1) + 1)
                embed(3)
                split_to(base2(l + 1) + 2)
                then = (apply2(l + 1, LA_PRE1), gain2(l + 1, 0)) if l + 1 < LAYERS2 else None
                post(l, 3, norm2(l, L_POSTPLE), gain2(l, 7), then)


def rope_slot(h):
    return (2, 0, 3, 1)[h % 4]


MOD_AHEAD = [34, 35]
POOL_LOW = [B_LOUT + i for i in range(1, 4)]
GATE_ENDS = (1, 3, 4)
ATANH_LAST = 17
LAM_STEPS = 5 + (ATANH_LAST - 3) // 2 + 4
TRIG_AT = [9, 16, 24, 31]
MOD_ORDER = ([(g, k) for g in (G_MIX0, G_A0, G_B0) for k in range(8)] + [(G_A1, k) for k in range(6)]
             + [(g, k) for k in range(8) for g in (G_KV, G_MIX1)] + [(G_A1, k) for k in range(6, 8)] + [(G_B1, k) for k in range(8)])
MOD_LAST = [2 * max(i for i, (h, _) in enumerate(MOD_ORDER) if h == g) + 2 for g in range(MOD_GROUPS)]
UP2 = 6
KEY_STEPS, ROPE_STEPS = 10, 14
WARM_BEFORE, WARM_AFTER = 10, 24
NORM_STEP = 10
OUT_ORDER = (2, 3, 0, 1)


def conv_count(i, k, m):
    return 5 * i + 2 * k + m + 1


def wide(w):
    return w.reshape(-1, P, w.shape[1]).transpose(1, 0, 2).reshape(P, -1)


def stream_slabs(a):
    win = a["lru_w_in"][0]
    for at in (LRU, 0):
        for i in range(5):
            yield wide(win[:, at + 256 * i:at + 256 * (i + 1)])
    g = a["lru_w_gates"][0]
    for i in range(0, LHEADS, 2):
        yield np.concatenate([wide(g[h]) if h < LHEADS else np.zeros((P, 1024), np.float32) for h in (i, i + 1)], axis=1)
    yield from tall(a["lru_w_out"][0])
    yield from ffn_slabs(a["ffn_w_gate"][0], a["ffn_w_up"][0], a["ffn_w_down"][0])
    for w in (a["w_kv"], a["attn_w_q"][0]):
        for i in range(4):
            yield wide(w[:, 256 * i:256 * (i + 1)])
    yield from tall(a["attn_w_o"][0])
    yield from ffn_slabs(a["ffn_w_gate"][1], a["ffn_w_up"][1], a["ffn_w_down"][1])
    for l in range(LAYERS2):
        yield from ffn_slabs(a["ffn_gate_2"][l, 0], a["ffn_up_2"][l, 0], a["ffn_down_2"][l, 0])
        w = a["w_in_2"][l]
        kr, rot = w[:, 384:416], np.concatenate([w[:, 400:416], w[:, 384:400]], axis=1)
        yield wide(w[:, 0:256])
        yield wide(np.concatenate([w[:, 256:384]] + [kr] * 4, axis=1))
        for part in range(2):
            for g in range(2):
                yield wide(w[:, 416 + 512 * part + 256 * g:416 + 512 * part + 256 * (g + 1)])
        for i in range(2):
            yield wide(w[:, 1440 + 256 * i:1440 + 256 * (i + 1)])
        up = a["w_kv_up_2"][l].reshape(P, HEADS, 2, 64).transpose(0, 2, 1, 3).reshape(P, 1024)
        yield np.concatenate([wide(np.concatenate([rot] * 4, axis=1)), up], axis=1)
        q = a["w_q_up_2"][l].reshape(256, HEADS, 96)
        slots = [4 * c + next(h for h in range(4) if rope_slot(h) == s) for c in range(2) for s in range(4)]
        pairs = q[:, slots, 64:]
        turned = np.concatenate([pairs[:, :, 16:], pairs[:, :, :16]], axis=2)
        yield wide(np.concatenate([q[:, :, :64].reshape(256, 512), pairs.reshape(256, 256), turned.reshape(256, 256)], axis=1))
        out = list(tall(a["w_out_2"][l]))
        yield from (out[i] for i in OUT_ORDER)
        yield from ffn_slabs(a["ffn_gate_2"][l, 1], a["ffn_up_2"][l, 1], a["ffn_down_2"][l, 1])
        yield from tall(a["w_ple_2"][l])
        w = a["w_ple_gate_2"][l]
        for i in range(4):
            yield wide(w[:, 256 * i:256 * (i + 1)])


def tall(w):
    for i in range(0, w.shape[0], 256):
        yield wide(w[i:i + 256])


def ffn_slabs(gate, up, down):
    d = list(tall(down))
    for j in range(FJ):
        yield wide(gate[:, 256 * j:256 * (j + 1)])
        yield wide(up[:, 256 * j:256 * (j + 1)])
        if j:
            yield d[j - 1]
    yield d[FJ - 1]


def mod_slabs(a):
    m, kv = a["mod_w"], a["kv_mod_w"]
    groups = [m[0][:, 0:2048], m[0][:, 2048:4096], m[0][:, 4096:6144], kv, m[1][:, 0:2048], m[1][:, 2048:4096], m[1][:, 4096:6144]]
    for g, k in MOD_ORDER:
        yield groups[g][P * k:P * (k + 1)]


def columns(a):
    def cut(v):
        return v.reshape(-1, P).T
    inv_m = (10000.0 ** (-np.arange(0, 32, 2, dtype=np.float32) / np.float32(32))).astype(np.float32)
    inv_d = (10000.0 ** (-np.arange(0, 64, 2, dtype=np.float32) / np.float32(64))).astype(np.float32)
    parts = {
        "c": cut(a["c"]), "norm_mix": cut(a["norm_mix"]), "norm_ffn": cut(a["norm_ffn"]), "kv_norm": cut(a["kv_norm"]),
        "final_norm": cut(a["final_norm"]), "gains2": cut(a["norm_gains_2"]), "q_norm2": cut(a["q_norm_2"]),
        "kv_norm2": cut(a["kv_norm_2"]), "group2": cut(a["group_out_norm_2"]), "conv_w": cut(a["lru_conv_w"]),
        "conv_b": cut(a["lru_conv_b"]), "b_gates": cut(a["lru_b_gates"]), "lambda": cut(a["lru_lambda"]),
        "mod_b": np.concatenate([cut(a["mod_b"][0]), cut(a["kv_mod_b"]), cut(a["mod_b"][1])], axis=1),
        "inv_mla": np.tile(inv_m, 8)[:, None], "inv_dil": np.tile(inv_d, 4)[:, None],
        "sign_mla": np.tile(np.repeat(np.array([-1.0, 1.0], np.float32), 16), 4)[:, None],
        "sign_dil": np.tile(np.repeat(np.array([-1.0, 1.0], np.float32), 32), 2)[:, None],
    }
    for n, k in COLS:
        assert parts[n].shape == (P, k), (n, parts[n].shape, k)
    return np.ascontiguousarray(np.concatenate([parts[n] for n, _ in COLS], axis=1))


def bucket(dist):
    if dist < 16:
        return dist
    return min(16 + int(math.log(dist / 16) / math.log(8) * 16 + 1e-9), 31)


def shape_constants():
    onehot = np.zeros((33, 512), np.float32)
    for y in range(512):
        if y <= 255:
            onehot[bucket(255 - y), y] = 1.0
        else:
            onehot[32, y] = NEG
    q, k = np.arange(S)[:, None], np.arange(S)[None, :]
    dist = q - k
    causal = np.where(dist >= 0, 0.0, NEG)
    times = (dist >= 0) * sum(((dist % d == 0) & (dist <= w)).astype(int) for w, d in ((128, 1), (512, 4), (2048, 16)))
    dilated = np.where(times > 0, np.log(np.maximum(times, 1)), NEG)
    masks = np.stack([np.concatenate([m[:P, :P], m[P:, :]], axis=1) for m in (causal, dilated)]).astype(np.float32)
    return onehot, masks


def kernel(**inputs):
    import concourse.bacc as bacc
    from concourse.bass_utils import run_bass_kernel_spmd

    a = {k: np.asarray(v) for k, v in inputs.items()}
    onehot, masks = shape_constants()
    stream = np.empty((SLABS, P, DINNER), np.float32)
    n = 0
    for slab in stream_slabs(a):
        stream[n] = slab
        n += 1
    assert n == SLABS
    mods = np.empty((8 * MOD_GROUPS, P, DINNER), np.float32)
    for n, slab in enumerate(mod_slabs(a)):
        mods[n] = slab
    arrays = {
        "stream": stream, "mods": mods,
        "x_t": np.ascontiguousarray(a["x"][0].T),
        "cols": columns(a),
        "onehot": onehot,
        "rb_t": np.ascontiguousarray(a["rel_bias"].T),
        "masks": masks,
        "pos": np.ascontiguousarray(np.broadcast_to(a["positions_2"], (P, S))),
        "p_t": np.ascontiguousarray(a["p_2"][:, 0].transpose(0, 2, 1)),
    }
    nc = bacc.Bacc("TRN2", target_bir_lowering=False, num_devices=1)
    args = {k: nc.dram_tensor("in_" + k, v.shape, mybir.dt.from_np(v.dtype), kind="ExternalInput").ap() for k, v in arrays.items()}
    out_t = nc.dram_tensor("out_t", (D, S), F32, kind="ExternalOutput").ap()
    build(nc, args["stream"], args["mods"], args["x_t"], args["cols"], args["onehot"], args["rb_t"], args["masks"], args["pos"],
          args["p_t"], out_t)
    r = run_bass_kernel_spmd(nc, [{"in_" + k: v for k, v in arrays.items()}], core_ids=[0])
    return np.ascontiguousarray(r.results[0]["out_t"].T)[None]
```
